# Optimizing a Trainium2 kernel written in Bass

```python
import jax, jax.numpy as jnp
from jax import lax
import numpy as np

D_MODEL = 1024
BATCH = 1
SEQ = 256
DEPTH = 2

N_A_LAYERS = DEPTH // 2
N_B_LAYERS = DEPTH - N_A_LAYERS

NSA_HEADS = 16
NSA_HEAD_DIM = D_MODEL // NSA_HEADS
NSA_KV_GROUPS = 2
NSA_HEADS_PER_GROUP = NSA_HEADS // NSA_KV_GROUPS
NSA_KV_WIDTH = NSA_KV_GROUPS * NSA_HEAD_DIM
NSA_GATE_WIDTH = 3 * NSA_HEADS
NSA_IN_WIDTH = D_MODEL + 6 * NSA_KV_WIDTH + NSA_GATE_WIDTH
CMP_BLOCK = 32
CMP_STRIDE = 16
CMP_MLP_HIDDEN = 128
SLC_BLOCK = 64
SLC_TOPK = 16
WINDOW = 512
NSA_Q_BLOCK = 64
FORCE_BONUS = 1000.0

DIFF_HEADS = 8
DIFF_HEAD_DIM = D_MODEL // (2 * DIFF_HEADS)
DIFF_V_DIM = 2 * DIFF_HEAD_DIM
DIFF_Q_BLOCK = 128

ROPE_THETA = 500000.0
ROPE_FRACTION = 4
D_FF = 2816
DEEPNORM_ALPHA = (2 * DEPTH) ** 0.25
DEEPNORM_BETA = (8 * DEPTH) ** -0.25
NORM_EPS = 1e-5
NEG = -1e30

kernel_name = 'yoco_nsa_diffattn_macaron_deepnorm'

def partial_rope(x, positions):
    d = x.shape[-1]
    r = d // ROPE_FRACTION
    half = r // 2
    inv = ROPE_THETA ** (-jnp.arange(half, dtype=jnp.float32) * 2.0 / r)
    ang = positions.astype(jnp.float32)[:, None] * inv[None, :]
    cos = jnp.cos(ang)[:, None, :].astype(x.dtype)
    sin = jnp.sin(ang)[:, None, :].astype(x.dtype)
    x1 = x[..., :half]
    x2 = x[..., half:r]
    return jnp.concatenate([x1 * cos - x2 * sin, x1 * sin + x2 * cos, x[..., r:]], axis=-1)

def layer_norm(x, g, b):
    xf = x.astype(jnp.float32)
    mu = jnp.mean(xf, axis=-1, keepdims=True)
    var = jnp.mean(jnp.square(xf - mu), axis=-1, keepdims=True)
    return ((xf - mu) * lax.rsqrt(var + NORM_EPS) * g + b).astype(x.dtype)

def rms_norm(x, g):
    xf = x.astype(jnp.float32)
    return (xf * lax.rsqrt(jnp.mean(jnp.square(xf), axis=-1, keepdims=True) + NORM_EPS) * g).astype(x.dtype)

def post_norm(x, f, g, b):
    return layer_norm(DEEPNORM_ALPHA * x + f, g, b)

def swiglu(x, w_gate, w_up, w_down):
    return (jax.nn.silu(x @ w_gate) * (x @ w_up)) @ w_down

def compress(k, pos_emb, w1, b1, w2):
    B, S, G, Dh = k.shape
    n_c = (S - CMP_BLOCK) // CMP_STRIDE + 1
    idx = np.arange(n_c)[:, None] * CMP_STRIDE + np.arange(CMP_BLOCK)[None, :]
    blocks = k[:, idx] + pos_emb[:, None, :]
    blocks = jnp.swapaxes(blocks, 2, 3).reshape(B, n_c, G, CMP_BLOCK * Dh)
    return jax.nn.gelu(blocks @ w1 + b1) @ w2

def cmp_to_slc_matrix(n_c, n_sel):
    c0 = np.arange(n_c)[:, None] * CMP_STRIDE
    s0 = np.arange(n_sel)[None, :] * SLC_BLOCK
    ov = np.minimum(c0 + CMP_BLOCK, s0 + SLC_BLOCK) - np.maximum(c0, s0)
    return (np.clip(ov, 0, None) / CMP_BLOCK).astype(np.float32)

def nsa_mixer(x, w_in, pos_k, w1_k, b1_k, w2_k, pos_v, w1_v, b1_v, w2_v, w_out, positions):
    B, S, _ = x.shape
    H, G, Hg, Dh = NSA_HEADS, NSA_KV_GROUPS, NSA_HEADS_PER_GROUP, NSA_HEAD_DIM
    QB = NSA_Q_BLOCK
    proj = x @ w_in
    cuts = [int(c) for c in np.cumsum([D_MODEL] + [NSA_KV_WIDTH] * 6)]
    q, kc, vc, ks, vs, kw, vw, gates = jnp.split(proj, cuts, axis=-1)
    q = q.reshape(B, S, H, Dh) * (Dh ** -0.5)
    q_rot = partial_rope(q, positions)
    kv = lambda t: t.reshape(B, S, G, Dh)
    k_cmp = compress(kv(kc), pos_k, w1_k, b1_k, w2_k)
    v_cmp = compress(kv(vc), pos_v, w1_v, b1_v, w2_v)
    n_c = k_cmp.shape[1]
    n_sel = S // SLC_BLOCK
    k_blocks = partial_rope(kv(ks), positions).reshape(B, n_sel, SLC_BLOCK, G, Dh).transpose(0, 3, 1, 2, 4)
    v_blocks = kv(vs).reshape(B, n_sel, SLC_BLOCK, G, Dh).transpose(0, 3, 1, 2, 4)
    pad = ((0, 0), (WINDOW, 0), (0, 0), (0, 0))
    kw_pad = jnp.pad(partial_rope(kv(kw), positions), pad)
    vw_pad = jnp.pad(kv(vw), pad)

    cmp_end = jnp.asarray(np.arange(n_c) * CMP_STRIDE + CMP_BLOCK - 1)
    overlap = jnp.asarray(cmp_to_slc_matrix(n_c, n_sel))
    k_top = min(SLC_TOPK, n_sel)
    nqb = S // QB
    bi = jnp.arange(B)[:, None, None, None]
    gi = jnp.arange(G)[None, None, :, None]
    blk = jnp.arange(n_sel)

    def to_blocks(t):
        return jnp.moveaxis(t.reshape(B, nqb, QB, G, Hg, Dh), 1, 0)

    def step(args):
        qc, qr, i = args
        t = i * QB + jnp.arange(QB)
        vis = cmp_end[None, :] <= t[:, None]
        s = jnp.einsum('bqghd,bcgd->bqghc', qc, k_cmp).astype(jnp.float32)
        s = jnp.where(vis[None, :, None, None, :], s, NEG)
        p_cmp = jax.nn.softmax(s, axis=-1) * jnp.any(vis, axis=-1)[None, :, None, None, None]
        o_cmp = jnp.einsum('bqghc,bcgd->bqghd', p_cmp.astype(v_cmp.dtype), v_cmp)
        cur = t // SLC_BLOCK
        imp = jnp.einsum('bqghc,cn->bqgn', p_cmp, overlap)
        forced = (blk[None] == 0) | (blk[None] == cur[:, None]) | (blk[None] == cur[:, None] - 1)
        valid = blk[None] <= cur[:, None]
        imp = jnp.where(valid[None, :, None, :], imp + jnp.where(forced, FORCE_BONUS, 0.0)[None, :, None, :], NEG)
        _, sel = lax.top_k(imp, k_top)
        k_sel = k_blocks[bi, gi, sel]
        v_sel = v_blocks[bi, gi, sel]
        key_pos = sel[..., None] * SLC_BLOCK + jnp.arange(SLC_BLOCK)
        ok = key_pos <= t[None, :, None, None, None]
        s = jnp.einsum('bqghd,bqgnkd->bqghnk', qr, k_sel).astype(jnp.float32)
        s = jnp.where(ok[:, :, :, None], s, NEG)
        p = jax.nn.softmax(s.reshape(s.shape[:4] + (-1,)), axis=-1).reshape(s.shape)
        o_slc = jnp.einsum('bqghnk,bqgnkd->bqghd', p.astype(v_sel.dtype), v_sel)
        start = i * QB
        k_win = lax.dynamic_slice_in_dim(kw_pad, start, QB + WINDOW, axis=1)
        v_win = lax.dynamic_slice_in_dim(vw_pad, start, QB + WINDOW, axis=1)
        kpos = start - WINDOW + jnp.arange(QB + WINDOW)
        okw = (kpos[None] <= t[:, None]) & (kpos[None] > t[:, None] - WINDOW) & (kpos[None] >= 0)
        s = jnp.einsum('bqghd,bkgd->bqghk', qr, k_win).astype(jnp.float32)
        s = jnp.where(okw[None, :, None, None, :], s, NEG)
        p = jax.nn.softmax(s, axis=-1)
        o_win = jnp.einsum('bqghk,bkgd->bqghd', p.astype(v_win.dtype), v_win)
        return o_cmp, o_slc, o_win

    outs = lax.map(step, (to_blocks(q), to_blocks(q_rot), jnp.arange(nqb)))
    o_cmp, o_slc, o_win = [jnp.moveaxis(o, 0, 1).reshape(B, S, H, Dh) for o in outs]
    g = jax.nn.sigmoid(gates.reshape(B, S, 3, H))[..., None]
    o = g[:, :, 0] * o_cmp + g[:, :, 1] * o_slc + g[:, :, 2] * o_win
    return o.reshape(B, S, D_MODEL) @ w_out

def shared_kv(x, w_kv, positions):
    B, S, _ = x.shape
    k, v = jnp.split(x @ w_kv, [D_MODEL], axis=-1)
    k = k.reshape(B, S, 2, DIFF_HEADS, DIFF_HEAD_DIM)
    k1 = partial_rope(k[:, :, 0], positions)
    k2 = partial_rope(k[:, :, 1], positions)
    return k1, k2, v.reshape(B, S, DIFF_HEADS, DIFF_V_DIM)

def diff_mixer(x, k1, k2, v, w_q, lq1, lk1, lq2, lk2, subln_g, w_out, positions, lambda_init):
    B, S, _ = x.shape
    H, Dh, QB = DIFF_HEADS, DIFF_HEAD_DIM, DIFF_Q_BLOCK
    q = (x @ w_q).reshape(B, S, 2, H, Dh) * (Dh ** -0.5)
    q1 = partial_rope(q[:, :, 0], positions)
    q2 = partial_rope(q[:, :, 1], positions)
    lam = (jnp.exp(jnp.sum(lq1.astype(jnp.float32) * lk1.astype(jnp.float32)))
           - jnp.exp(jnp.sum(lq2.astype(jnp.float32) * lk2.astype(jnp.float32))) + lambda_init)
    nqb = S // QB
    to_blocks = lambda t: jnp.moveaxis(t.reshape(B, nqb, QB, H, Dh), 1, 0)
    kpos = jnp.arange(S)

    def step(args):
        q1b, q2b, i = args
        t = i * QB + jnp.arange(QB)
        mask = (kpos[None, :] <= t[:, None])[None, None]

        def attn_map(qb, k):
            s = jnp.einsum('bqhd,bkhd->bhqk', qb, k).astype(jnp.float32)
            return jax.nn.softmax(jnp.where(mask, s, NEG), axis=-1)

        a = attn_map(q1b, k1) - lam * attn_map(q2b, k2)
        return jnp.einsum('bhqk,bkhe->bqhe', a.astype(v.dtype), v)

    o = lax.map(step, (to_blocks(q1), to_blocks(q2), jnp.arange(nqb)))
    o = jnp.moveaxis(o, 0, 1).reshape(B, S, H, DIFF_V_DIM)
    o = rms_norm(o, subln_g) * (1.0 - lambda_init)
    return o.reshape(B, S, D_MODEL) @ w_out

def setup_inputs(seed: int = 0) -> dict:
    key = jax.random.key(seed)
    ks = jax.random.split(key, 32)
    f32 = jnp.float32
    nrm = lambda k, shape, scale: jax.random.normal(k, shape, f32) * scale
    D, F, Dh = D_MODEL, D_FF, NSA_HEAD_DIM
    L_flat = CMP_BLOCK * Dh
    return {
        'x': nrm(ks[0], (BATCH, SEQ, D), 1.0),
        'ffn1_w_gate': nrm(ks[1], (DEPTH, D, F), D ** -0.5),
        'ffn1_w_up': nrm(ks[2], (DEPTH, D, F), D ** -0.5),
        'ffn1_w_down': nrm(ks[3], (DEPTH, F, D), F ** -0.5 * DEEPNORM_BETA),
        'ffn2_w_gate': nrm(ks[4], (DEPTH, D, F), D ** -0.5),
        'ffn2_w_up': nrm(ks[5], (DEPTH, D, F), D ** -0.5),
        'ffn2_w_down': nrm(ks[6], (DEPTH, F, D), F ** -0.5 * DEEPNORM_BETA),
        'ln_g': 1.0 + nrm(ks[7], (DEPTH, 3, D), 0.02),
        'ln_b': nrm(ks[8], (DEPTH, 3, D), 0.02),
        'a_w_in': nrm(ks[9], (N_A_LAYERS, D, NSA_IN_WIDTH), D ** -0.5),
        'a_cmp_pos_k': nrm(ks[10], (N_A_LAYERS, CMP_BLOCK, Dh), 0.02),
        'a_cmp_w1_k': nrm(ks[11], (N_A_LAYERS, L_flat, CMP_MLP_HIDDEN), L_flat ** -0.5),
        'a_cmp_b1_k': nrm(ks[12], (N_A_LAYERS, CMP_MLP_HIDDEN), 0.02),
        'a_cmp_w2_k': nrm(ks[13], (N_A_LAYERS, CMP_MLP_HIDDEN, Dh), CMP_MLP_HIDDEN ** -0.5),
        'a_cmp_pos_v': nrm(ks[14], (N_A_LAYERS, CMP_BLOCK, Dh), 0.02),
        'a_cmp_w1_v': nrm(ks[15], (N_A_LAYERS, L_flat, CMP_MLP_HIDDEN), L_flat ** -0.5),
        'a_cmp_b1_v': nrm(ks[16], (N_A_LAYERS, CMP_MLP_HIDDEN), 0.02),
        'a_cmp_w2_v': nrm(ks[17], (N_A_LAYERS, CMP_MLP_HIDDEN, Dh), CMP_MLP_HIDDEN ** -0.5),
        'a_w_out': nrm(ks[18], (N_A_LAYERS, D, D), D ** -0.5 * DEEPNORM_BETA),
        'b_w_kv_shared': nrm(ks[19], (D, 2 * D), D ** -0.5),
        'b_w_q': nrm(ks[20], (N_B_LAYERS, D, D), D ** -0.5),
        'b_lambda_q1': nrm(ks[21], (N_B_LAYERS, DIFF_HEAD_DIM), 0.1),
        'b_lambda_k1': nrm(ks[22], (N_B_LAYERS, DIFF_HEAD_DIM), 0.1),
        'b_lambda_q2': nrm(ks[23], (N_B_LAYERS, DIFF_HEAD_DIM), 0.1),
        'b_lambda_k2': nrm(ks[24], (N_B_LAYERS, DIFF_HEAD_DIM), 0.1),
        'b_subln_g': 1.0 + nrm(ks[25], (N_B_LAYERS, DIFF_V_DIM), 0.02),
        'b_w_out': nrm(ks[26], (N_B_LAYERS, D, D), D ** -0.5 * DEEPNORM_BETA),
    }

def reference(x, ffn1_w_gate, ffn1_w_up, ffn1_w_down, ffn2_w_gate, ffn2_w_up, ffn2_w_down,
              ln_g, ln_b, a_w_in, a_cmp_pos_k, a_cmp_w1_k, a_cmp_b1_k, a_cmp_w2_k,
              a_cmp_pos_v, a_cmp_w1_v, a_cmp_b1_v, a_cmp_w2_v, a_w_out,
              b_w_kv_shared, b_w_q, b_lambda_q1, b_lambda_k1, b_lambda_q2, b_lambda_k2,
              b_subln_g, b_w_out):
    S = x.shape[1]
    positions = jnp.arange(S)
    k1 = k2 = v = None
    for layer in range(DEPTH):
        x = post_norm(x, 0.5 * swiglu(x, ffn1_w_gate[layer], ffn1_w_up[layer], ffn1_w_down[layer]),
                      ln_g[layer, 0], ln_b[layer, 0])
        if layer < N_A_LAYERS:
            mix = nsa_mixer(x, a_w_in[layer], a_cmp_pos_k[layer], a_cmp_w1_k[layer], a_cmp_b1_k[layer],
                            a_cmp_w2_k[layer], a_cmp_pos_v[layer], a_cmp_w1_v[layer], a_cmp_b1_v[layer],
                            a_cmp_w2_v[layer], a_w_out[layer], positions)
        else:
            j = layer - N_A_LAYERS
            lambda_init = 0.8 - 0.6 * float(np.exp(-0.3 * layer))
            mix = diff_mixer(x, k1, k2, v, b_w_q[j], b_lambda_q1[j], b_lambda_k1[j], b_lambda_q2[j],
                             b_lambda_k2[j], b_subln_g[j], b_w_out[j], positions, lambda_init)
        x = post_norm(x, mix, ln_g[layer, 1], ln_b[layer, 1])
        x = post_norm(x, 0.5 * swiglu(x, ffn2_w_gate[layer], ffn2_w_up[layer], ffn2_w_down[layer]),
                      ln_g[layer, 2], ln_b[layer, 2])
        if layer == N_A_LAYERS - 1:
            k1, k2, v = shared_kv(x, b_w_kv_shared, positions)
    return x


_drawn_inputs = setup_inputs


def setup_inputs(seed=0):
    import zlib

    import numpy as np

    out = dict(_drawn_inputs(seed))
    spreads = {}
    factors = {'a_cmp_pos_k': 23.298,
     'a_cmp_w1_k': 2.775,
     'a_cmp_b1_k': 64.0,
     'a_cmp_w2_k': 2.895,
     'a_cmp_pos_v': 8.0,
     'a_cmp_b1_v': 8.0,
     'b_lambda_q1': 8.0,
     'b_lambda_k1': 8.0,
     'b_subln_g': 27.523}
    for name, (base, spread) in spreads.items():
        noise = np.random.default_rng([zlib.crc32(name.encode()), seed]).standard_normal(out[name].shape)
        drawn = base * np.exp(spread * noise) if base else spread * noise
        out[name] = __import__('jax').numpy.asarray(drawn.astype(out[name].dtype))
    for name, factor in factors.items():
        out[name] = (out[name] * factor).astype(out[name].dtype)
    return out
```

```python
from contextlib import ExitStack

import concourse.bass as bass
from concourse import mybir

F32 = mybir.dt.float32
F32R = mybir.dt.float32r
BF16 = mybir.dt.bfloat16
ALU = mybir.AluOpType
ACT = mybir.ActivationFunctionType
AX = mybir.AxisListType

P = 128
SEQ, D, FF, DEPTH = 256, 1024, 2816, 2
TOKS = SEQ // P
KT = D // P
FT = FF // P
NSA_HEADS, NSA_GROUPS, DH = 16, 2, 64
CMP_BLOCK, CMP_STRIDE, HID = 32, 16, 128
N_CMP = (SEQ - CMP_BLOCK) // CMP_STRIDE + 1
SLC_BLOCK, SLC_TOPK, WINDOW = 64, 16, 512
DIFF_HEADS, DIFF_V = 8, 128
ROT = DH // 4
KV_COLS = 6 * NSA_GROUPS * DH + 3 * NSA_HEADS
ALPHA = (2 * DEPTH) ** 0.25
EPS = 1e-5
NEG = -1e30
LAMBDA_INIT = 0.8 - 0.6 * 0.7408182206817179

assert SEQ // SLC_BLOCK <= SLC_TOPK and SEQ <= WINDOW
assert TOKS == 2 and KT == 8

C_ID, C_DIAG, C_COS, C_SIN, C_CMP, C_ANY, C_HEAD = 0, 128, 256, 288, 320, 352, 354
C_COLS = 362
KC, VC, KS, VS, KW, VW, GT = 0, 128, 256, 384, 512, 640, 768

SLOTS = 4
UNIT = 2048
G_FULL = FF // 512
HALF = FF - 512 * G_FULL
UNITS_GU = 4 * G_FULL + 2
UNITS_DOWN = FT // 2
UNITS_FFN = UNITS_GU + UNITS_DOWN
DOWN_GROUPS = [[0, 1, 2], [3, 4, 5, 6], [7, 8, 9, 10]]
assert HALF == 256 and DOWN_GROUPS[-1][-1] == UNITS_DOWN - 1

STAGES = ["ffn0", "nsa_in", "nsa_out", "ffn1", "kv", "ffn2", "diff_q", "diff_out", "ffn3"]
STAGE_UNITS = {"nsa_in": 8, "nsa_out": 4, "kv": 8, "diff_q": 4, "diff_out": 4}
STAGE_UNITS.update({f"ffn{i}": UNITS_FFN for i in range(4)})
NORM_OF = {"ffn0": 0, "nsa_out": 1, "ffn1": 2, "ffn2": 3, "diff_out": 4, "ffn3": 5}


def attention_jobs(heads_per_turn):
    jobs, turns = [], []
    for tok in range(TOKS):
        for share in range(2):
            h0 = share * heads_per_turn
            if tok == 0:
                sets = [[h, h + 2] for h in range(h0, h0 + heads_per_turn) if h % 4 < 2]
            else:
                sets = [[h] for h in range(h0, h0 + heads_per_turn)]
            jobs += [(len(turns), tok, heads, heads is sets[-1]) for heads in sets]
            turns.append((tok, share))
    return jobs, turns


NSA_JOBS, NSA_TURNS = attention_jobs(NSA_HEADS // 2)
DIFF_JOBS, DIFF_TURNS = attention_jobs(DIFF_HEADS // 2)


def job_steps(jobs):
    for i in range(len(jobs) + 3):
        yield i, i < len(jobs), 0 <= i - 2 < len(jobs), i - 3


def ends_turn(jobs, j, turn):
    return j >= 0 and jobs[j][3] and jobs[j][0] == turn


def count_events():
    unit, fill, turn = {}, {}, []
    n = 0
    for stage in STAGES:
        unit[stage] = n
        n += STAGE_UNITS[stage]
    e = 1
    for stage in STAGES:
        groups = G_FULL + 2 if stage.startswith("ffn") else 2 if stage in ("nsa_in", "kv") else 1
        for g in range(groups):
            for tok in range(TOKS):
                fill[stage, g, tok] = e
                e += 1

    def pair(*name):
        turn.extend([(*name, 0), (*name, 1)])

    pair("x", "start", 0)
    pair("x", "start", 1)
    for stage in STAGES:
        if stage.startswith("ffn"):
            for g in range(G_FULL + 1):
                turn.extend([("h", stage, g, 0), ("h", stage, g, 1)])
        if stage == "nsa_in":
            turn.extend([("kc", 0), ("kc", 1), ("kr", 0), ("kr", 1)])
            pair("q", 0)
            pair("qr", "nsa", 0)
            pair("q", 1)
            for i, _, tr, pv in job_steps(NSA_JOBS):
                if tr:
                    turn.append(("p", "nsa", i - 2))
                if i == 2:
                    turn.append(("pc",))
                if i == 4:
                    pair("qr", "nsa", 1)
                if ends_turn(NSA_JOBS, pv, 2):
                    pair("x", "nsa_o", 0)
            pair("x", "nsa_o", 1)
        if stage == "kv":
            for tok in range(TOKS):
                pair("k", tok)
        if stage == "diff_q":
            pair("qr", "diff", 0)
            for i, _, tr, pv in job_steps(DIFF_JOBS):
                if tr:
                    turn.append(("p", "diff", i - 2))
                if i == 3:
                    pair("qr", "diff", 1)
                if ends_turn(DIFF_JOBS, pv, 2):
                    pair("x", "diff_o", 0)
            pair("x", "diff_o", 1)
        if stage in NORM_OF and stage != "ffn3":
            for tok in range(TOKS):
                pair("x", stage, tok)
    return unit, fill, {name: i for i, name in enumerate(turn)}, {
        name: i for i, name in enumerate([t for t in turn if t[0] in "xh"])}


UNIT_OF, FILL_OF, TURN_OF, SPLIT_OF = count_events()


def units_through(stage, g):
    if stage.startswith("ffn"):
        in_stage = min(4 * (g + 1), UNITS_GU) if g <= G_FULL else UNITS_FFN
    else:
        in_stage = 4 * (g + 1)
    return UNIT_OF[stage] + in_stage


TILE0_FILLS = {(s, g): e // TOKS + 1 for (s, g, tok), e in FILL_OF.items() if tok == 0}
N_UNITS = UNIT_OF["ffn3"] + UNITS_FFN


def unit_shape(n):
    stage = [s for s in STAGES if UNIT_OF[s] <= n][-1]
    j = n - UNIT_OF[stage]
    if stage.startswith("ffn"):
        return (4, 512) if j < 4 * G_FULL else (8, HALF) if j < UNITS_GU else (2, D)
    if stage in ("nsa_out", "diff_out"):
        return 2, D
    if stage == "nsa_in" and j in (2, 3):
        return 4, KV_COLS - 512
    return 4, 512


def build_program(nc, x_in, const, w_gates, w_ups, w_downs, ln_g, ln_b, w_in, w_out_a, cmp_pos, cmp_w1, cmp_b1,
                  cmp_w2, w_kv, w_q, lambdas, subln_g, w_out_b, out):
    with ExitStack() as ctx:
        def sb(name, shape, dt=F32, scope=ctx):
            return scope.enter_context(nc.sbuf_tensor(name, shape, dt))

        def sem(name):
            return ctx.enter_context(nc.semaphore(name))

        raw = sb("raw", [P, SLOTS, UNIT])
        w_hi = sb("w_hi", [P, SLOTS, UNIT], F32R)
        w_lo = sb("w_lo", [P, SLOTS, UNIT], F32R)
        x = sb("x", [P, TOKS, D])
        y = sb("y", [P, TOKS, D])
        xt_hi = sb("xt_hi", [P, KT, SEQ], F32R)
        xt_lo = sb("xt_lo", [P, KT, SEQ], F32R)
        norm_gb = sb("norm_gb", [P, 2, D])
        w1k = norm_gb[:].rearrange("p a (b h) -> p (a b) h", h=HID)
        cst = sb("cst", [P, C_COLS])
        id_bf = sb("id_bf", [P, P], BF16)
        diag_bf = sb("diag_bf", [P, P], BF16)
        pos_sb = sb("pos_sb", [P, 2, CMP_BLOCK // 2])
        b1_sb = sb("b1_sb", [P, 2])
        w2_sb = sb("w2_sb", [P, 2, DH])
        w2k2 = sb("w2k2", [P, 2, DH])
        lam_in = sb("lam_in", [P, 4, DH])
        lam_pr = sb("lam_pr", [P, 2, DH])
        lam = sb("lam", [P, 4])
        sub_g = sb("sub_g", [P, DIFF_V])
        half_pow = sb("half_pow", [P, 4])
        stats = sb("stats", [P, TOKS, 2, 6])
        mean_var = sb("mean_var", [P, TOKS, 2])
        rstd = sb("rstd", [P, TOKS, 2])
        rope_a = sb("rope_a", [P, 16, ROT])
        rope_b = sb("rope_b", [P, 16, ROT])
        neg_max = sb("neg_max", [P, 3, 4])
        sums = sb("sums", [P, TOKS, 2, NSA_HEADS])
        share = sb("share", [P, 2, NSA_HEADS])
        rms = sb("rms", [P, 2, 4])

        late = ExitStack()
        with late:
            kt_b = sb("kt_b", [P, KT, SEQ], scope=late)
            v_b = sb("v_b", [P, TOKS, D], scope=late)
            ffn = ExitStack()
            with ffn:
                ht_hi = sb("ht_hi", [P, FT, SEQ], F32R, ffn)
                ht_lo = sb("ht_lo", [P, FT, SEQ], F32R, ffn)
            dif = ExitStack()
            with dif:
                dq = sb("dq", [P, TOKS, D], scope=dif)
                dqt = sb("dqt", [P, KT, SEQ], scope=dif)
                dp = sb("dp", [P, 3, 512], scope=dif)
        nsa = ExitStack()
        with nsa:
            kv_a = sb("kv_a", [P, TOKS, KV_COLS], scope=nsa)
            nq = sb("nq", [P, TOKS, D], scope=nsa)
            nqt = sb("nqt", [P, KT, SEQ], scope=nsa)
            nqrt = sb("nqrt", [P, KT, SEQ], scope=nsa)
            kt_a = sb("kt_a", [P, 2, NSA_GROUPS, SEQ], scope=nsa)
            blk = sb("blk", [P, 2, CMP_BLOCK // 2, NSA_GROUPS * N_CMP], scope=nsa)
            w1v = sb("w1v", [P, CMP_BLOCK // 2, HID], scope=nsa)
            hid = sb("hid", [P, 2, NSA_GROUPS * N_CMP], scope=nsa)
            hid_rep = sb("hid_rep", [P, NSA_GROUPS, 8, 16], scope=nsa)
            kcb = sb("kcb", [P, NSA_GROUPS, 2, 16], scope=nsa)
            vcb = sb("vcb", [P, NSA_GROUPS, 8, DH], scope=nsa)
            cs = sb("cs", [P, TOKS, NSA_HEADS, 16], scope=nsa)
            cmax = sb("cmax", [P, TOKS, NSA_HEADS], scope=nsa)
            csum = sb("csum", [P, TOKS, NSA_HEADS], scope=nsa)
            pct = sb("pct", [P, 4, P], scope=nsa)
            gate = sb("gate", [P, TOKS, 3 * NSA_HEADS], scope=nsa)
            np_ = sb("np_", [P, 3, 512], scope=nsa)
        sil = y[:, :, 0:512]
        h_nat = y[:, :, 512:1024]
        npt = dpt = y[:, 0, :].rearrange("p (a c) -> p a c", a=2)
        ntmp = dtmp = y[:, 1, 0:512]

        acc = ctx.enter_context(nc.psum_tensor("acc", [P, 4, 512], F32))
        trb = ctx.enter_context(nc.psum_tensor("trb", [P, 2, 512], F32))
        aux = ctx.enter_context(nc.psum_tensor("aux", [P, 2, 512], F32))
        score_bank = [acc[:, 0], acc[:, 1], aux[:, 0]]

        const_in = sem("const_in")
        x_landed = sem("x_landed")
        small_in = sem("small_in")
        norm_in = sem("norm_in")
        w1_in = sem("w1_in")
        raw_in = [sem(f"raw_in{i}") for i in range(SLOTS)]
        hi_ready = sem("hi_ready")
        lo_ready = sem("lo_ready")
        unit_used = sem("unit_used")
        tile0_full = sem("tile0_full")
        acc_free = sem("acc_free")
        silu_done = sem("silu_done")
        tr_full = sem("tr_full")
        tr_hi = sem("tr_hi")
        tr_free = sem("tr_free")
        x_ready = sem("x_ready")
        stats_ready = sem("stats_ready")
        rstd_ready = sem("rstd_ready")
        masks_ready = sem("masks_ready")
        rope_done = sem("rope_done")
        k_dup = sem("k_dup")
        hid_full = sem("hid_full")
        hid_ready = sem("hid_ready")
        cmp_full = sem("cmp_full")
        cmp_ready = sem("cmp_ready")
        cs_full = sem("cs_full")
        cs_shifted = sem("cs_shifted")
        cs_copied = sem("cs_copied")
        cexp_done = sem("cexp_done")
        gate_exp = sem("gate_exp")
        score_full = sem("score_full")
        max_ready = sem("max_ready")
        exp_done = sem("exp_done")
        turn_full = sem("turn_full")
        turn_mixed = sem("turn_mixed")
        lam_sum = sem("lam_sum")
        lam_exp = sem("lam_exp")
        dve_step = sem("dve_step")
        pool_step = sem("pool_step")
        rms_ready = sem("rms_ready")
        rms_pow = sem("rms_pow")
        out_done = sem("out_done")

        ident = cst[:, C_ID:C_ID + P]
        cos2 = cst[:, C_COS:C_COS + 32].rearrange("p (t r) -> p t r", t=TOKS)
        sin2 = cst[:, C_SIN:C_SIN + 32].rearrange("p (t r) -> p t r", t=TOKS)
        cmp_mask = cst[:, C_CMP:C_CMP + 32].rearrange("p (t c) -> p t c", t=TOKS)

        def weights(buf, n):
            k, c = unit_shape(n)
            return buf[:, n % SLOTS, 0:k * c].rearrange("p (k c) -> p k c", k=k)

        def rows(w, r0, k, c0, c):
            return w[r0:r0 + k * P, c0:c0 + c].rearrange("(k p) c -> p k c", p=P)

        def bc(ap, *shape):
            return ap.broadcast_to(list(shape))

        def filled(eng, stage, g, tok):
            if tok == 0:
                eng.wait_ge(tile0_full, TILE0_FILLS[stage, g])
            else:
                eng.wait_ge(unit_used, units_through(stage, g))

        block = ctx.enter_context(nc.Block())

        @block.sync
        def _(sp):
            sp.dma_start(cst[:], const).then_inc(const_in, 16)
            for tok in range(TOKS):
                sp.dma_start(x[:, tok, :], x_in[tok * P:(tok + 1) * P, :]).then_inc(x_landed, 16)

            def load(n, src, freed=None):
                if freed is not None:
                    sp.wait_ge(lo_ready, freed)
                elif n >= SLOTS:
                    sp.wait_ge(lo_ready, n - SLOTS + 1)
                sp.dma_start(weights(raw, n), src).then_inc(raw_in[n % SLOTS], 16)

            def load_ffn(stage):
                i = int(stage[3])
                n0 = UNIT_OF[stage]
                wg, wu, wd = w_gates[i], w_ups[i], w_downs[i]

                def group(g, peeled):
                    for j, (w, half) in enumerate([(wg, 0), (wg, 1), (wu, 0), (wu, 1)]):
                        src = w[half * 512:(half + 1) * 512, bass.ds(g * 512, 512)].rearrange(
                            "(k p) c -> p k c", p=P)
                        load(n0 + j, src, None if peeled else g * 4 + (n0 + j - SLOTS + 1))

                group(0, True)
                with sp.Fori(1, G_FULL) as g:
                    group(g, False)
                load(n0 + 4 * G_FULL, rows(wg, 0, KT, 512 * G_FULL, HALF))
                load(n0 + 4 * G_FULL + 1, rows(wu, 0, KT, 512 * G_FULL, HALF))
                for j in range(UNITS_DOWN):
                    load(n0 + UNITS_GU + j, rows(wd, 2 * P * j, 2, 0, D))

            def load_columns(stage, w, chunks):
                n = UNIT_OF[stage]
                for c0, c in chunks:
                    for half in range(2):
                        load(n, rows(w, half * 512, 4, c0, c))
                        n += 1

            def load_rows(stage, w):
                for j in range(KT // 2):
                    load(UNIT_OF[stage] + j, rows(w, 2 * P * j, 2, 0, D))

            load_ffn("ffn0")
            load_columns("nsa_in", w_in, [(D, 512), (D + 512, KV_COLS - 512), (0, 512), (512, 512)])
            load_rows("nsa_out", w_out_a)
            load_ffn("ffn1")
            load_columns("kv", w_kv, [(c, 512) for c in range(0, 2 * D, 512)])
            load_ffn("ffn2")
            load_columns("diff_q", w_q, [(0, 512), (512, 512)])
            load_rows("diff_out", w_out_b)
            load_ffn("ffn3")
            for tok in range(TOKS):
                sp.wait_ge(x_ready, 2 * len(NORM_OF) - 1 + tok)
                sp.dma_start(out[tok * P:(tok + 1) * P, :], x[:, tok, :]).then_inc(out_done, 16)
            sp.wait_ge(out_done, 16 * TOKS)

        @block.gpsimd
        def _(pool):
            step = [0]

            def link(ins):
                step[0] += 1
                ins.then_inc(pool_step, 1)
                pool.wait_ge(pool_step, step[0])

            small = 0
            for dst, src in ((pos_sb[:], cmp_pos.rearrange("b p l -> p b l")), (b1_sb[:], cmp_b1),
                             (w2_sb[:], cmp_w2.rearrange("b h d -> h b d")),
                             (lam_in[:], lambdas.partition_broadcast(P)), (sub_g[:], subln_g.partition_broadcast(P))):
                pool.dma_start(dst, src).then_inc(small_in, 16)

            def load_norm(k):
                if k:
                    pool.wait_ge(x_ready, 2 * k)
                if k == 1:
                    pool.wait_ge(hid_full, 1)
                for j, w in enumerate((ln_g, ln_b)):
                    pool.dma_start(norm_gb[:, j, :], w[k].partition_broadcast(P)).then_inc(norm_in, 16)

            def inverse_root(k):
                for tok in range(TOKS):
                    pool.wait_ge(stats_ready, 2 * k + tok + 1)
                    link(pool.tensor_scalar(rstd[:, tok, 0:1], mean_var[:, tok, 1:2], EPS, None, ALU.add))
                    pool.tensor_tensor(rstd[:, tok, 1:2], rstd[:, tok, 0:1], half_pow[:, 0:1],
                                       ALU.pow).then_inc(rstd_ready, 1)

            def rotate(v, tok, heads):
                a, b = rope_a[:, 0:heads], rope_b[:, 0:heads]
                r, h = v[:, :, 0:ROT], ROT // 2
                link(pool.tensor_tensor(a, r, bc(cos2[:, tok:tok + 1, :], P, heads, ROT), ALU.mult))
                link(pool.tensor_tensor(b, r, bc(sin2[:, tok:tok + 1, :], P, heads, ROT), ALU.mult))
                link(pool.tensor_tensor(v[:, :, 0:h], a[:, :, 0:h], b[:, :, h:ROT], ALU.subtract))
                return pool.tensor_tensor(v[:, :, h:ROT], b[:, :, 0:h], a[:, :, h:ROT], ALU.add)

            def heads_of(v, tok, c0, heads):
                return v[:, tok, c0:c0 + heads * DH].rearrange("p (h d) -> p h d", d=DH)

            link(pool.memset(half_pow[:], -0.5))
            load_norm(0)
            pool.wait_ge(const_in, 16)
            inverse_root(0)
            pool.wait_ge(x_ready, 2)
            pool.dma_start(w1k, cmp_w1[0].rearrange("(l p) h -> p l h", p=P)).then_inc(w1_in, 16)
            pool.dma_start(w1v[:], cmp_w1[1].rearrange("(l p) h -> p l h", p=P)).then_inc(w1_in, 16)
            for tok in range(TOKS):
                pool.wait_ge(acc_free, FILL_OF["nsa_in", 0, tok] + 1)
                for j, c in enumerate((KC, VC)):
                    dst = y[:, tok, j * 256:(j + 1) * 256].rearrange("p (g r d) -> p g r d", g=2, r=2)
                    for r in range(2):
                        ins = pool.tensor_copy(dst[:, :, r, :], heads_of(kv_a, tok, c, 2))
                ins.then_inc(k_dup, 1)
            for tok in range(TOKS):
                for j, c in enumerate((KS, KW)):
                    link(rotate(heads_of(kv_a, tok, c, 2), tok, 2))
                    dst = y[:, tok, 512 + j * 256:512 + (j + 1) * 256].rearrange("p (g r d) -> p g r d", g=2, r=2)
                    for r in range(2):
                        ins = pool.tensor_copy(dst[:, :, r, :], heads_of(kv_a, tok, c, 2))
                ins.then_inc(k_dup, 1)
            for tok in range(TOKS):
                pool.wait_ge(acc_free, FILL_OF["nsa_in", 1, tok] + 1)
                pool.wait_ge(tr_full, TURN_OF["q", tok, 1] + 1)
                if tok:
                    pool.wait_ge(rope_done, 1)
                rotate(heads_of(nq, tok, 0, 16), tok, 16).then_inc(rope_done, 1)
            load_norm(1)
            inverse_root(1)
            load_norm(2)
            inverse_root(2)
            for tok in range(TOKS):
                pool.wait_ge(acc_free, FILL_OF["kv", 0, tok] + 1)
                if tok:
                    pool.wait_ge(rope_done, 3)
                rotate(heads_of(y, tok, 0, 16), tok, 16).then_inc(rope_done, 1)
            load_norm(3)
            inverse_root(3)
            for tok in range(TOKS):
                pool.wait_ge(acc_free, FILL_OF["diff_q", 0, tok] + 1)
                if tok:
                    pool.wait_ge(rope_done, 5)
                rotate(heads_of(dq, tok, 0, 16), tok, 16).then_inc(rope_done, 1)
            load_norm(4)
            for k in range(len(DIFF_TURNS)):
                pool.wait_ge(rms_ready, k + 1)
                pool.tensor_tensor(rms[:, 1, :], rms[:, 0, :], half_pow[:], ALU.pow).then_inc(rms_pow, 1)
            inverse_root(4)
            load_norm(5)
            inverse_root(5)

        @block.scalar
        def _(act):
            def split_unit(n, slot, in_count, used):
                act.wait_ge(raw_in[slot], in_count)
                if used is not None:
                    act.wait_ge(unit_used, used)
                k, c = unit_shape(n)
                act.activation(w_hi[:, slot, 0:k * c], raw[:, slot, 0:k * c], ACT.Copy).then_inc(hi_ready, 1)

            def split_units(n0, n1):
                for n in range(n0, min(n1, N_UNITS)):
                    split_unit(n, n % SLOTS, 16 * (n // SLOTS + 1), n - SLOTS + 1 if n >= SLOTS else None)

            def high_part(name, dst):
                act.wait_ge(tr_full, TURN_OF[name] + 1)
                act.activation(dst, trb[:, TURN_OF[name] % 2].rearrange("p (k c) -> p k c", c=P), ACT.Copy).then_inc(
                    tr_hi, 1)

            def x_high(of, tok):
                for part in range(2):
                    high_part(("x", of, tok, part), xt_hi[:, 4 * part:4 * part + 4, tok * P:(tok + 1) * P])

            def ffn_stage(stage, pending):
                n0, e0, t0 = UNIT_OF[stage], FILL_OF[stage, 0, 0], TURN_OF["h", stage, 0, 0]
                pending()

                def silu(tok, c):
                    act.activation(sil[:, tok, 0:c], acc[:, 2 * tok, 0:c], ACT.Silu).then_inc(silu_done, 1)

                def h_high(t, bank, g, tok, k):
                    act.wait_ge(tr_full, t + 1)
                    act.activation(ht_hi[:, bass.ds(4 * g, k), tok * P:(tok + 1) * P],
                                   trb[:, bank, 0:k * P].rearrange("p (k c) -> p k c", c=P),
                                   ACT.Copy).then_inc(tr_hi, 1)

                with act.Fori(0, G_FULL - 1) as g:
                    act.wait_ge(tile0_full, g + TILE0_FILLS[stage, 0])
                    silu(0, 512)
                    for j in range(4):
                        n = n0 + 4 + j
                        split_unit(n, n % SLOTS, g * 16 + 16 * (n // SLOTS + 1), g * 4 + (n - SLOTS + 1))
                    act.wait_ge(unit_used, 4 * g + (n0 + 4))
                    silu(1, 512)
                    h_high(2 * g + t0, t0 % 2, g, 0, 4)
                    h_high(2 * g + (t0 + 1), (t0 + 1) % 2, g, 1, 4)
                for g in (G_FULL - 1, G_FULL):
                    c = 512 if g < G_FULL else HALF
                    filled(act, stage, g, 0)
                    silu(0, c)
                    n = n0 + 4 * (g + 1)
                    split_units(n, n + c // 128)
                    filled(act, stage, g, 1)
                    silu(1, c)
                    for tok in range(TOKS):
                        h_high(t0 + 2 * g + tok, (t0 + tok) % 2, g, tok, c // P)
                n = n0 + UNITS_GU + SLOTS
                for grp in DOWN_GROUPS[:-1]:
                    split_units(n - 2 + 0, n - 2 + len(grp)) if False else None
                split_units(n0 + UNITS_GU + 4, n0 + UNITS_FFN + 2)
                if stage != "ffn3":
                    x_high(stage, 0)
                split_units(n0 + UNITS_FFN + 2, n0 + UNITS_FFN + 4)

            def exps(kind, jobs, i, base, s_sb, p_sb):
                turn, tok, heads, _ = jobs[i]
                width = P * (tok + 1)
                act.wait_ge(max_ready, base + i + 1)
                if i >= 3:
                    act.wait_ge(tr_full, TURN_OF["p", kind, i - 3] + 1)
                k = 0
                for h in heads:
                    for m in range(2):
                        ins = act.activation(p_sb[:, i % 3, k * width:(k + 1) * width],
                                             score_bank[i % 3][:, k * width:(k + 1) * width], ACT.Exp,
                                             bias=neg_max[:, i % 3, k:k + 1],
                                             accum_out=sums[:, tok, m, h:h + 1])
                        k += 1
                ins.then_inc(exp_done, 1)

            split_units(0, 4)
            x_high("start", 0)
            ffn_stage("ffn0", lambda: x_high("start", 1))

            n0 = UNIT_OF["nsa_in"]
            x_high("ffn0", 1)
            split_units(n0 + 4, n0 + 8)
            split_units(n0 + 8, n0 + 12)
            act.wait_ge(acc_free, FILL_OF["nsa_in", 0, 1] + 1)
            for tok in range(TOKS):
                ins = act.activation(gate[:, tok, :], kv_a[:, tok, GT:GT + 48], ACT.Exp, scale=-1.0)
            ins.then_inc(gate_exp, 1)
            act.wait_ge(small_in, 80)
            for b in range(2):
                act.wait_ge(hid_full, b + 1)
                act.activation(hid[:, b, :], aux[:, b, 0:2 * N_CMP], ACT.Gelu_apprx_tanh,
                               bias=b1_sb[:, b:b + 1]).then_inc(hid_ready, 1)
            for tok in range(TOKS):
                act.wait_ge(cs_shifted, tok + 1)
                act.activation(cs[:, tok], cs[:, tok], ACT.Exp).then_inc(cexp_done, 1)
            for i, sc, tr, pv in job_steps(NSA_JOBS):
                if sc:
                    exps("nsa", NSA_JOBS, i, 0, None, np_)
                if ends_turn(NSA_JOBS, pv, 2):
                    x_high("nsa_o", 0)
            x_high("nsa_o", 1)
            n0 = UNIT_OF["nsa_out"]
            split_units(n0 + 4, n0 + 6)
            x_high("nsa_out", 0)
            split_units(n0 + 6, n0 + 8)
            ffn_stage("ffn1", lambda: x_high("nsa_out", 1))

            n0 = UNIT_OF["kv"]
            x_high("ffn1", 1)
            split_units(n0 + 4, n0 + 12)
            ffn_stage("ffn2", lambda: None)

            n0 = UNIT_OF["diff_q"]
            x_high("ffn2", 1)
            split_units(n0 + 4, n0 + 8)
            act.wait_ge(lam_sum, 1)
            act.activation(lam[:, 0:2], lam[:, 0:2], ACT.Exp).then_inc(lam_exp, 1)
            for i, sc, tr, pv in job_steps(DIFF_JOBS):
                if sc:
                    exps("diff", DIFF_JOBS, i, len(NSA_JOBS), None, dp)
                if ends_turn(DIFF_JOBS, pv, 2):
                    x_high("diff_o", 0)
            x_high("diff_o", 1)
            n0 = UNIT_OF["diff_out"]
            split_units(n0 + 4, n0 + 6)
            x_high("diff_out", 0)
            split_units(n0 + 6, n0 + 8)
            ffn_stage("ffn3", lambda: x_high("diff_out", 1))

        @block.vector
        def _(dve):
            step = [0]

            def link(ins):
                step[0] += 1
                ins.then_inc(dve_step, 1)
                dve.wait_ge(dve_step, step[0])

            def split_unit(n, slot, ready):
                dve.wait_ge(hi_ready, ready)
                k, c = unit_shape(n)
                dve.tensor_tensor(w_lo[:, slot, 0:k * c], raw[:, slot, 0:k * c],
                                  w_hi[:, slot, 0:k * c].bitcast(F32), ALU.subtract).then_inc(lo_ready, 1)

            def split_units(n0, n1):
                for n in range(n0, min(n1, N_UNITS)):
                    split_unit(n, n % SLOTS, n + 1)

            def low_part(name, hi, lo):
                t = TURN_OF[name]
                dve.wait_ge(tr_hi, SPLIT_OF[name] + 1)
                dve.tensor_tensor(lo, trb[:, t % 2].rearrange("p (k c) -> p k c", c=P), hi.bitcast(F32),
                                  ALU.subtract).then_inc(tr_free, 1)

            def x_low(of, tok):
                for part in range(2):
                    at = slice(4 * part, 4 * part + 4), slice(tok * P, (tok + 1) * P)
                    low_part(("x", of, tok, part), xt_hi[:, at[0], at[1]], xt_lo[:, at[0], at[1]])

            def copy_turned(name, dst, k=4):
                t = TURN_OF[name]
                dve.wait_ge(tr_full, t + 1)
                dve.tensor_copy(dst, trb[:, t % 2].rearrange("p (k c) -> p k c", k=k)).then_inc(tr_free, 1)

            def norm(stage, tok):
                k = NORM_OF[stage]
                group = G_FULL + 1 if stage.startswith("ffn") else 0
                e = FILL_OF[stage, group, tok]
                filled(dve, stage, group, tok)
                dve.scalar_tensor_tensor(y[:, tok, :], x[:, tok, :], ALPHA,
                                         acc[:, 2 * tok:2 * tok + 2].rearrange("p a c -> p (a c)"),
                                         ALU.mult, ALU.add).then_inc(acc_free, 1)
                dve.wait_ge(acc_free, e + 1)
                for half in range(2):
                    ins = dve.bn_stats(stats[:, tok, half, :], y[:, tok, half * 512:(half + 1) * 512])
                link(ins)
                dve.bn_aggr(mean_var[:, tok, :], stats[:, tok].rearrange("p a b -> p (a b)")).then_inc(stats_ready, 1)
                dve.wait_ge(stats_ready, 2 * k + tok + 1)
                dve.wait_ge(norm_in, 32 * (k + 1))
                link(dve.scalar_tensor_tensor(y[:, tok, :], y[:, tok, :], mean_var[:, tok, 0:1], norm_gb[:, 0, :],
                                              ALU.subtract, ALU.mult))
                dve.wait_ge(rstd_ready, 2 * k + tok + 1)
                dve.scalar_tensor_tensor(x[:, tok, :], y[:, tok, :], rstd[:, tok, 1:2], norm_gb[:, 1, :],
                                         ALU.mult, ALU.add).then_inc(x_ready, 1)

            def ffn_stage(stage, pending):
                n0, e0, s0 = UNIT_OF[stage], FILL_OF[stage, 0, 0], SPLIT_OF["h", stage, 0, 0]
                t0 = TURN_OF["h", stage, 0, 0]
                i0 = 2 * (G_FULL + 1) * int(stage[3])
                pending()

                def gated(i, tok, c):
                    dve.wait_ge(silu_done, i + 1)
                    dve.scalar_tensor_tensor(h_nat[:, tok, 0:c], sil[:, tok, 0:c], 0.5, acc[:, 2 * tok + 1, 0:c],
                                             ALU.mult, ALU.mult).then_inc(acc_free, 1)

                def h_low(s, bank, g, tok, k):
                    dve.wait_ge(tr_hi, s + 1)
                    dve.tensor_tensor(ht_lo[:, bass.ds(4 * g, k), tok * P:(tok + 1) * P],
                                      trb[:, bank, 0:k * P].rearrange("p (k c) -> p k c", c=P),
                                      ht_hi[:, bass.ds(4 * g, k), tok * P:(tok + 1) * P].bitcast(F32),
                                      ALU.subtract).then_inc(tr_free, 1)

                with dve.Fori(0, G_FULL - 1) as g:
                    gated(2 * g + i0, 0, 512)
                    for j in range(4):
                        n = n0 + 4 + j
                        split_unit(n, n % SLOTS, 4 * g + (n + 1))
                    gated(2 * g + (i0 + 1), 1, 512)
                    h_low(2 * g + s0, t0 % 2, g, 0, 4)
                    h_low(2 * g + (s0 + 1), (t0 + 1) % 2, g, 1, 4)
                for g in (G_FULL - 1, G_FULL):
                    c = 512 if g < G_FULL else HALF
                    gated(i0 + 2 * g, 0, c)
                    n = n0 + 4 * (g + 1)
                    split_units(n, n + c // 128)
                    gated(i0 + 2 * g + 1, 1, c)
                    for tok in range(TOKS):
                        h_low(s0 + 2 * g + tok, (t0 + tok) % 2, g, tok, c // P)
                split_units(n0 + UNITS_GU + 4, n0 + UNITS_FFN)
                norm(stage, 0)
                split_units(n0 + UNITS_FFN, n0 + UNITS_FFN + 2)
                if stage != "ffn3":
                    x_low(stage, 0)
                split_units(n0 + UNITS_FFN + 2, n0 + UNITS_FFN + 3)
                norm(stage, 1)
                split_units(n0 + UNITS_FFN + 3, n0 + UNITS_FFN + 4)

            def out_stage(stage):
                n = UNIT_OF[stage] + 4
                norm(stage, 0)
                split_units(n, n + 2)
                x_low(stage, 0)
                split_units(n + 2, n + 3)
                norm(stage, 1)
                split_units(n + 3, n + 4)

            def maxima(jobs, i, base):
                _, tok, heads, _ = jobs[i]
                maps = 2 * len(heads)
                dve.wait_ge(score_full, base + i + 1)
                dve.tensor_reduce(neg_max[:, i % 3, 0:maps],
                                  score_bank[i % 3].rearrange("p (m k) -> p m k", m=maps), AX.X, ALU.max,
                                  negate=True).then_inc(max_ready, 1)

            dve.wait_ge(const_in, 16)
            dve.tensor_copy(id_bf[:], ident).then_inc(acc_free, 1)
            dve.tensor_copy(diag_bf[:], cst[:, C_DIAG:C_DIAG + P]).then_inc(masks_ready, 1)
            split_units(0, 2)
            x_low("start", 0)
            split_units(2, 4)
            ffn_stage("ffn0", lambda: x_low("start", 1))

            n0 = UNIT_OF["nsa_in"]
            x_low("ffn0", 1)
            dve.wait_ge(small_in, 80)
            dve.tensor_copy(w2k2[:, 0, :], w2_sb[:, 0, :])
            dve.tensor_copy(w2k2[:, 1, :], w2_sb[:, 0, :])
            dve.memset(hid_rep[:], 0.0)
            link(dve.memset(kcb[:], 0.0))
            for tok in range(TOKS):
                filled(dve, "nsa_in", 0, tok)
                dve.tensor_copy(kv_a[:, tok, :], acc[:, 2 * tok:2 * tok + 2].rearrange("p a c -> p (a c)")[
                    :, 0:KV_COLS]).then_inc(acc_free, 1)
                split_units(n0 + 4 + 2 * tok, n0 + 6 + 2 * tok)
            for b in range(2):
                t = TURN_OF["kc", b]
                dve.wait_ge(tr_full, t + 1)
                for g in range(NSA_GROUPS):
                    for r in range(2):
                        rr = slice(r * DH, (r + 1) * DH)
                        lanes = trb[rr, t % 2, g * SEQ:(g + 1) * SEQ].rearrange("p (c l r) -> p c l r", l=8, r=2)
                        for a in range(2):
                            ins = dve.tensor_tensor(
                                blk[rr, b, 8 * a:8 * a + 8, g * N_CMP:(g + 1) * N_CMP],
                                lanes[:, a:a + N_CMP, :, r].rearrange("p c l -> p l c"),
                                bc(pos_sb[rr, b, 8 * a:8 * a + 8].unsqueeze(2), DH, 8, N_CMP), ALU.add)
                ins.then_inc(tr_free, 1)
            for j in range(2):
                copy_turned(("kr", j), kt_a[:, j], k=2)
            filled(dve, "nsa_in", 1, 0)
            dve.tensor_scalar(nq[:, 0, :], acc[:, 0:2].rearrange("p a c -> p (a c)"), DH ** -0.5, None,
                              ALU.mult).then_inc(acc_free, 1)
            split_units(n0 + 8, n0 + 10)
            for part in range(2):
                copy_turned(("q", 0, part), nqt[:, 4 * part:4 * part + 4, 0:P])
            filled(dve, "nsa_in", 1, 1)
            dve.tensor_scalar(nq[:, 1, :], acc[:, 2:4].rearrange("p a c -> p (a c)"), DH ** -0.5, None,
                              ALU.mult).then_inc(acc_free, 1)
            dve.wait_ge(gate_exp, 1)
            gates = gate[:].rearrange("p t c -> p (t c)")
            link(dve.tensor_scalar(gates, gates, 1.0, None, ALU.add))
            link(dve.reciprocal(gates, gates))
            dve.wait_ge(hid_ready, 2)
            for g in range(NSA_GROUPS):
                ins = dve.tensor_copy(hid_rep[:, g, :, 0:N_CMP],
                                      bc(hid[:, 1:2, g * N_CMP:(g + 1) * N_CMP], P, 8, N_CMP))
            ins.then_inc(cmp_ready, 1)
            dve.wait_ge(cmp_full, 1)
            for r in range(2):
                rr = slice(r * DH, (r + 1) * DH)
                ins = dve.tensor_copy(kcb[rr, :, r, 0:N_CMP],
                                      aux[rr, 0, 64:64 + 2 * N_CMP].rearrange("p (g c) -> p g c", g=2))
            ins.then_inc(cmp_ready, 1)
            dve.wait_ge(cmp_full, 2)
            heads8 = cst[:, C_HEAD:C_HEAD + 8].unsqueeze(2)
            for g in range(NSA_GROUPS):
                ins = dve.tensor_tensor(vcb[:, g], bc(aux[:, 1, 64 + g * DH:64 + (g + 1) * DH].unsqueeze(1), P, 8, DH),
                                        bc(heads8, P, 8, DH), ALU.mult)
            ins.then_inc(cmp_ready, 1)
            for part in range(2):
                copy_turned(("qr", "nsa", 0, part), nqrt[:, 4 * part:4 * part + 4, 0:P])
            for part in range(2):
                copy_turned(("q", 1, part), nqt[:, 4 * part:4 * part + 4, P:SEQ])
            split_units(n0 + 10, n0 + 12)
            for tok in range(TOKS):
                dve.wait_ge(cs_full, tok + 1)
                dve.tensor_tensor(cs[:, tok], aux[:, tok, 0:256].rearrange("p (h c) -> p h c", c=16),
                                  bc(cmp_mask[:, tok:tok + 1, :], P, NSA_HEADS, 16), ALU.add).then_inc(cs_copied, 1)
                dve.wait_ge(cs_copied, tok + 1)
                link(dve.tensor_reduce(cmax[:, tok, :], cs[:, tok], AX.X, ALU.max))
                dve.tensor_tensor(cs[:, tok], cs[:, tok], bc(cmax[:, tok, :].unsqueeze(2), P, NSA_HEADS, 16),
                                  ALU.subtract).then_inc(cs_shifted, 1)
            for tok in range(TOKS):
                dve.wait_ge(cexp_done, tok + 1)
                link(dve.tensor_reduce(csum[:, tok, :], cs[:, tok], AX.X, ALU.add))
                link(dve.reciprocal(csum[:, tok, :], csum[:, tok, :]))
                link(dve.scalar_tensor_tensor(csum[:, tok, :], csum[:, tok, :], cst[:, C_ANY + tok:C_ANY + tok + 1],
                                              gate[:, tok, 0:NSA_HEADS], ALU.mult, ALU.mult))

            def nsa_mix(turn):
                tok, g = NSA_TURNS[turn]
                h0 = g * 8
                heads = slice(h0, h0 + 8)
                dve.wait_ge(turn_full, turn + 1)
                link(dve.reciprocal(share[:, :, 0:8], sums[:, tok, :, heads]))
                link(dve.tensor_tensor(share[:, :, 0:8], share[:, :, 0:8],
                                       gate[:, tok, NSA_HEADS:].rearrange("p (m h) -> p m h", m=2)[:, :, heads],
                                       ALU.mult))
                o = nq[:, tok, h0 * DH:(h0 + 8) * DH].rearrange("p (h d) -> p h d", d=DH)
                t = ntmp.rearrange("p (h d) -> p h d", d=DH)
                parts = [(aux[:, 1], csum[:, tok, heads]), (acc[:, 2], share[:, 0, 0:8]), (acc[:, 3], share[:, 1, 0:8])]
                for j, (bank, f) in enumerate(parts):
                    ins = dve.tensor_tensor(t if j else o, bank.rearrange("p (h d) -> p h d", d=DH),
                                            bc(f.unsqueeze(2), P, 8, DH), ALU.mult)
                    link(ins)
                    if j:
                        ins = dve.tensor_tensor(o, o, t, ALU.add)
                        if j < 2:
                            link(ins)
                ins.then_inc(turn_mixed, 1)

            for i, sc, tr, pv in job_steps(NSA_JOBS):
                if sc:
                    maxima(NSA_JOBS, i, 0)
                if tr:
                    copy_turned(("p", "nsa", i - 2), npt[:, i % 2].rearrange("p (k c) -> p k c", k=4))
                if i == 2:
                    copy_turned(("pc",), pct[:])
                if i == 4:
                    for part in range(2):
                        copy_turned(("qr", "nsa", 1, part), nqrt[:, 4 * part:4 * part + 4, P:SEQ])
                if pv >= 0 and NSA_JOBS[pv][3]:
                    nsa_mix(NSA_JOBS[pv][0])
                if ends_turn(NSA_JOBS, pv, 2):
                    x_low("nsa_o", 0)
            x_low("nsa_o", 1)
            out_stage("nsa_out")
            ffn_stage("ffn1", lambda: x_low("nsa_out", 1))

            n0 = UNIT_OF["kv"]
            x_low("ffn1", 1)
            for tok in range(TOKS):
                filled(dve, "kv", 0, tok)
                dve.tensor_copy(y[:, tok, :], acc[:, 2 * tok:2 * tok + 2].rearrange("p a c -> p (a c)")).then_inc(
                    acc_free, 1)
                split_units(n0 + 4 + 2 * tok, n0 + 6 + 2 * tok)
            for tok in range(TOKS):
                for part in range(2):
                    copy_turned(("k", tok, part), kt_b[:, 4 * part:4 * part + 4, tok * P:(tok + 1) * P])
                filled(dve, "kv", 1, tok)
                dve.tensor_copy(v_b[:, tok, :], acc[:, 2 * tok:2 * tok + 2].rearrange("p a c -> p (a c)")).then_inc(
                    acc_free, 1)
                split_units(n0 + 8 + 2 * tok, n0 + 10 + 2 * tok)
            ffn_stage("ffn2", lambda: None)

            n0 = UNIT_OF["diff_q"]
            x_low("ffn2", 1)
            link(dve.tensor_tensor(lam_pr[:], lam_in[:, 0:4:2, :], lam_in[:, 1:4:2, :], ALU.mult))
            dve.tensor_reduce(lam[:, 0:2], lam_pr[:], AX.X, ALU.add).then_inc(lam_sum, 1)
            for tok in range(TOKS):
                filled(dve, "diff_q", 0, tok)
                dve.tensor_scalar(dq[:, tok, :], acc[:, 2 * tok:2 * tok + 2].rearrange("p a c -> p (a c)"),
                                  DH ** -0.5, None, ALU.mult).then_inc(acc_free, 1)
                split_units(n0 + 4 + 2 * tok, n0 + 6 + 2 * tok)
            dve.wait_ge(lam_exp, 1)
            link(dve.tensor_tensor(lam[:, 2:3], lam[:, 0:1], lam[:, 1:2], ALU.subtract))
            link(dve.tensor_scalar(lam[:, 3:4], lam[:, 2:3], LAMBDA_INIT, None, ALU.add))
            for part in range(2):
                copy_turned(("qr", "diff", 0, part), dqt[:, 4 * part:4 * part + 4, 0:P])

            def diff_mix(turn):
                tok, g = DIFF_TURNS[turn]
                heads = slice(4 * g, 4 * g + 4)
                dve.wait_ge(turn_full, len(NSA_TURNS) + turn + 1)
                link(dve.reciprocal(share[:, :, 0:4], sums[:, tok, :, heads]))
                link(dve.tensor_scalar(share[:, 1, 0:4], share[:, 1, 0:4], lam[:, 3:4], None, ALU.mult))
                o = dq[:, tok, g * 512:(g + 1) * 512].rearrange("p (h d) -> p h d", d=DIFF_V)
                t = dtmp.rearrange("p (h d) -> p h d", d=DIFF_V)
                for m, dst in ((0, o), (1, t)):
                    ins = dve.tensor_tensor(dst, acc[:, 2 + m].rearrange("p (h d) -> p h d", d=DIFF_V),
                                            bc(share[:, m, 0:4].unsqueeze(2), P, 4, DIFF_V), ALU.mult)
                link(ins)
                link(dve.tensor_tensor(o, o, t, ALU.subtract))
                link(dve.tensor_tensor(t, o, o, ALU.mult))
                link(dve.tensor_reduce(rms[:, 0, :], t, AX.X, ALU.add))
                dve.tensor_scalar(rms[:, 0, :], rms[:, 0, :], 1.0 / DIFF_V, EPS, ALU.mult, ALU.add).then_inc(
                    rms_ready, 1)
                dve.wait_ge(rms_pow, turn + 1)
                link(dve.tensor_tensor(o, o, bc(rms[:, 1, :].unsqueeze(2), P, 4, DIFF_V), ALU.mult))
                dve.scalar_tensor_tensor(o, o, 1.0 - LAMBDA_INIT, bc(sub_g[:].unsqueeze(1), P, 4, DIFF_V),
                                         ALU.mult, ALU.mult).then_inc(turn_mixed, 1)

            for i, sc, tr, pv in job_steps(DIFF_JOBS):
                if sc:
                    maxima(DIFF_JOBS, i, len(NSA_JOBS))
                if tr:
                    copy_turned(("p", "diff", i - 2), dpt[:, i % 2].rearrange("p (k c) -> p k c", k=4))
                if i == 3:
                    for part in range(2):
                        copy_turned(("qr", "diff", 1, part), dqt[:, 4 * part:4 * part + 4, P:SEQ])
                if pv >= 0 and DIFF_JOBS[pv][3]:
                    diff_mix(DIFF_JOBS[pv][0])
                if ends_turn(DIFF_JOBS, pv, 2):
                    x_low("diff_o", 0)
            x_low("diff_o", 1)
            out_stage("diff_out")
            ffn_stage("ffn3", lambda: x_low("diff_out", 1))

        @block.tensor
        def _(pe):
            def three(out_ap, s_hi, s_lo, hi, lo, first, last):
                pe.matmul(out_ap, s_hi, hi, start=first, stop=False)
                pe.matmul(out_ap, s_hi, lo, start=False, stop=False)
                return pe.matmul(out_ap, s_lo, hi, start=False, stop=last)

            def columns_unit(n, j, tok):
                hi, lo = weights(w_hi, n), weights(w_lo, n)
                cols = hi.shape[2]
                for k in range(4):
                    kt = 4 * (j % 2) + k
                    ins = three(acc[:, 2 * tok + j // 2, 0:cols], xt_hi[:, kt, tok * P:(tok + 1) * P],
                                xt_lo[:, kt, tok * P:(tok + 1) * P], hi[:, k, :], lo[:, k, :], kt == 0, kt == KT - 1)
                return ins

            def half_unit(n, j, tok):
                hi, lo = weights(w_hi, n), weights(w_lo, n)
                for kt in range(KT):
                    ins = three(acc[:, 2 * tok + j, 0:HALF], xt_hi[:, kt, tok * P:(tok + 1) * P],
                                xt_lo[:, kt, tok * P:(tok + 1) * P], hi[:, kt, :], lo[:, kt, :], kt == 0,
                                kt == KT - 1)
                return ins

            def rows_unit(s_hi, s_lo, tiles):
                def emit(n, j, tok):
                    hi, lo = weights(w_hi, n), weights(w_lo, n)
                    for k in range(2):
                        kt = 2 * j + k
                        sh, sl = (s[:, kt, tok * P:(tok + 1) * P] for s in (s_hi, s_lo))
                        for c in range(2):
                            cols = slice(c * 512, (c + 1) * 512)
                            ins = three(acc[:, 2 * tok + c], sh, sl, hi[:, k, cols], lo[:, k, cols], kt == 0,
                                        kt == tiles - 1)
                    return ins
                return emit

            def run_units(tok, n0, js, emit, ready=None, between=None):
                for pos, j in enumerate(js):
                    n = n0 + j
                    if between and pos in between:
                        between[pos]()
                    if tok == 0:
                        pe.wait_ge(lo_ready, n + 1 if ready is None else ready + pos)
                    ins = emit(n, j, tok)
                    if tok == 1:
                        ins.then_inc(unit_used, 1)
                return ins

            def turn_blocks(t, bank, blocks, wait):
                if wait is not None:
                    pe.wait_ge(tr_free, wait)
                for j, b in enumerate(blocks):
                    ins = pe.transpose(trb[:, bank, j * P:(j + 1) * P], b, ident)
                ins.then_inc(tr_full, 1)

            def turn(name, blocks):
                t = TURN_OF[name]
                turn_blocks(t, t % 2, blocks, t - 1 if t >= 2 else None)

            def turn_wide(name, src):
                for part in range(2):
                    turn((*name, part), [src[:, (4 * part + j) * P:(4 * part + j + 1) * P] for j in range(4)])

            def turn_x(stage, tok):
                pe.wait_ge(x_ready, 2 * NORM_OF[stage] + tok + 1)
                turn_wide(("x", stage, tok), x[:, tok, :])

            def split_ready(name):
                pe.wait_ge(tr_free, TURN_OF[name] + 1)

            def open_acc(e):
                if e >= 2:
                    pe.wait_ge(acc_free, e - 1)

            def finish(tok, ins):
                if tok == 0:
                    ins.then_inc(tile0_full, 1)

            def group(tok, e, n0, js, emit, between=None, operand=None):
                open_acc(e)
                if operand is not None:
                    split_ready(operand)
                finish(tok, run_units(tok, n0, js, emit, between=between))

            def ffn_stage(stage, turn_rest, operand, next_x):
                n0, e0, t0 = UNIT_OF[stage], FILL_OF[stage, 0, 0], TURN_OF["h", stage, 0, 0]

                def turn_h(g, tok, e, t, k):
                    pe.wait_ge(acc_free, e + 1)
                    turn_blocks(t, (t0 + tok) % 2, [h_nat[:, tok, j * P:(j + 1) * P] for j in range(k)], t - 1)

                group(0, e0, n0, range(4), columns_unit, {3: turn_rest}, (*operand, 0, 1))
                split_ready((*operand, 1, 1))
                with pe.Fori(0, G_FULL - 1) as g:
                    pe.wait_ge(acc_free, 2 * g + e0)
                    ins = run_units(1, n0, range(4), columns_unit,
                                    between={3: lambda: turn_h(g, 0, 2 * g + e0, 2 * g + t0, 4)})
                    finish(1, ins)
                    pe.wait_ge(acc_free, 2 * g + (e0 + 1))
                    ins = run_units(0, n0, range(4), columns_unit, ready=4 * g + (n0 + 5),
                                    between={3: lambda: turn_h(g, 1, 2 * g + (e0 + 1), 2 * g + (t0 + 1), 4)})
                    finish(0, ins)
                g = G_FULL - 1
                group(1, e0 + 2 * g + 1, n0 + 4 * g, range(4), columns_unit,
                      {3: lambda: turn_h(g, 0, e0 + 2 * g, t0 + 2 * g, 4)})
                group(0, e0 + 2 * g + 2, n0 + 4 * g + 4, range(2), half_unit,
                      {1: lambda: turn_h(g, 1, e0 + 2 * g + 1, t0 + 2 * g + 1, 4)})
                g = G_FULL
                group(1, e0 + 2 * g + 1, n0 + 4 * g, range(2), half_unit,
                      {1: lambda: turn_h(g, 0, e0 + 2 * g, t0 + 2 * g, 2)})
                emit = rows_unit(ht_hi, ht_lo, FT)
                e = e0 + 2 * (G_FULL + 1)
                open_acc(e)
                split_ready(("h", stage, G_FULL, 0))
                for i, js in enumerate(DOWN_GROUPS):
                    ins = run_units(0, n0 + UNITS_GU, js, emit, between={
                        len(js) - 1: lambda: turn_h(G_FULL, 1, e0 + 2 * G_FULL + 1, t0 + 2 * G_FULL + 1, 2)}
                        if i == 0 else None)
                    if i == len(DOWN_GROUPS) - 1:
                        finish(0, ins)
                    if i == 0:
                        open_acc(e + 1)
                        split_ready(("h", stage, G_FULL, 1))
                    ins = run_units(1, n0 + UNITS_GU, js, emit, between={
                        3: lambda: turn_x(stage, 0)} if next_x and i == len(DOWN_GROUPS) - 1 else None)
                    if i == len(DOWN_GROUPS) - 1:
                        finish(1, ins)

            def out_stage(stage, o_name):
                n0, e = UNIT_OF[stage], FILL_OF[stage, 0, 0]
                emit = rows_unit(xt_hi, xt_lo, KT)
                turns = len(NSA_TURNS) if stage == "nsa_out" else len(NSA_TURNS) + len(DIFF_TURNS)
                jobs = len(NSA_JOBS) if stage == "nsa_out" else len(NSA_JOBS) + len(DIFF_JOBS)
                src = nq if stage == "nsa_out" else dq

                def turn_o():
                    pe.wait_ge(turn_mixed, turns)
                    turn_wide(("x", o_name, 1), src[:, 1, :])

                pe.wait_ge(exp_done, jobs)
                group(0, e, n0, range(4), emit, {3: turn_o}, ("x", o_name, 0, 1))
                group(1, e + 1, n0, range(4), emit, {3: lambda: turn_x(stage, 0)}, ("x", o_name, 1, 1))

            def scores(jobs, i, base, q_t, key_t):
                _, tok, heads, _ = jobs[i]
                width = P * (tok + 1)
                if i >= 3:
                    pe.wait_ge(exp_done, base + i - 2)
                bank, k = score_bank[i % 3], 0
                for h in heads:
                    for m in range(2):
                        rr = slice((h % 2) * DH, (h % 2 + 1) * DH)
                        pe.matmul(bank[:, k * width:(k + 1) * width], q_t(h, m)[rr, tok * P:(tok + 1) * P],
                                  key_t(h, m)[rr, 0:width], start=True, stop=False)
                        ins = pe.matmul(bank[:, (k + 1) * width - P:(k + 1) * width], id_bf[:], diag_bf[:],
                                        start=False, stop=True)
                        k += 1
                ins.then_inc(score_full, 1)

            def turn_p(kind, i, base, p_sb):
                pe.wait_ge(exp_done, base + i + 1)
                turn(("p", kind, i), [p_sb[:, i % 3, j * P:(j + 1) * P] for j in range(4)])

            def values(kind, jobs, j, base, pt_sb, v_of, width, first, per_turn):
                turn_no, tok, heads, last = jobs[j]
                if j == 0 or jobs[j - 1][3]:
                    first(turn_no)
                pe.wait_ge(tr_free, TURN_OF["p", kind, j] + 1)
                k = 0
                for h in heads:
                    for m in range(2):
                        for kb in range(tok + 1):
                            ins = pe.matmul(acc[:, 2 + m, (h % per_turn) * width:(h % per_turn + 1) * width],
                                            pt_sb[:, j % 2, k * P:(k + 1) * P], v_of(h, m, kb), start=(kb == 0),
                                            stop=(kb == tok))
                            k += 1
                if last:
                    ins.then_inc(turn_full, 1)

            pe.wait_ge(const_in, 16)
            for tok in range(TOKS):
                if tok == 0:
                    pe.wait_ge(x_landed, 32)
                    turn_wide(("x", "start", 0), x[:, 0, :])
            ffn_stage("ffn0", lambda: turn_wide(("x", "start", 1), x[:, 1, :]), ("x", "start"), True)

            n0 = UNIT_OF["nsa_in"]

            def twice(tok_block, what, j):
                c = what * 512 + j * 256
                return [y[:, tok, c + g * P:c + (g + 1) * P] for g in range(NSA_GROUPS) for tok in range(TOKS)]

            def turn_kc(b):
                pe.wait_ge(k_dup, 2)
                turn(("kc", b), twice(None, 0, b))

            def turn_kr(j):
                pe.wait_ge(k_dup, 4)
                turn(("kr", j), twice(None, 1, j))

            def hidden(b):
                pe.wait_ge(tr_free, TURN_OF["kc", b] + 1)
                pe.wait_ge(w1_in, 32)
                w = w1k if b == 0 else w1v[:]
                for pair in range(CMP_BLOCK // 2):
                    ins = pe.matmul(aux[:, b, 0:2 * N_CMP], w[:, pair, :], blk[:, b, pair, :], start=(pair == 0),
                                    stop=(pair == CMP_BLOCK // 2 - 1))
                ins.then_inc(hid_full, 1)

            def second_layer():
                pe.wait_ge(hid_ready, 1)
                pe.matmul(aux[:, 0, 64:64 + 2 * N_CMP], w2k2[:].rearrange("p r d -> p (r d)"), hid[:, 0, :],
                          start=True, stop=True).then_inc(cmp_full, 1)
                pe.wait_ge(cmp_ready, 1)
                for g in range(NSA_GROUPS):
                    ins = pe.matmul(aux[:, 1, 64 + g * DH:64 + (g + 1) * DH],
                                    hid_rep[:, g].rearrange("p h c -> p (h c)"), w2_sb[:, 1, :], start=True, stop=True)
                ins.then_inc(cmp_full, 1)

            def turn_q(tok):
                pe.wait_ge(acc_free, FILL_OF["nsa_in", 1, tok] + 1)
                turn_wide(("q", tok), nq[:, tok, :])

            def turn_qr(kind, tok, count, src):
                pe.wait_ge(rope_done, count)
                turn_wide(("qr", kind, tok), src[:, tok, :])

            def compressed_scores(tok):
                if tok == 0:
                    pe.wait_ge(cmp_ready, 3)
                for pair in range(NSA_HEADS // 2):
                    ins = pe.matmul(aux[:, tok, pair * 32:(pair + 1) * 32], nqt[:, pair, tok * P:(tok + 1) * P],
                                    kcb[:, pair // 4].rearrange("p r c -> p (r c)"), start=True, stop=True)
                ins.then_inc(cs_full, 1)

            e = FILL_OF["nsa_in", 0, 0]
            group(0, e, n0, range(4), columns_unit, {3: lambda: turn_x("ffn0", 1)}, ("x", "ffn0", 0, 1))
            group(1, e + 1, n0, range(4), columns_unit, None, ("x", "ffn0", 1, 1))
            group(0, e + 2, n0 + 4, range(4), columns_unit, {2: lambda: turn_kc(0), 3: lambda: turn_kc(1)})
            group(1, e + 3, n0 + 4, range(4), columns_unit,
                  {0: lambda: hidden(0), 1: lambda: (hidden(1), turn_kr(0)), 2: lambda: turn_kr(1),
                   3: lambda: turn_q(0)})
            second_layer()
            turn_qr("nsa", 0, 1, nq)
            turn_q(1)
            pe.wait_ge(tr_free, TURN_OF["q", 1, 1] + 1)
            for tok in range(TOKS):
                compressed_scores(tok)

            def nsa_first(turn_no):
                tok, g = NSA_TURNS[turn_no]
                if turn_no:
                    pe.wait_ge(turn_mixed, turn_no)
                else:
                    pe.wait_ge(cs_copied, 2)
                    pe.wait_ge(tr_free, TURN_OF[("pc",)] + 1)
                pe.matmul(aux[:, 1], pct[:, 2 * tok + g, :], vcb[:, g].rearrange("p h d -> p (h d)"), start=True,
                          stop=True)

            masks = [masks_ready]
            pe.wait_ge(masks_ready, 1)
            pe.wait_ge(acc_free, e + 4)
            pe.wait_ge(cs_copied, 1)
            for i, sc, tr, pv in job_steps(NSA_JOBS):
                if i == 8:
                    pe.wait_ge(tr_free, TURN_OF["qr", "nsa", 1, 1] + 1)
                if sc:
                    scores(NSA_JOBS, i, 0, lambda h, m: nqrt[:, h // 2], lambda h, m: kt_a[:, m, h // 8])
                if tr:
                    turn_p("nsa", i - 2, 0, np_)
                if i == 2:
                    pe.wait_ge(cexp_done, 2)
                    turn(("pc",), [cs[:, tok, 8 * g:8 * g + 8].rearrange("p h c -> p (h c)")
                                   for tok in range(TOKS) for g in range(NSA_GROUPS)])
                if i == 4:
                    turn_qr("nsa", 1, 2, nq)
                if pv >= 0:
                    values("nsa", NSA_JOBS, pv, 0, npt,
                           lambda h, m, kb: kv_a[:, kb, (VS, VW)[m] + (h // 8) * DH:(VS, VW)[m] + (h // 8 + 1) * DH],
                           DH, nsa_first, 8)
                if ends_turn(NSA_JOBS, pv, 2):
                    pe.wait_ge(turn_mixed, 2)
                    turn_wide(("x", "nsa_o", 0), nq[:, 0, :])
            out_stage("nsa_out", "nsa_o")
            ffn_stage("ffn1", lambda: turn_x("nsa_out", 1), ("x", "nsa_out"), True)

            n0, e = UNIT_OF["kv"], FILL_OF["kv", 0, 0]

            def turn_k(tok):
                pe.wait_ge(rope_done, 3 + tok)
                turn_wide(("k", tok), y[:, tok, :])

            group(0, e, n0, range(4), columns_unit, {3: lambda: turn_x("ffn1", 1)}, ("x", "ffn1", 0, 1))
            group(1, e + 1, n0, range(4), columns_unit, None, ("x", "ffn1", 1, 1))
            group(0, e + 2, n0 + 4, range(4), columns_unit, {3: lambda: turn_k(0)})
            group(1, e + 3, n0 + 4, range(4), columns_unit, {3: lambda: turn_k(1)})
            ffn_stage("ffn2", lambda: None, ("x", "ffn1"), True)

            n0, e = UNIT_OF["diff_q"], FILL_OF["diff_q", 0, 0]
            group(0, e, n0, range(4), columns_unit, {3: lambda: turn_x("ffn2", 1)}, ("x", "ffn2", 0, 1))
            group(1, e + 1, n0, range(4), columns_unit, {3: lambda: turn_qr("diff", 0, 5, dq)}, ("x", "ffn2", 1, 1))
            pe.wait_ge(tr_free, TURN_OF["qr", "diff", 0, 1] + 1)
            pe.wait_ge(acc_free, e + 2)
            base = len(NSA_JOBS)
            pe.wait_ge(exp_done, base)

            def diff_first(turn_no):
                if turn_no:
                    pe.wait_ge(turn_mixed, len(NSA_TURNS) + turn_no)

            for i, sc, tr, pv in job_steps(DIFF_JOBS):
                if i == 4:
                    pe.wait_ge(tr_free, TURN_OF["qr", "diff", 1, 1] + 1)
                if sc:
                    scores(DIFF_JOBS, i, base, lambda h, m: dqt[:, 4 * m + h // 2], lambda h, m: kt_b[:, 4 * m + h // 2])
                if tr:
                    turn_p("diff", i - 2, base, dp)
                if i == 3:
                    turn_qr("diff", 1, 6, dq)
                if pv >= 0:
                    values("diff", DIFF_JOBS, pv, base, dpt,
                           lambda h, m, kb: v_b[:, kb, h * DIFF_V:(h + 1) * DIFF_V], DIFF_V, diff_first, 4)
                if ends_turn(DIFF_JOBS, pv, 2):
                    pe.wait_ge(turn_mixed, len(NSA_TURNS) + 2)
                    turn_wide(("x", "diff_o", 0), dq[:, 0, :])
            out_stage("diff_out", "diff_o")
            ffn_stage("ffn3", lambda: turn_x("diff_out", 1), ("x", "diff_out"), False)


def constants():
    import numpy as np
    c = np.zeros((P, C_COLS), np.float32)
    q = np.arange(P)
    c[:, C_ID:C_ID + P] = np.eye(P)
    c[:, C_DIAG:C_DIAG + P] = np.where(q[None, :] <= q[:, None], 0.0, NEG)
    half = ROT // 2
    inv = np.float32(500000.0) ** (-np.arange(half, dtype=np.float32) * np.float32(2.0) / np.float32(ROT))
    ang = np.arange(SEQ, dtype=np.float32)[:, None] * inv[None, :].astype(np.float32)
    for tok in range(TOKS):
        a = np.tile(ang[tok * P:(tok + 1) * P], (1, 2))
        c[:, C_COS + tok * ROT:C_COS + (tok + 1) * ROT] = np.cos(a)
        c[:, C_SIN + tok * ROT:C_SIN + (tok + 1) * ROT] = np.sin(a)
        end = np.arange(16) * CMP_STRIDE + CMP_BLOCK - 1
        sees = (end[None, :] <= (q + tok * P)[:, None]) & (np.arange(16) < N_CMP)[None, :]
        c[:, C_CMP + tok * 16:C_CMP + (tok + 1) * 16] = np.where(sees, 0.0, NEG)
        c[:, C_ANY + tok] = sees.any(1)
    c[:, C_HEAD:C_HEAD + 8] = (q[:, None] // 16) == np.arange(8)[None, :]
    return c


def kernel(**inputs):
    import numpy as np
    import concourse.bacc as bacc
    from concourse.bass_utils import run_bass_kernel_spmd as run

    nc = bacc.Bacc("TRN2", target_bir_lowering=False, num_devices=1)
    arrays = {}

    def dram(name, a):
        a = np.ascontiguousarray(a)
        arrays[name] = a
        return nc.dram_tensor(name, a.shape, mybir.dt.from_np(a.dtype), kind="ExternalInput").ap()

    a = {k: np.asarray(v) for k, v in inputs.items()}

    def ffn(which):
        return [dram(f"ffn{b}_{which}_{layer}", a[f"ffn{b}_{which}"][layer]) for layer in range(DEPTH) for b in (1, 2)]

    def two(name):
        return [a[f"a_cmp_{name}_k"][0], a[f"a_cmp_{name}_v"][0]]

    args = [
        dram("x_in", a["x"][0]),
        dram("const", constants()),
        ffn("w_gate"), ffn("w_up"), ffn("w_down"),
        dram("norm_gain", a["ln_g"].reshape(3 * DEPTH, D)),
        dram("norm_bias", a["ln_b"].reshape(3 * DEPTH, D)),
        dram("w_in", a["a_w_in"][0]),
        dram("w_out_a", a["a_w_out"][0]),
        dram("cmp_pos", np.stack([p.reshape(CMP_BLOCK // 2, 2 * DH).T for p in two("pos")])),
        dram("cmp_w1", np.stack(two("w1"))),
        dram("cmp_b1", np.stack(two("b1"), axis=1)),
        dram("cmp_w2", np.stack(two("w2"))),
        dram("w_kv", a["b_w_kv_shared"]),
        dram("w_q", a["b_w_q"][0]),
        dram("lambdas", np.stack([a[f"b_lambda_{n}"][0] for n in ("q1", "k1", "q2", "k2")])),
        dram("subln_g", a["b_subln_g"][0]),
        dram("w_out_b", a["b_w_out"][0]),
        nc.dram_tensor("out", (SEQ, D), F32, kind="ExternalOutput").ap(),
    ]
    build_program(nc, *args)
    r = run(nc, [arrays], core_ids=[0])
    return r.results[0]["out"].reshape(1, SEQ, D)
```

```python
from contextlib import ExitStack

import concourse.bass as bass
from concourse import mybir

F32 = mybir.dt.float32
F32R = mybir.dt.float32r
BF16 = mybir.dt.bfloat16
ALU = mybir.AluOpType
ACT = mybir.ActivationFunctionType
AX = mybir.AxisListType

P = 128
SEQ, D, FF, DEPTH = 256, 1024, 2816, 2
TOKS = SEQ // P
KT = D // P
FT = FF // P
NSA_HEADS, NSA_GROUPS, DH = 16, 2, 64
CMP_BLOCK, CMP_STRIDE, HID = 32, 16, 128
N_CMP = (SEQ - CMP_BLOCK) // CMP_STRIDE + 1
SLC_BLOCK, SLC_TOPK, WINDOW = 64, 16, 512
DIFF_HEADS, DIFF_V = 8, 128
ROT = DH // 4
KV_COLS = 6 * NSA_GROUPS * DH + 3 * NSA_HEADS
ALPHA = (2 * DEPTH) ** 0.25
EPS = 1e-5
NEG = -1e30
LAMBDA_INIT = 0.8 - 0.6 * 0.7408182206817179

assert SEQ // SLC_BLOCK <= SLC_TOPK and SEQ <= WINDOW
assert TOKS == 2 and KT == 8

C_COS, C_SIN, C_CMP, C_ANY, C_HEAD, C_COLS = 0, 32, 64, 96, 98, 106
KC, VC, KS, VS, KW, VW, GT = 0, 128, 256, 384, 512, 640, 768

SLOTS = 4
UNIT = 2048
G_FULL = FF // 512
HALF = FF - 512 * G_FULL
UNITS_GU = 4 * G_FULL + 2
UNITS_DOWN = FT // 2
UNITS_FFN = UNITS_GU + UNITS_DOWN
DOWN_GROUPS = [[0, 1, 2], [3, 4, 5, 6], [7, 8, 9, 10]]
assert HALF == 256 and DOWN_GROUPS[-1][-1] == UNITS_DOWN - 1

STAGES = ["ffn0", "nsa_in", "nsa_out", "ffn1", "kv", "ffn2", "diff_q", "diff_out", "ffn3"]
STAGE_UNITS = {"nsa_in": 8, "nsa_out": 4, "kv": 8, "diff_q": 4, "diff_out": 4}
STAGE_UNITS.update({f"ffn{i}": UNITS_FFN for i in range(4)})
NORM_OF = {"ffn0": 0, "nsa_out": 1, "ffn1": 2, "ffn2": 3, "diff_out": 4, "ffn3": 5}


def attention_jobs(heads_per_turn):
    jobs, turns = [], []
    for tok in range(TOKS):
        for share in range(2):
            h0 = share * heads_per_turn
            per_job = 2 - tok
            sets = [list(range(h, h + per_job)) for h in range(h0, h0 + heads_per_turn, per_job)]
            jobs += [(len(turns), tok, heads, heads is sets[-1]) for heads in sets]
            turns.append((tok, share))
    return jobs, turns


NSA_JOBS, NSA_TURNS = attention_jobs(NSA_HEADS // 2)
DIFF_JOBS, DIFF_TURNS = attention_jobs(DIFF_HEADS // 2)

NSA_UNIT_STEPS, DIFF_UNIT_STEPS = (8, 12, 14, 21), (2, 7, 8, 12)
LATE_PARTS = {2: (0, 1), 3: (2, 3)}


def job_steps(jobs):
    for i in range(len(jobs) + 3):
        yield i, i < len(jobs), 0 <= i - 2 < len(jobs), i - 3


def ends_turn(jobs, j, turn):
    return j >= 0 and jobs[j][3] and jobs[j][0] == turn


def jobs_through(jobs, turn):
    return sum(job[0] <= turn for job in jobs)


def count_events():
    unit, fill, turn = {}, {}, []
    n = 0
    for stage in STAGES:
        unit[stage] = n
        n += STAGE_UNITS[stage]
    e = 1
    for stage in STAGES:
        groups = G_FULL + 2 if stage.startswith("ffn") else 2 if stage in ("nsa_in", "kv") else 1
        for g in range(groups):
            for tok in range(TOKS):
                fill[stage, g, tok] = e
                e += 1

    def pair(*name):
        turn.extend([(*name, 0), (*name, 1)])

    def four(*name):
        turn.extend([(*name, part) for part in range(4)])

    pair("x", "start", 0)
    pair("x", "start", 1)
    for stage in STAGES:
        if stage.startswith("ffn"):
            for g in range(G_FULL + 1):
                turn.extend([("h", stage, g, 0), ("h", stage, g, 1)])
        if stage == "nsa_in":
            turn.extend([("kc", 0), ("kc", 1)])
            pair("q", 0)
            turn.extend([("kr", 0), ("kr", 1), ("ks", 0), ("ks", 1)])
            four("qr", "nsa", 0)
            for i, _, tr, pv in job_steps(NSA_JOBS):
                if i == 0:
                    pair("q", 1)
                if tr:
                    turn.append(("p", "nsa", i - 2))
                if i == 3:
                    turn.append(("pc",))
                if 3 <= i < 7:
                    turn.append(("qr", "nsa", 1, i - 3))
                if ends_turn(NSA_JOBS, pv, 2):
                    pair("x", "nsa_o", 0)
            pair("x", "nsa_o", 1)
        if stage == "diff_q":
            for name in ("kr", "ks"):
                for tok in range(TOKS):
                    four(name, "diff", tok)
            four("qr", "diff", 0)
            for i, _, tr, pv in job_steps(DIFF_JOBS):
                if tr:
                    turn.append(("p", "diff", i - 2))
                for part in LATE_PARTS.get(i, ()):
                    turn.append(("qr", "diff", 1, part))
                if ends_turn(DIFF_JOBS, pv, 2):
                    pair("x", "diff_o", 0)
            pair("x", "diff_o", 1)
        if stage in NORM_OF and stage != "ffn3":
            for tok in range(TOKS):
                pair("x", stage, tok)
    return unit, fill, {name: i for i, name in enumerate(turn)}, {
        name: i for i, name in enumerate([t for t in turn if t[0] in "xh"])}


UNIT_OF, FILL_OF, TURN_OF, SPLIT_OF = count_events()


def units_through(stage, g):
    if stage.startswith("ffn"):
        in_stage = min(4 * (g + 1), UNITS_GU) if g <= G_FULL else UNITS_FFN
    else:
        in_stage = 4 * (g + 1)
    return UNIT_OF[stage] + in_stage


TILE0_FILLS = {(s, g): e // TOKS + 1 for (s, g, tok), e in FILL_OF.items() if tok == 0}
N_UNITS = UNIT_OF["ffn3"] + UNITS_FFN


def unit_shape(n):
    stage = [s for s in STAGES if UNIT_OF[s] <= n][-1]
    j = n - UNIT_OF[stage]
    if stage.startswith("ffn"):
        return (4, 512) if j < 4 * G_FULL else (8, HALF) if j < UNITS_GU else (2, D)
    if stage in ("nsa_out", "diff_out"):
        return 2, D
    if stage == "nsa_in" and j in (2, 3):
        return 4, KV_COLS - 512
    return 4, 512


def build_program(nc, x_in, const, squares_in, w_gates, w_ups, w_downs, ln_g, ln_b, w_in, w_out_a, cmp_pos, cmp_w1, cmp_b1,
                  cmp_w2, w_kv, w_q, lambdas, subln_g, w_out_b, out):
    with ExitStack() as ctx:
        def sb(name, shape, dt=F32, scope=ctx):
            return scope.enter_context(nc.sbuf_tensor(name, shape, dt))

        def sem(name):
            return ctx.enter_context(nc.semaphore(name))

        raw = sb("raw", [P, SLOTS, UNIT])
        w_hi = sb("w_hi", [P, SLOTS, UNIT], F32R)
        w_lo = sb("w_lo", [P, SLOTS, UNIT], F32R)
        x = sb("x", [P, TOKS, D])
        y = sb("y", [P, TOKS, D])
        xt_hi = sb("xt_hi", [P, KT, SEQ], F32R)
        xt_lo = sb("xt_lo", [P, KT, SEQ], F32R)
        norm_gb = sb("norm_gb", [P, 2, D])
        probs = norm_gb[:].rearrange("p a c -> p (a c)")[:, 0:1536].rearrange("p (j c) -> p j c", j=3)
        w1k = norm_gb[:].rearrange("p a (b h) -> p (a b) h", h=HID)
        cst = sb("cst", [P, C_COLS])
        id_r = sb("id_r", [P, P + DH], F32R)
        id_bf = sb("id_bf", [P, P], BF16)
        diag_bf = sb("diag_bf", [P, P], BF16)
        pos_sb = sb("pos_sb", [P, 2, CMP_BLOCK // 2])
        b1_sb = sb("b1_sb", [P, 2])
        w2_sb = sb("w2_sb", [P, 2, DH])
        w2k2 = sb("w2k2", [P, 2, DH])
        lam_in = sb("lam_in", [P, 4, DH])
        lam = sb("lam", [P, 4])
        sub_g = sb("sub_g", [P, DIFF_V])
        half_pow = sb("half_pow", [P, 4])
        stats = sb("stats", [P, TOKS, 2, 6])
        mean_var = sb("mean_var", [P, TOKS, 2])
        rstd = sb("rstd", [P, TOKS, 2])
        rope_a = sb("rope_a", [P, 16, ROT])
        rope_b = sb("rope_b", [P, 16, ROT])
        neg_max = sb("neg_max", [P, 3, 4])
        sums = sb("sums", [P, TOKS, 2, NSA_HEADS])
        share = sb("share", [P, 2, NSA_HEADS])
        rms = sb("rms", [P, 2, 4])

        late = ExitStack()
        with late:
            k_nat = sb("k_nat", [P, TOKS, D], scope=late)
            v_b = sb("v_b", [P, TOKS, D], scope=late)
            ffn = ExitStack()
            with ffn:
                ht_hi = sb("ht_hi", [P, FT, SEQ], F32R, ffn)
                ht_lo = sb("ht_lo", [P, FT, SEQ], F32R, ffn)
            dif = ExitStack()
            with dif:
                dqs = sb("dqs", [P, 2 * DIFF_HEADS, SEQ], F32R, dif)
                dks = sb("dks", [P, 2, 2 * DIFF_HEADS, SEQ], F32R, dif)
        nsa = ExitStack()
        with nsa:
            kv_a = sb("kv_a", [P, TOKS, KV_COLS], scope=nsa)
            nq = sb("nq", [P, TOKS, D], scope=nsa)
            nqs = sb("nqs", [P, NSA_HEADS, SEQ], F32R, nsa)
            nks = sb("nks", [P, 2, 2, NSA_GROUPS, SEQ], F32R, nsa)
            blk = sb("blk", [P, 2, CMP_BLOCK // 2, NSA_GROUPS * N_CMP], scope=nsa)
            w1v = sb("w1v", [P, CMP_BLOCK // 2, HID], scope=nsa)
            hid = sb("hid", [P, 2, NSA_GROUPS * N_CMP], scope=nsa)
            hid_rep = sb("hid_rep", [P, NSA_GROUPS, 8, 16], scope=nsa)
            kcb = sb("kcb", [P, NSA_GROUPS, 2, 16], scope=nsa)
            vcb = sb("vcb", [P, NSA_GROUPS, 8, DH], scope=nsa)
            cs = sb("cs", [P, TOKS, NSA_HEADS, 16], scope=nsa)
            cmax = sb("cmax", [P, TOKS, NSA_HEADS], scope=nsa)
            csum = sb("csum", [P, TOKS, NSA_HEADS], scope=nsa)
            pct = sb("pct", [P, 4, P], scope=nsa)
            gate = sb("gate", [P, TOKS, 3 * NSA_HEADS], scope=nsa)
        lam_pr = y[:, 0, 0:2 * DH].rearrange("p (a d) -> p a d", d=DH)
        squares = y[:, 1, 0:2 * P]
        sil = y[:, :, 0:512]
        h_nat = y[:, :, 512:1024]
        dq = k_nat
        nqt = y[:].rearrange("p t (k s) -> p (t k) s", s=SEQ)
        def flat(t):
            return t[:].rearrange("p a b -> p (a b)")

        beside = [v[:, a:a + 2 * DH * h].rearrange("p (h s d) -> p h s d", s=2, d=DH) for v, a, h in (
            (flat(nqs), 0, 4), (flat(nqs), 2048, 4), (flat(w1v).bitcast(F32R), 0, 16), (flat(xt_lo), 0, 16),
            (flat(dqs), 0, 16), (flat(dqs), 2048, 16), (flat(y).bitcast(F32R), 0, 16), (flat(xt_lo), 0, 16))]
        rotated = [kv_a[:, tok, KS:KS + 512].rearrange("p (m g d) -> p m g d", m=2, d=DH)[:, :, 0:2, :]
                   for tok in range(TOKS)] + [v[:, tok, :].rearrange("p (h d) -> p h d", d=DH)
                                              for v in (nq, k_nat, dq) for tok in range(TOKS)]
        npt = dpt = y[:, 0, :].rearrange("p (a c) -> p a c", a=2)
        branch = [y[:, 1, 0:512], y[:, 1, 512:1024]]

        acc = ctx.enter_context(nc.psum_tensor("acc", [P, 4, 512], F32))
        trb = ctx.enter_context(nc.psum_tensor("trb", [P, 2, 512], F32))
        aux = ctx.enter_context(nc.psum_tensor("aux", [P, 2, 512], F32))
        score_bank = [acc[:, 0], acc[:, 1], aux[:, 0]]

        const_in = sem("const_in")
        x_landed = sem("x_landed")
        small_in = sem("small_in")
        norm_in = sem("norm_in")
        w1_in = sem("w1_in")
        raw_in = [sem(f"raw_in{i}") for i in range(SLOTS)]
        hi_ready = sem("hi_ready")
        lo_ready = sem("lo_ready")
        unit_used = sem("unit_used")
        tile0_full = sem("tile0_full")
        acc_free = sem("acc_free")
        silu_done = sem("silu_done")
        tr_full = sem("tr_full")
        tr_hi = sem("tr_hi")
        tr_free = [sem(f"tr_free{bank}") for bank in range(2)]
        beside_hi = sem("beside_hi")
        beside_ready = sem("beside_ready")
        k_dup = sem("k_dup")
        x_ready = sem("x_ready")
        stats_ready = sem("stats_ready")
        rstd_ready = sem("rstd_ready")
        masks_ready = sem("masks_ready")
        rope_done = sem("rope_done")
        hid_full = sem("hid_full")
        hid_ready = sem("hid_ready")
        cmp_full = sem("cmp_full")
        cmp_ready = sem("cmp_ready")
        cs_full = sem("cs_full")
        cs_shifted = sem("cs_shifted")
        cs_copied = sem("cs_copied")
        cexp_done = sem("cexp_done")
        gate_exp = sem("gate_exp")
        score_full = sem("score_full")
        max_ready = sem("max_ready")
        exp_done = sem("exp_done")
        turn_full = sem("turn_full")
        turn_read = sem("turn_read")
        turn_mixed = sem("turn_mixed")
        lam_sum = sem("lam_sum")
        lam_exp = sem("lam_exp")
        dve_step = sem("dve_step")
        pool_step = sem("pool_step")
        rms_ready = sem("rms_ready")
        rms_pow = sem("rms_pow")
        out_done = sem("out_done")

        ident = id_r[:, 0:P].bitcast(F32)
        swap = id_r[:, DH:DH + P]
        cos2 = cst[:, C_COS:C_COS + 32].rearrange("p (t r) -> p t r", t=TOKS)
        sin2 = cst[:, C_SIN:C_SIN + 32].rearrange("p (t r) -> p t r", t=TOKS)
        cmp_mask = cst[:, C_CMP:C_CMP + 32].rearrange("p (t c) -> p t c", t=TOKS)

        def weights(buf, n):
            k, c = unit_shape(n)
            return buf[:, n % SLOTS, 0:k * c].rearrange("p (k c) -> p k c", k=k)

        def rows(w, r0, k, c0, c):
            return w[r0:r0 + k * P, c0:c0 + c].rearrange("(k p) c -> p k c", p=P)

        def bc(ap, *shape):
            return ap.broadcast_to(list(shape))

        def filled(eng, stage, g, tok):
            if tok == 0:
                eng.wait_ge(tile0_full, TILE0_FILLS[stage, g])
            else:
                eng.wait_ge(unit_used, units_through(stage, g))

        block = ctx.enter_context(nc.Block())

        @block.sync
        def _(sp):
            sp.dma_start(squares, squares_in).then_inc(const_in, 16)
            sp.dma_start(cst[:], const).then_inc(const_in, 16)
            for tok in range(TOKS):
                sp.dma_start(x[:, tok, :], x_in[tok * P:(tok + 1) * P, :]).then_inc(x_landed, 16)

            def load(n, src, freed=None):
                if freed is not None:
                    sp.wait_ge(lo_ready, freed)
                elif n >= SLOTS:
                    sp.wait_ge(lo_ready, n - SLOTS + 1)
                sp.dma_start(weights(raw, n), src).then_inc(raw_in[n % SLOTS], 16)

            def load_ffn(stage):
                i = int(stage[3])
                n0 = UNIT_OF[stage]
                wg, wu, wd = w_gates[i], w_ups[i], w_downs[i]

                def group(g, peeled):
                    for j, (w, half) in enumerate([(wg, 0), (wg, 1), (wu, 0), (wu, 1)]):
                        src = w[half * 512:(half + 1) * 512, bass.ds(g * 512, 512)].rearrange(
                            "(k p) c -> p k c", p=P)
                        load(n0 + j, src, None if peeled else g * 4 + (n0 + j - SLOTS + 1))

                group(0, True)
                with sp.Fori(1, G_FULL) as g:
                    group(g, False)
                load(n0 + 4 * G_FULL, rows(wg, 0, KT, 512 * G_FULL, HALF))
                load(n0 + 4 * G_FULL + 1, rows(wu, 0, KT, 512 * G_FULL, HALF))
                for j in range(UNITS_DOWN):
                    load(n0 + UNITS_GU + j, rows(wd, 2 * P * j, 2, 0, D))

            def load_columns(stage, w, chunks):
                n = UNIT_OF[stage]
                for c0, c in chunks:
                    for half in range(2):
                        load(n, rows(w, half * 512, 4, c0, c))
                        n += 1

            def load_rows(stage, w):
                for j in range(KT // 2):
                    load(UNIT_OF[stage] + j, rows(w, 2 * P * j, 2, 0, D))

            load_ffn("ffn0")
            load_columns("nsa_in", w_in, [(D, 512), (D + 512, KV_COLS - 512), (0, 512), (512, 512)])
            load_rows("nsa_out", w_out_a)
            load_ffn("ffn1")
            load_columns("kv", w_kv, [(c, 512) for c in range(0, 2 * D, 512)])
            load_ffn("ffn2")
            load_columns("diff_q", w_q, [(0, 512), (512, 512)])
            load_rows("diff_out", w_out_b)
            load_ffn("ffn3")
            for tok in range(TOKS):
                sp.wait_ge(x_ready, 2 * len(NORM_OF) - 1 + tok)
                sp.dma_start(out[tok * P:(tok + 1) * P, :], x[:, tok, :]).then_inc(out_done, 16)
            sp.wait_ge(out_done, 16 * TOKS)

        @block.gpsimd
        def _(pool):
            step = [0]

            def link(ins):
                step[0] += 1
                ins.then_inc(pool_step, 1)
                pool.wait_ge(pool_step, step[0])

            small = 0
            for dst, src in ((pos_sb[:], cmp_pos.rearrange("b p l -> p b l")), (b1_sb[:], cmp_b1),
                             (w2_sb[:], cmp_w2.rearrange("b h d -> h b d")),
                             (lam_in[:], lambdas.partition_broadcast(P)), (sub_g[:], subln_g.partition_broadcast(P))):
                pool.dma_start(dst, src).then_inc(small_in, 16)

            def load_norm(k):
                if k:
                    pool.wait_ge(x_ready, 2 * k)
                if k in (1, 4):
                    kind, jobs = ("nsa", NSA_JOBS) if k == 1 else ("diff", DIFF_JOBS)
                    pool.wait_ge(tr_full, TURN_OF["p", kind, len(jobs) - 1] + 1)
                for j, w in enumerate((ln_g, ln_b)):
                    pool.dma_start(norm_gb[:, j, :], w[k].partition_broadcast(P)).then_inc(norm_in, 16)

            def inverse_root(k):
                for tok in range(TOKS):
                    pool.wait_ge(stats_ready, 2 * k + tok + 1)
                    link(pool.tensor_scalar(rstd[:, tok, 0:1], mean_var[:, tok, 1:2], EPS, None, ALU.add))
                    pool.tensor_tensor(rstd[:, tok, 1:2], rstd[:, tok, 0:1], half_pow[:, 0:1],
                                       ALU.pow).then_inc(rstd_ready, 1)

            def rotate(v, tok, heads):
                a, b = rope_a[:, 0:heads], rope_b[:, 0:heads]
                r, h = v[:, :, 0:ROT], ROT // 2
                link(pool.tensor_tensor(a, r, bc(cos2[:, tok:tok + 1, :], P, heads, ROT), ALU.mult))
                link(pool.tensor_tensor(b, r, bc(sin2[:, tok:tok + 1, :], P, heads, ROT), ALU.mult))
                link(pool.tensor_tensor(v[:, :, 0:h], a[:, :, 0:h], b[:, :, h:ROT], ALU.subtract))
                return pool.tensor_tensor(v[:, :, h:ROT], b[:, :, 0:h], a[:, :, h:ROT], ALU.add)

            def heads_of(v, tok, c0, heads):
                return v[:, tok, c0:c0 + heads * DH].rearrange("p (h d) -> p h d", d=DH)

            link(pool.memset(half_pow[:], -0.5))
            load_norm(0)
            pool.wait_ge(const_in, 32)
            inverse_root(0)
            pool.wait_ge(x_ready, 2)
            pool.dma_start(w1k, cmp_w1[0].rearrange("(l p) h -> p l h", p=P)).then_inc(w1_in, 16)
            pool.dma_start(w1v[:], cmp_w1[1].rearrange("(l p) h -> p l h", p=P)).then_inc(w1_in, 16)
            for tok in range(TOKS):
                pool.wait_ge(acc_free, FILL_OF["nsa_in", 0, tok] + 1)
                for j, c in enumerate((KC, VC)):
                    dst = y[:, tok, j * 256:(j + 1) * 256].rearrange("p (g r d) -> p g r d", g=2, r=2)
                    for r in range(2):
                        ins = pool.tensor_copy(dst[:, :, r, :], heads_of(kv_a, tok, c, 2))
                ins.then_inc(k_dup, 1)
                link(rotate(heads_of(kv_a, tok, KS, 2), tok, 2))
                ins = rotate(heads_of(kv_a, tok, KW, 2), tok, 2)
                ins.then_inc(rope_done, 1)
                pool.wait_ge(rope_done, tok + 1)
            for tok in range(TOKS):
                pool.wait_ge(acc_free, FILL_OF["nsa_in", 1, tok] + 1)
                pool.wait_ge(tr_full, TURN_OF["q", tok, 1] + 1)
                if tok:
                    pool.wait_ge(rope_done, 3)
                rotate(heads_of(nq, tok, 0, 16), tok, 16).then_inc(rope_done, 1)
            load_norm(1)
            inverse_root(1)
            load_norm(2)
            inverse_root(2)
            for tok in range(TOKS):
                pool.wait_ge(acc_free, FILL_OF["kv", 0, tok] + 1)
                if tok:
                    pool.wait_ge(rope_done, 5)
                rotate(heads_of(k_nat, tok, 0, 16), tok, 16).then_inc(rope_done, 1)
            load_norm(3)
            inverse_root(3)
            for tok in range(TOKS):
                pool.wait_ge(acc_free, FILL_OF["diff_q", 0, tok] + 1)
                if tok:
                    pool.wait_ge(rope_done, 7)
                rotate(heads_of(dq, tok, 0, 16), tok, 16).then_inc(rope_done, 1)
            for k in range(len(DIFF_TURNS)):
                pool.wait_ge(rms_ready, k + 1)
                pool.tensor_tensor(rms[:, 1, :], rms[:, 0, :], half_pow[:], ALU.pow).then_inc(rms_pow, 1)
                if k == len(DIFF_TURNS) - 2:
                    load_norm(4)
            inverse_root(4)
            load_norm(5)
            inverse_root(5)

        @block.scalar
        def _(act):
            def split_unit(n, slot, in_count, used):
                act.wait_ge(raw_in[slot], in_count)
                if used is not None:
                    act.wait_ge(unit_used, used)
                k, c = unit_shape(n)
                act.activation(w_hi[:, slot, 0:k * c], raw[:, slot, 0:k * c], ACT.Copy).then_inc(hi_ready, 1)

            def split_units(n0, n1):
                for n in range(n0, min(n1, N_UNITS)):
                    split_unit(n, n % SLOTS, 16 * (n // SLOTS + 1), n - SLOTS + 1 if n >= SLOTS else None)

            def high_part(name, dst):
                act.wait_ge(tr_full, TURN_OF[name] + 1)
                act.activation(dst, trb[:, TURN_OF[name] % 2].rearrange("p (k c) -> p k c", c=P), ACT.Copy).then_inc(
                    tr_hi, 1)

            def copy_turned(name, dst):
                t = TURN_OF[name]
                act.wait_ge(tr_full, t + 1)
                act.activation(dst, trb[:, t % 2].rearrange("p (k c) -> p k c", c=P), ACT.Copy).then_inc(
                    tr_free[t % 2], 1)

            def copy_heads(name, tok, part, dst):
                copy_turned((*name, tok, part), dst[:, 4 * part:4 * part + 4, tok * P:(tok + 1) * P])

            def split_beside(k):
                act.wait_ge(rope_done, k + 1)
                dst, src = beside[k][:, :, 0, :], rotated[k]
                if len(src.shape) == 4:
                    for m in range(2):
                        ins = act.activation(dst[:, 2 * m:2 * m + 2], src[:, m], ACT.Copy)
                else:
                    ins = act.activation(dst, src, ACT.Copy)
                ins.then_inc(beside_hi, 1)

            def x_high(of, tok):
                for part in range(2):
                    high_part(("x", of, tok, part), xt_hi[:, 4 * part:4 * part + 4, tok * P:(tok + 1) * P])

            def ffn_stage(stage, pending):
                n0, e0, t0 = UNIT_OF[stage], FILL_OF[stage, 0, 0], TURN_OF["h", stage, 0, 0]
                pending()

                def silu(tok, c):
                    act.activation(sil[:, tok, 0:c], acc[:, 2 * tok, 0:c], ACT.Silu).then_inc(silu_done, 1)

                def h_high(t, bank, g, tok, k):
                    act.wait_ge(tr_full, t + 1)
                    act.activation(ht_hi[:, bass.ds(4 * g, k), tok * P:(tok + 1) * P],
                                   trb[:, bank, 0:k * P].rearrange("p (k c) -> p k c", c=P),
                                   ACT.Copy).then_inc(tr_hi, 1)

                with act.Fori(0, G_FULL - 1) as g:
                    act.wait_ge(tile0_full, g + TILE0_FILLS[stage, 0])
                    silu(0, 512)
                    for j in range(4):
                        n = n0 + 4 + j
                        if j == 3:
                            act.wait_ge(unit_used, 4 * g + (n0 + 4))
                            silu(1, 512)
                        split_unit(n, n % SLOTS, g * 16 + 16 * (n // SLOTS + 1), g * 4 + (n - SLOTS + 1))
                    h_high(2 * g + t0, t0 % 2, g, 0, 4)
                    h_high(2 * g + (t0 + 1), (t0 + 1) % 2, g, 1, 4)
                for g in (G_FULL - 1, G_FULL):
                    c = 512 if g < G_FULL else HALF
                    filled(act, stage, g, 0)
                    silu(0, c)
                    n = n0 + 4 * (g + 1)
                    split_units(n, n + c // 128 - 1)
                    if g == G_FULL:
                        h_high(t0 + 2 * g, t0 % 2, g, 0, c // P)
                    filled(act, stage, g, 1)
                    silu(1, c)
                    split_units(n + c // 128 - 1, n + c // 128)
                    for tok in range(TOKS):
                        if tok or g < G_FULL:
                            h_high(t0 + 2 * g + tok, (t0 + tok) % 2, g, tok, c // P)
                split_units(n0 + UNITS_GU + 4, n0 + UNITS_FFN + 2)
                if stage != "ffn3":
                    x_high(stage, 0)
                split_units(n0 + UNITS_FFN + 2, n0 + UNITS_FFN + 4)

            def exps(kind, jobs, i, base):
                turn, tok, heads, _ = jobs[i]
                width = P * (tok + 1)
                act.wait_ge(max_ready, base + i + 1)
                if i >= 3:
                    act.wait_ge(tr_full, TURN_OF["p", kind, i - 3] + 1)
                k = 0
                for h in heads:
                    for m in range(2):
                        ins = act.activation(probs[:, i % 3, k * width:(k + 1) * width],
                                             score_bank[i % 3][:, k * width:(k + 1) * width], ACT.Exp,
                                             bias=neg_max[:, i % 3, k:k + 1],
                                             accum_out=sums[:, tok, m, h:h + 1])
                        k += 1
                ins.then_inc(exp_done, 1)

            def copy_p(kind, j, dst):
                copy_turned(("p", kind, j), dst[:, j % 2].rearrange("p (k c) -> p k c", c=P))

            x_high("start", 0)
            split_units(0, 4)
            ffn_stage("ffn0", lambda: x_high("start", 1))

            n0 = UNIT_OF["nsa_in"]
            x_high("ffn0", 1)
            split_units(n0 + 4, n0 + 8)
            for k in range(2):
                split_beside(k)
            act.wait_ge(small_in, 80)
            for b in range(2):
                act.wait_ge(hid_full, b + 1)
                act.activation(hid[:, b, :], aux[:, b, 0:2 * N_CMP], ACT.Gelu_apprx_tanh,
                               bias=b1_sb[:, b:b + 1]).then_inc(hid_ready, 1)
            for j in range(2):
                copy_turned(("kr", j), nks[:, 0, j].rearrange("p g (t c) -> p (g t) c", c=P))
            split_beside(2)
            for j in range(2):
                copy_turned(("ks", j), nks[:, 1, j].rearrange("p g (t c) -> p (g t) c", c=P))
            act.wait_ge(acc_free, FILL_OF["nsa_in", 0, 1] + 1)
            for tok in range(TOKS):
                ins = act.activation(gate[:, tok, :], kv_a[:, tok, GT:GT + 48], ACT.Exp, scale=-1.0)
            ins.then_inc(gate_exp, 1)
            for part in range(4):
                copy_heads(("qr", "nsa"), 0, part, nqs)

            def compressed_exp(tok):
                act.wait_ge(cs_shifted, tok + 1)
                act.activation(cs[:, tok], cs[:, tok], ACT.Exp).then_inc(cexp_done, 1)

            compressed_exp(0)
            for i, sc, tr, pv in job_steps(NSA_JOBS):
                if tr:
                    copy_p("nsa", i - 2, npt)
                if i == 3:
                    copy_turned(("pc",), pct[:])
                if 3 <= i < 7:
                    copy_heads(("qr", "nsa"), 1, i - 3, nqs)
                if sc:
                    exps("nsa", NSA_JOBS, i, 0)
                if i == 1:
                    compressed_exp(1)
                    split_beside(3)
                if i in NSA_UNIT_STEPS:
                    k = NSA_UNIT_STEPS.index(i)
                    split_units(n0 + 8 + k, n0 + 9 + k)
                if ends_turn(NSA_JOBS, pv, 2):
                    x_high("nsa_o", 0)
            x_high("nsa_o", 1)
            n0 = UNIT_OF["nsa_out"]
            split_units(n0 + 4, n0 + 6)
            x_high("nsa_out", 0)
            split_units(n0 + 6, n0 + 8)
            ffn_stage("ffn1", lambda: x_high("nsa_out", 1))

            n0 = UNIT_OF["kv"]
            x_high("ffn1", 1)
            split_units(n0 + 4, n0 + 12)
            ffn_stage("ffn2", lambda: None)

            n0 = UNIT_OF["diff_q"]
            x_high("ffn2", 1)
            for k in range(4, 6):
                split_beside(k)
            act.wait_ge(lam_sum, 1)
            act.activation(lam[:, 0:2], lam[:, 0:2], ACT.Exp).then_inc(lam_exp, 1)
            for part in (0, 2):
                copy_heads(("kr", "diff"), 0, part, dks[:, 0])
            split_beside(6)
            for part in (0, 2):
                copy_heads(("kr", "diff"), 1, part, dks[:, 0])
            for tok in range(TOKS):
                for part in (0, 2):
                    copy_heads(("ks", "diff"), tok, part, dks[:, 1])
            for part in (0, 2):
                copy_heads(("qr", "diff"), 0, part, dqs)
            split_beside(7)
            for i, sc, tr, pv in job_steps(DIFF_JOBS):
                if tr:
                    copy_p("diff", i - 2, dpt)
                for part in LATE_PARTS.get(i, ()):
                    copy_heads(("qr", "diff"), 1, part, dqs)
                if sc:
                    exps("diff", DIFF_JOBS, i, len(NSA_JOBS))
                if i in DIFF_UNIT_STEPS:
                    k = DIFF_UNIT_STEPS.index(i)
                    split_units(n0 + 4 + k, n0 + 5 + k)
                if ends_turn(DIFF_JOBS, pv, 2):
                    x_high("diff_o", 0)
            x_high("diff_o", 1)
            n0 = UNIT_OF["diff_out"]
            split_units(n0 + 4, n0 + 6)
            x_high("diff_out", 0)
            split_units(n0 + 6, n0 + 8)
            ffn_stage("ffn3", lambda: x_high("diff_out", 1))

        @block.vector
        def _(dve):
            step = [0]

            def link(ins):
                step[0] += 1
                ins.then_inc(dve_step, 1)
                dve.wait_ge(dve_step, step[0])

            def split_unit(n, slot, ready):
                dve.wait_ge(hi_ready, ready)
                k, c = unit_shape(n)
                dve.tensor_tensor(w_lo[:, slot, 0:k * c], raw[:, slot, 0:k * c],
                                  w_hi[:, slot, 0:k * c].bitcast(F32), ALU.subtract).then_inc(lo_ready, 1)

            def split_units(n0, n1):
                for n in range(n0, min(n1, N_UNITS)):
                    split_unit(n, n % SLOTS, n + 1)

            def low_part(name, hi, lo):
                t = TURN_OF[name]
                dve.wait_ge(tr_hi, SPLIT_OF[name] + 1)
                dve.tensor_tensor(lo, trb[:, t % 2].rearrange("p (k c) -> p k c", c=P), hi.bitcast(F32),
                                  ALU.subtract).then_inc(tr_free[t % 2], 1)

            def x_low(of, tok):
                for part in range(2):
                    at = slice(4 * part, 4 * part + 4), slice(tok * P, (tok + 1) * P)
                    low_part(("x", of, tok, part), xt_hi[:, at[0], at[1]], xt_lo[:, at[0], at[1]])

            def split_beside(k):
                dve.wait_ge(beside_hi, k + 1)
                hi, lo, src = beside[k][:, :, 0, :], beside[k][:, :, 1, :], rotated[k]
                if len(src.shape) == 4:
                    for m in range(2):
                        ins = dve.tensor_tensor(lo[:, 2 * m:2 * m + 2], src[:, m],
                                                hi[:, 2 * m:2 * m + 2].bitcast(F32), ALU.subtract)
                else:
                    ins = dve.tensor_tensor(lo, src, hi.bitcast(F32), ALU.subtract)
                ins.then_inc(beside_ready, 1)

            def copy_turned(name, dst, k=4):
                t = TURN_OF[name]
                dve.wait_ge(tr_full, t + 1)
                dve.tensor_copy(dst, trb[:, t % 2].rearrange("p (k c) -> p k c", k=k)).then_inc(tr_free[t % 2], 1)

            def norm(stage, tok):
                k = NORM_OF[stage]
                group = G_FULL + 1 if stage.startswith("ffn") else 0
                e = FILL_OF[stage, group, tok]
                filled(dve, stage, group, tok)
                dve.scalar_tensor_tensor(y[:, tok, :], x[:, tok, :], ALPHA,
                                         acc[:, 2 * tok:2 * tok + 2].rearrange("p a c -> p (a c)"),
                                         ALU.mult, ALU.add).then_inc(acc_free, 1)
                dve.wait_ge(acc_free, e + 1)
                for half in range(2):
                    ins = dve.bn_stats(stats[:, tok, half, :], y[:, tok, half * 512:(half + 1) * 512])
                link(ins)
                dve.bn_aggr(mean_var[:, tok, :], stats[:, tok].rearrange("p a b -> p (a b)")).then_inc(stats_ready, 1)
                dve.wait_ge(stats_ready, 2 * k + tok + 1)
                dve.wait_ge(norm_in, 32 * (k + 1))
                link(dve.scalar_tensor_tensor(y[:, tok, :], y[:, tok, :], mean_var[:, tok, 0:1], norm_gb[:, 0, :],
                                              ALU.subtract, ALU.mult))
                dve.wait_ge(rstd_ready, 2 * k + tok + 1)
                dve.scalar_tensor_tensor(x[:, tok, :], y[:, tok, :], rstd[:, tok, 1:2], norm_gb[:, 1, :],
                                         ALU.mult, ALU.add).then_inc(x_ready, 1)

            def ffn_stage(stage, pending):
                n0, e0, s0 = UNIT_OF[stage], FILL_OF[stage, 0, 0], SPLIT_OF["h", stage, 0, 0]
                t0 = TURN_OF["h", stage, 0, 0]
                i0 = 2 * (G_FULL + 1) * int(stage[3])
                pending()

                def gated(i, tok, c):
                    dve.wait_ge(silu_done, i + 1)
                    dve.scalar_tensor_tensor(h_nat[:, tok, 0:c], sil[:, tok, 0:c], 0.5, acc[:, 2 * tok + 1, 0:c],
                                             ALU.mult, ALU.mult).then_inc(acc_free, 1)

                def h_low(s, bank, g, tok, k):
                    dve.wait_ge(tr_hi, s + 1)
                    dve.tensor_tensor(ht_lo[:, bass.ds(4 * g, k), tok * P:(tok + 1) * P],
                                      trb[:, bank, 0:k * P].rearrange("p (k c) -> p k c", c=P),
                                      ht_hi[:, bass.ds(4 * g, k), tok * P:(tok + 1) * P].bitcast(F32),
                                      ALU.subtract).then_inc(tr_free[bank], 1)

                with dve.Fori(0, G_FULL - 1) as g:
                    gated(2 * g + i0, 0, 512)
                    for j in range(4):
                        n = n0 + 4 + j
                        if j == 3:
                            gated(2 * g + (i0 + 1), 1, 512)
                        split_unit(n, n % SLOTS, 4 * g + (n + 1))
                    h_low(2 * g + s0, t0 % 2, g, 0, 4)
                    h_low(2 * g + (s0 + 1), (t0 + 1) % 2, g, 1, 4)
                for g in (G_FULL - 1, G_FULL):
                    c = 512 if g < G_FULL else HALF
                    gated(i0 + 2 * g, 0, c)
                    n = n0 + 4 * (g + 1)
                    split_units(n, n + c // 128 - 1)
                    if g == G_FULL:
                        h_low(s0 + 2 * g, t0 % 2, g, 0, c // P)
                    gated(i0 + 2 * g + 1, 1, c)
                    split_units(n + c // 128 - 1, n + c // 128)
                    for tok in range(TOKS):
                        if tok or g < G_FULL:
                            h_low(s0 + 2 * g + tok, (t0 + tok) % 2, g, tok, c // P)
                split_units(n0 + UNITS_GU + 4, n0 + UNITS_FFN)
                norm(stage, 0)
                split_units(n0 + UNITS_FFN, n0 + UNITS_FFN + 2)
                if stage != "ffn3":
                    x_low(stage, 0)
                split_units(n0 + UNITS_FFN + 2, n0 + UNITS_FFN + 3)
                norm(stage, 1)
                split_units(n0 + UNITS_FFN + 3, n0 + UNITS_FFN + 4)

            def out_stage(stage):
                n = UNIT_OF[stage] + 4
                norm(stage, 0)
                split_units(n, n + 2)
                x_low(stage, 0)
                split_units(n + 2, n + 3)
                norm(stage, 1)
                split_units(n + 3, n + 4)

            def maxima(jobs, i, base):
                _, tok, heads, _ = jobs[i]
                maps = 2 * len(heads)
                dve.wait_ge(score_full, base + i + 1)
                dve.tensor_reduce(neg_max[:, i % 3, 0:maps],
                                  score_bank[i % 3].rearrange("p (m k) -> p m k", m=maps), AX.X, ALU.max,
                                  negate=True).then_inc(max_ready, 1)

            dve.wait_ge(const_in, 32)
            dve.tensor_copy(id_r[:, 0:P], squares[:, 0:P])
            dve.tensor_copy(id_r[:, P:P + DH], squares[:, 0:DH]).then_inc(masks_ready, 1)
            dve.tensor_copy(id_bf[:], squares[:, 0:P]).then_inc(acc_free, 1)
            dve.tensor_copy(diag_bf[:], squares[:, P:2 * P]).then_inc(masks_ready, 1)
            x_low("start", 0)
            split_units(0, 4)
            ffn_stage("ffn0", lambda: x_low("start", 1))

            n0 = UNIT_OF["nsa_in"]
            x_low("ffn0", 1)
            dve.wait_ge(small_in, 80)
            dve.tensor_copy(w2k2[:, 0, :], w2_sb[:, 0, :])
            dve.tensor_copy(w2k2[:, 1, :], w2_sb[:, 0, :])
            dve.memset(hid_rep[:], 0.0)
            link(dve.memset(kcb[:], 0.0))
            for tok in range(TOKS):
                filled(dve, "nsa_in", 0, tok)
                dve.tensor_copy(kv_a[:, tok, :], acc[:, 2 * tok:2 * tok + 2].rearrange("p a c -> p (a c)")[
                    :, 0:KV_COLS]).then_inc(acc_free, 1)
                split_units(n0 + 4 + 2 * tok, n0 + 6 + 2 * tok)
            for k in range(2):
                split_beside(k)
            for b in range(2):
                t = TURN_OF["kc", b]
                dve.wait_ge(tr_full, t + 1)
                for g in range(NSA_GROUPS):
                    for r in range(2):
                        rr = slice(r * DH, (r + 1) * DH)
                        lanes = trb[rr, t % 2, g * SEQ:(g + 1) * SEQ].rearrange("p (c l r) -> p c l r", l=8, r=2)
                        for a in range(2):
                            ins = dve.tensor_tensor(
                                blk[rr, b, 8 * a:8 * a + 8, g * N_CMP:(g + 1) * N_CMP],
                                lanes[:, a:a + N_CMP, :, r].rearrange("p c l -> p l c"),
                                bc(pos_sb[rr, b, 8 * a:8 * a + 8].unsqueeze(2), DH, 8, N_CMP), ALU.add)
                ins.then_inc(tr_free[t % 2], 1)

            def queries_out(tok):
                filled(dve, "nsa_in", 1, tok)
                dve.tensor_scalar(nq[:, tok, :], acc[:, 2 * tok:2 * tok + 2].rearrange("p a c -> p (a c)"),
                                  DH ** -0.5, None, ALU.mult).then_inc(acc_free, 1)

            def copy_queries(tok):
                for part in range(2):
                    copy_turned(("q", tok, part), nqt[:, 4 * part:4 * part + 4, tok * P:(tok + 1) * P])

            queries_out(0)
            copy_queries(0)
            dve.wait_ge(hid_ready, 2)
            for g in range(NSA_GROUPS):
                ins = dve.tensor_copy(hid_rep[:, g, :, 0:N_CMP],
                                      bc(hid[:, 1:2, g * N_CMP:(g + 1) * N_CMP], P, 8, N_CMP))
            ins.then_inc(cmp_ready, 1)
            dve.wait_ge(cmp_full, 1)
            for r in range(2):
                rr = slice(r * DH, (r + 1) * DH)
                ins = dve.tensor_copy(kcb[rr, :, r, 0:N_CMP],
                                      aux[rr, 0, 64:64 + 2 * N_CMP].rearrange("p (g c) -> p g c", g=2))
            ins.then_inc(cmp_ready, 1)
            dve.wait_ge(cmp_full, 2)
            heads8 = cst[:, C_HEAD:C_HEAD + 8].unsqueeze(2)
            for g in range(NSA_GROUPS):
                ins = dve.tensor_tensor(vcb[:, g], bc(aux[:, 1, 64 + g * DH:64 + (g + 1) * DH].unsqueeze(1), P, 8, DH),
                                        bc(heads8, P, 8, DH), ALU.mult)
            ins.then_inc(cmp_ready, 1)
            split_beside(2)
            dve.wait_ge(gate_exp, 1)
            gates = gate[:].rearrange("p t c -> p (t c)")
            link(dve.tensor_scalar(gates, gates, 1.0, None, ALU.add))
            dve.reciprocal(gates, gates)
            queries_out(1)

            def compressed_shift(tok):
                dve.wait_ge(cs_full, tok + 1)
                dve.tensor_tensor(cs[:, tok], aux[:, tok, 0:256].rearrange("p (h c) -> p h c", c=16),
                                  bc(cmp_mask[:, tok:tok + 1, :], P, NSA_HEADS, 16), ALU.add).then_inc(cs_copied, 1)
                dve.wait_ge(cs_copied, tok + 1)
                link(dve.tensor_reduce(cmax[:, tok, :], cs[:, tok], AX.X, ALU.max))
                dve.tensor_tensor(cs[:, tok], cs[:, tok], bc(cmax[:, tok, :].unsqueeze(2), P, NSA_HEADS, 16),
                                  ALU.subtract).then_inc(cs_shifted, 1)

            def compressed_share(tok):
                dve.wait_ge(cexp_done, tok + 1)
                link(dve.tensor_reduce(csum[:, tok, :], cs[:, tok], AX.X, ALU.add))
                link(dve.reciprocal(csum[:, tok, :], csum[:, tok, :]))
                link(dve.scalar_tensor_tensor(csum[:, tok, :], csum[:, tok, :], cst[:, C_ANY + tok:C_ANY + tok + 1],
                                              gate[:, tok, 0:NSA_HEADS], ALU.mult, ALU.mult))

            def nsa_mix(turn):
                tok, g = NSA_TURNS[turn]
                h0 = g * 8
                heads = slice(h0, h0 + 8)
                dve.wait_ge(exp_done, jobs_through(NSA_JOBS, turn))
                link(dve.reciprocal(share[:, :, 0:8], sums[:, tok, :, heads]))
                link(dve.tensor_tensor(share[:, :, 0:8], share[:, :, 0:8],
                                       gate[:, tok, NSA_HEADS:].rearrange("p (m h) -> p m h", m=2)[:, :, heads],
                                       ALU.mult))
                dve.wait_ge(turn_full, turn + 1)
                o = nq[:, tok, h0 * DH:(h0 + 8) * DH].rearrange("p (h d) -> p h d", d=DH)
                dst = [o] + [b.rearrange("p (h d) -> p h d", d=DH) for b in branch]
                parts = [(aux[:, 1], csum[:, tok, heads]), (acc[:, 2], share[:, 0, 0:8]), (acc[:, 3], share[:, 1, 0:8])]
                for to, (bank, f) in zip(dst, parts):
                    ins = dve.tensor_tensor(to, bank.rearrange("p (h d) -> p h d", d=DH),
                                            bc(f.unsqueeze(2), P, 8, DH), ALU.mult)
                ins.then_inc(turn_read, 1)
                dve.wait_ge(turn_read, turn + 1)
                link(dve.tensor_tensor(o, o, dst[1], ALU.add))
                dve.tensor_tensor(o, o, dst[2], ALU.add).then_inc(turn_mixed, 1)

            compressed_shift(0)
            for i, sc, tr, pv in job_steps(NSA_JOBS):
                if sc:
                    maxima(NSA_JOBS, i, 0)
                if i == 0:
                    copy_queries(1)
                if i == 1:
                    compressed_shift(1)
                if i == 2:
                    split_beside(3)
                    for tok in range(TOKS):
                        compressed_share(tok)
                if pv >= 0 and NSA_JOBS[pv][3]:
                    nsa_mix(NSA_JOBS[pv][0])
                if i - 1 in NSA_UNIT_STEPS:
                    k = NSA_UNIT_STEPS.index(i - 1)
                    split_units(n0 + 8 + k, n0 + 9 + k)
                if ends_turn(NSA_JOBS, pv, 2):
                    x_low("nsa_o", 0)
            x_low("nsa_o", 1)
            out_stage("nsa_out")
            ffn_stage("ffn1", lambda: x_low("nsa_out", 1))

            n0 = UNIT_OF["kv"]
            x_low("ffn1", 1)
            for tok in range(TOKS):
                filled(dve, "kv", 0, tok)
                dve.tensor_copy(k_nat[:, tok, :], acc[:, 2 * tok:2 * tok + 2].rearrange("p a c -> p (a c)")).then_inc(
                    acc_free, 1)
                split_units(n0 + 4 + 2 * tok, n0 + 6 + 2 * tok)
            for tok in range(TOKS):
                filled(dve, "kv", 1, tok)
                dve.tensor_copy(v_b[:, tok, :], acc[:, 2 * tok:2 * tok + 2].rearrange("p a c -> p (a c)")).then_inc(
                    acc_free, 1)
                split_units(n0 + 8 + 2 * tok, n0 + 10 + 2 * tok)
            ffn_stage("ffn2", lambda: None)

            n0 = UNIT_OF["diff_q"]
            x_low("ffn2", 1)
            link(dve.tensor_tensor(lam_pr, lam_in[:, 0:4:2, :], lam_in[:, 1:4:2, :], ALU.mult))
            dve.tensor_reduce(lam[:, 0:2], lam_pr, AX.X, ALU.add).then_inc(lam_sum, 1)
            for k in range(4, 6):
                split_beside(k)

            def diff_queries_out(tok):
                filled(dve, "diff_q", 0, tok)
                dve.wait_ge(beside_ready, 5 + tok)
                dve.tensor_scalar(dq[:, tok, :], acc[:, 2 * tok:2 * tok + 2].rearrange("p a c -> p (a c)"),
                                  DH ** -0.5, None, ALU.mult).then_inc(acc_free, 1)

            diff_queries_out(0)
            dve.wait_ge(lam_exp, 1)
            link(dve.tensor_tensor(lam[:, 2:3], lam[:, 0:1], lam[:, 1:2], ALU.subtract))
            dve.tensor_scalar(lam[:, 3:4], lam[:, 2:3], LAMBDA_INIT, None, ALU.add)

            def copy_heads(name, tok, part, dst):
                copy_turned((name, "diff", tok, part), dst[:, 4 * part:4 * part + 4, tok * P:(tok + 1) * P])

            for part in (1, 3):
                copy_heads("kr", 0, part, dks[:, 0])
            split_beside(6)
            for part in (1, 3):
                copy_heads("kr", 1, part, dks[:, 0])
            for part in (1, 3):
                copy_heads("ks", 0, part, dks[:, 1])
            copy_heads("ks", 1, 1, dks[:, 1])
            diff_queries_out(1)
            copy_heads("ks", 1, 3, dks[:, 1])
            for part in (1, 3):
                copy_heads("qr", 0, part, dqs)
            split_beside(7)

            def diff_read(turn):
                tok, g = DIFF_TURNS[turn]
                heads = slice(4 * g, 4 * g + 4)
                dve.wait_ge(exp_done, len(NSA_JOBS) + jobs_through(DIFF_JOBS, turn))
                link(dve.reciprocal(share[:, :, 0:4], sums[:, tok, :, heads]))
                link(dve.tensor_scalar(share[:, 1, 0:4], share[:, 1, 0:4], lam[:, 3:4], None, ALU.mult))
                dve.wait_ge(turn_full, len(NSA_TURNS) + turn + 1)
                for m, dst in enumerate(diff_parts(turn)):
                    ins = dve.tensor_tensor(dst, acc[:, 2 + m].rearrange("p (h d) -> p h d", d=DIFF_V),
                                            bc(share[:, m, 0:4].unsqueeze(2), P, 4, DIFF_V), ALU.mult)
                ins.then_inc(turn_read, 1)

            def diff_parts(turn):
                tok, g = DIFF_TURNS[turn]
                return [v.rearrange("p (h d) -> p h d", d=DIFF_V)
                        for v in (dq[:, tok, g * 512:(g + 1) * 512], branch[0])]

            def diff_subtract(turn):
                o, t = diff_parts(turn)
                dve.wait_ge(turn_read, len(NSA_TURNS) + turn + 1)
                link(dve.tensor_tensor(o, o, t, ALU.subtract))
                link(dve.tensor_tensor(t, o, o, ALU.mult))
                link(dve.tensor_reduce(rms[:, 0, :], t, AX.X, ALU.add))
                dve.tensor_scalar(rms[:, 0, :], rms[:, 0, :], 1.0 / DIFF_V, EPS, ALU.mult, ALU.add).then_inc(
                    rms_ready, 1)

            def diff_norm(turn):
                o, _ = diff_parts(turn)
                dve.wait_ge(rms_pow, turn + 1)
                link(dve.tensor_tensor(o, o, bc(rms[:, 1, :].unsqueeze(2), P, 4, DIFF_V), ALU.mult))
                dve.scalar_tensor_tensor(o, o, 1.0 - LAMBDA_INIT, bc(sub_g[:].unsqueeze(1), P, 4, DIFF_V),
                                         ALU.mult, ALU.mult).then_inc(turn_mixed, 1)

            last = len(DIFF_TURNS) - 1
            for i, sc, tr, pv in job_steps(DIFF_JOBS):
                if sc:
                    maxima(DIFF_JOBS, i, len(NSA_JOBS))
                for turn in range(last):
                    if ends_turn(DIFF_JOBS, pv - 1, turn):
                        diff_subtract(turn)
                    if ends_turn(DIFF_JOBS, pv - 2, turn):
                        diff_norm(turn)
                if pv >= 0 and DIFF_JOBS[pv][3]:
                    diff_read(DIFF_JOBS[pv][0])
                if i - 1 in DIFF_UNIT_STEPS:
                    k = DIFF_UNIT_STEPS.index(i - 1)
                    split_units(n0 + 4 + k, n0 + 5 + k)
                if ends_turn(DIFF_JOBS, pv, 2):
                    x_low("diff_o", 0)
            diff_subtract(last)
            diff_norm(last)
            x_low("diff_o", 1)
            out_stage("diff_out")
            ffn_stage("ffn3", lambda: x_low("diff_out", 1))

        @block.tensor
        def _(pe):
            def three(out_ap, s_hi, s_lo, hi, lo, first, last):
                pe.matmul(out_ap, s_hi, hi, start=first, stop=False)
                pe.matmul(out_ap, s_hi, lo, start=False, stop=False)
                return pe.matmul(out_ap, s_lo, hi, start=False, stop=last)

            def columns_unit(n, j, tok):
                hi, lo = weights(w_hi, n), weights(w_lo, n)
                cols = hi.shape[2]
                for k in range(4):
                    kt = 4 * (j % 2) + k
                    ins = three(acc[:, 2 * tok + j // 2, 0:cols], xt_hi[:, kt, tok * P:(tok + 1) * P],
                                xt_lo[:, kt, tok * P:(tok + 1) * P], hi[:, k, :], lo[:, k, :], kt == 0, kt == KT - 1)
                return ins

            def half_unit(n, j, tok):
                hi, lo = weights(w_hi, n), weights(w_lo, n)
                for kt in range(KT):
                    ins = three(acc[:, 2 * tok + j, 0:HALF], xt_hi[:, kt, tok * P:(tok + 1) * P],
                                xt_lo[:, kt, tok * P:(tok + 1) * P], hi[:, kt, :], lo[:, kt, :], kt == 0,
                                kt == KT - 1)
                return ins

            def rows_unit(s_hi, s_lo, tiles):
                def emit(n, j, tok):
                    hi, lo = weights(w_hi, n), weights(w_lo, n)
                    for k in range(2):
                        kt = 2 * j + k
                        sh, sl = (s[:, kt, tok * P:(tok + 1) * P] for s in (s_hi, s_lo))
                        for c in range(2):
                            cols = slice(c * 512, (c + 1) * 512)
                            ins = three(acc[:, 2 * tok + c], sh, sl, hi[:, k, cols], lo[:, k, cols], kt == 0,
                                        kt == tiles - 1)
                    return ins
                return emit

            def run_units(tok, n0, js, emit, ready=None, between=None):
                for pos, j in enumerate(js):
                    n = n0 + j
                    if between and pos in between:
                        between[pos]()
                    if tok == 0:
                        pe.wait_ge(lo_ready, n + 1 if ready is None else ready + pos)
                    ins = emit(n, j, tok)
                    if tok == 1:
                        ins.then_inc(unit_used, 1)
                return ins

            def turn_blocks(t, bank, blocks, wait):
                if wait is not None:
                    pe.wait_ge(tr_free[bank], wait)
                for j, b in enumerate(blocks):
                    ins = pe.transpose(trb[:, bank, j * P:(j + 1) * P], b, ident)
                ins.then_inc(tr_full, 1)

            def turn(name, blocks):
                t = TURN_OF[name]
                turn_blocks(t, t % 2, blocks, t // 2 if t >= 2 else None)

            def turn_wide(name, src):
                for part in range(2):
                    turn((*name, part), [src[:, (4 * part + j) * P:(4 * part + j + 1) * P] for j in range(4)])

            def turn_x(stage, tok):
                pe.wait_ge(x_ready, 2 * NORM_OF[stage] + tok + 1)
                turn_wide(("x", stage, tok), x[:, tok, :])

            def copied(*name):
                t = TURN_OF[name]
                pe.wait_ge(tr_free[t % 2], t // 2 + 1)

            def open_acc(e):
                if e >= 2:
                    pe.wait_ge(acc_free, e - 1)

            def finish(tok, ins):
                if tok == 0:
                    ins.then_inc(tile0_full, 1)

            def group(tok, e, n0, js, emit, between=None, operand=None):
                open_acc(e)
                if operand is not None:
                    for part in range(2):
                        copied(*operand, part)
                finish(tok, run_units(tok, n0, js, emit, between=between))

            def ffn_stage(stage, turn_rest, operand, next_x):
                n0, e0, t0 = UNIT_OF[stage], FILL_OF[stage, 0, 0], TURN_OF["h", stage, 0, 0]

                def turn_h(g, tok, k):
                    pe.wait_ge(acc_free, 2 * g + (e0 + tok + 1))
                    turn_blocks(None, (t0 + tok) % 2, [h_nat[:, tok, j * P:(j + 1) * P] for j in range(k)],
                                g + (t0 + tok) // 2)

                group(0, e0, n0, range(4), columns_unit, {3: turn_rest}, (*operand, 0))
                for part in range(2):
                    copied(*operand, 1, part)
                with pe.Fori(0, G_FULL - 1) as g:
                    pe.wait_ge(acc_free, 2 * g + e0)
                    ins = run_units(1, n0, range(4), columns_unit,
                                    between={3: lambda: turn_h(g, 0, 4)})
                    finish(1, ins)
                    pe.wait_ge(acc_free, 2 * g + (e0 + 1))
                    ins = run_units(0, n0, range(4), columns_unit, ready=4 * g + (n0 + 5),
                                    between={3: lambda: turn_h(g, 1, 4)})
                    finish(0, ins)
                g = G_FULL - 1
                group(1, e0 + 2 * g + 1, n0 + 4 * g, range(4), columns_unit,
                      {3: lambda: turn_h(G_FULL - 1, 0, 4)})
                group(0, e0 + 2 * g + 2, n0 + 4 * g + 4, range(2), half_unit,
                      {1: lambda: turn_h(G_FULL - 1, 1, 4)})
                g = G_FULL
                group(1, e0 + 2 * g + 1, n0 + 4 * g, range(2), half_unit,
                      {1: lambda: turn_h(g, 0, 2)})
                emit = rows_unit(ht_hi, ht_lo, FT)
                e = e0 + 2 * (G_FULL + 1)
                open_acc(e)
                for i, js in enumerate(DOWN_GROUPS):
                    if i == len(DOWN_GROUPS) - 1:
                        for tok in range(TOKS):
                            copied("h", stage, G_FULL, tok)
                    ins = run_units(0, n0 + UNITS_GU, js, emit, between={
                        len(js) - 1: lambda: turn_h(G_FULL, 1, 2)}
                        if i == 0 else None)
                    if i == len(DOWN_GROUPS) - 1:
                        finish(0, ins)
                    if i == 0:
                        open_acc(e + 1)
                    ins = run_units(1, n0 + UNITS_GU, js, emit, between={
                        3: lambda: turn_x(stage, 0)} if next_x and i == len(DOWN_GROUPS) - 1 else None)
                    if i == len(DOWN_GROUPS) - 1:
                        finish(1, ins)

            def out_stage(stage, o_name):
                n0, e = UNIT_OF[stage], FILL_OF[stage, 0, 0]
                emit = rows_unit(xt_hi, xt_lo, KT)
                turns = len(NSA_TURNS) if stage == "nsa_out" else len(NSA_TURNS) + len(DIFF_TURNS)
                jobs = len(NSA_JOBS) if stage == "nsa_out" else len(NSA_JOBS) + len(DIFF_JOBS)
                src = nq if stage == "nsa_out" else dq

                def turn_o():
                    pe.wait_ge(turn_mixed, turns)
                    turn_wide(("x", o_name, 1), src[:, 1, :])

                pe.wait_ge(exp_done, jobs)
                group(0, e, n0, range(4), emit, {3: turn_o}, ("x", o_name, 0))
                group(1, e + 1, n0, range(4), emit, {3: lambda: turn_x(stage, 0)}, ("x", o_name, 1))

            def scores(jobs, i, base, q_t, key_t):
                _, tok, heads, _ = jobs[i]
                width = P * (tok + 1)
                if i >= 3:
                    pe.wait_ge(exp_done, base + i - 2)
                bank, k = score_bank[i % 3], 0
                for h in heads:
                    for m in range(2):
                        for part in range(2):
                            pe.matmul(bank[:, k * width:(k + 1) * width], q_t(h, m)[:, tok * P:(tok + 1) * P],
                                      key_t(h, m, part)[:, 0:width], start=(part == 0), stop=False)
                        ins = pe.matmul(bank[:, (k + 1) * width - P:(k + 1) * width], id_bf[:], diag_bf[:],
                                        start=False, stop=True)
                        k += 1
                ins.then_inc(score_full, 1)

            def turn_p(kind, i, base):
                pe.wait_ge(exp_done, base + i + 1)
                turn(("p", kind, i), [probs[:, i % 3, j * P:(j + 1) * P] for j in range(4)])

            def values(kind, jobs, j, base, pt_sb, v_of, width, first, per_turn):
                turn_no, tok, heads, last = jobs[j]
                if j == 0 or jobs[j - 1][3]:
                    first(turn_no)
                copied("p", kind, j)
                k = 0
                for h in heads:
                    for m in range(2):
                        for kb in range(tok + 1):
                            ins = pe.matmul(acc[:, 2 + m, (h % per_turn) * width:(h % per_turn + 1) * width],
                                            pt_sb[:, j % 2, k * P:(k + 1) * P], v_of(h, m, kb), start=(kb == 0),
                                            stop=(kb == tok))
                            k += 1
                if last:
                    ins.then_inc(turn_full, 1)

            pe.wait_ge(masks_ready, 1)
            for tok in range(TOKS):
                if tok == 0:
                    pe.wait_ge(x_landed, 32)
                    turn_wide(("x", "start", 0), x[:, 0, :])
            ffn_stage("ffn0", lambda: turn_wide(("x", "start", 1), x[:, 1, :]), ("x", "start"), True)

            n0 = UNIT_OF["nsa_in"]

            def turn_kc(b):
                pe.wait_ge(k_dup, 2)
                turn(("kc", b), [y[:, tok, b * 256 + g * P:b * 256 + (g + 1) * P] for g in range(NSA_GROUPS)
                                 for tok in range(TOKS)])

            def turn_kr(m):
                pe.wait_ge(beside_ready, 2)
                turn(("kr", m), [beside[tok][:, 2 * m + g].rearrange("p s d -> p (s d)").bitcast(F32)
                                 for g in range(NSA_GROUPS) for tok in range(TOKS)])

            def swap_halves(name, of, src):
                t = TURN_OF[name]
                copied(*of)
                pe.wait_ge(tr_free[t % 2], t // 2)
                pe.matmul(trb[:, t % 2], swap, src, start=True, stop=True).then_inc(tr_full, 1)

            def hidden(b):
                copied("kc", b)
                pe.wait_ge(w1_in, 32)
                w = w1k if b == 0 else w1v[:]
                for pair in range(CMP_BLOCK // 2):
                    ins = pe.matmul(aux[:, b, 0:2 * N_CMP], w[:, pair, :], blk[:, b, pair, :], start=(pair == 0),
                                    stop=(pair == CMP_BLOCK // 2 - 1))
                ins.then_inc(hid_full, 1)

            def second_layer():
                pe.wait_ge(hid_ready, 1)
                pe.matmul(aux[:, 0, 64:64 + 2 * N_CMP], w2k2[:].rearrange("p r d -> p (r d)"), hid[:, 0, :],
                          start=True, stop=True).then_inc(cmp_full, 1)
                pe.wait_ge(cmp_ready, 1)
                for g in range(NSA_GROUPS):
                    ins = pe.matmul(aux[:, 1, 64 + g * DH:64 + (g + 1) * DH],
                                    hid_rep[:, g].rearrange("p h c -> p (h c)"), w2_sb[:, 1, :], start=True, stop=True)
                ins.then_inc(cmp_full, 1)

            def turn_q(tok):
                pe.wait_ge(acc_free, FILL_OF["nsa_in", 1, tok] + 1)
                turn_wide(("q", tok), nq[:, tok, :])

            def turn_heads(name, tok, part, k):
                pe.wait_ge(beside_ready, k + 1)
                turn((*name, tok, part), [beside[k][:, 4 * part + j].rearrange("p s d -> p (s d)").bitcast(F32)
                                          for j in range(4)])

            def compressed_scores(tok):
                for part in range(2):
                    copied("q", tok, part)
                if tok == 0:
                    pe.wait_ge(cmp_ready, 3)
                for pair in range(NSA_HEADS // 2):
                    ins = pe.matmul(aux[:, tok, pair * 32:(pair + 1) * 32], nqt[:, pair, tok * P:(tok + 1) * P],
                                    kcb[:, pair // 4].rearrange("p r c -> p (r c)"), start=True, stop=True)
                ins.then_inc(cs_full, 1)

            e = FILL_OF["nsa_in", 0, 0]
            group(0, e, n0, range(4), columns_unit, {3: lambda: turn_x("ffn0", 1)}, ("x", "ffn0", 0))
            group(1, e + 1, n0, range(4), columns_unit, None, ("x", "ffn0", 1))
            group(0, e + 2, n0 + 4, range(4), columns_unit, {2: lambda: turn_kc(0), 3: lambda: turn_kc(1)})
            group(1, e + 3, n0 + 4, range(4), columns_unit,
                  {0: lambda: hidden(0), 1: lambda: (hidden(1), turn_q(0)),
                   2: lambda: (turn_kr(0), turn_kr(1), second_layer()),
                   3: lambda: [swap_halves(("ks", m), ("kr", m), nks[:, 0, m].rearrange("p g t -> p (g t)"))
                               for m in range(2)]})
            compressed_scores(0)
            for part in range(4):
                turn_heads(("qr", "nsa"), 0, part, 2)

            def nsa_first(turn_no):
                tok, g = NSA_TURNS[turn_no]
                if turn_no:
                    pe.wait_ge(turn_read, turn_no)
                else:
                    pe.wait_ge(cs_copied, 2)
                    copied("pc")
                pe.matmul(aux[:, 1], pct[:, 2 * tok + g, :], vcb[:, g].rearrange("p h d -> p (h d)"), start=True,
                          stop=True)

            pe.wait_ge(masks_ready, 2)
            pe.wait_ge(acc_free, e + 3)
            for i, sc, tr, pv in job_steps(NSA_JOBS):
                if i in (0, 8):
                    for part in range(4):
                        copied("qr", "nsa", i // 8, part)
                if i == 0:
                    for m in range(2):
                        copied("ks", m)
                if i == 2:
                    pe.wait_ge(cs_copied, 1)
                if sc:
                    scores(NSA_JOBS, i, 0, lambda h, m: nqs[:, h], lambda h, m, part: nks[:, part, m, h // 8])
                if i == 0:
                    turn_q(1)
                if i == 1:
                    compressed_scores(1)
                if tr:
                    turn_p("nsa", i - 2, 0)
                if i == 3:
                    pe.wait_ge(cexp_done, 2)
                    turn(("pc",), [cs[:, tok, 8 * g:8 * g + 8].rearrange("p h c -> p (h c)")
                                   for tok in range(TOKS) for g in range(NSA_GROUPS)])
                if 3 <= i < 7:
                    turn_heads(("qr", "nsa"), 1, i - 3, 3)
                if pv >= 0:
                    values("nsa", NSA_JOBS, pv, 0, npt,
                           lambda h, m, kb: kv_a[:, kb, (VS, VW)[m] + (h // 8) * DH:(VS, VW)[m] + (h // 8 + 1) * DH],
                           DH, nsa_first, 8)
                if ends_turn(NSA_JOBS, pv, 2):
                    pe.wait_ge(turn_mixed, 2)
                    turn_wide(("x", "nsa_o", 0), nq[:, 0, :])
            out_stage("nsa_out", "nsa_o")
            ffn_stage("ffn1", lambda: turn_x("nsa_out", 1), ("x", "nsa_out"), True)

            n0, e = UNIT_OF["kv"], FILL_OF["kv", 0, 0]

            group(0, e, n0, range(4), columns_unit, {3: lambda: turn_x("ffn1", 1)}, ("x", "ffn1", 0))
            group(1, e + 1, n0, range(4), columns_unit, None, ("x", "ffn1", 1))
            group(0, e + 2, n0 + 4, range(4), columns_unit)
            group(1, e + 3, n0 + 4, range(4), columns_unit)
            ffn_stage("ffn2", lambda: None, ("x", "ffn1"), True)

            n0, e = UNIT_OF["diff_q"], FILL_OF["diff_q", 0, 0]
            def swap_keys(parts):
                for tok, part in parts:
                    swap_halves(("ks", "diff", tok, part), ("kr", "diff", tok, part),
                                dks[:, 0, 4 * part:4 * part + 4, tok * P:(tok + 1) * P])

            parts = [(tok, part) for tok in range(TOKS) for part in range(4)]
            group(0, e, n0, range(4), columns_unit,
                  {3: lambda: turn_x("ffn2", 1)}, ("x", "ffn2", 0))
            group(1, e + 1, n0, range(4), columns_unit,
                  {1: lambda: [turn_heads(("kr", "diff"), tok, part, 4 + tok) for tok, part in parts[:4]],
                   2: lambda: [turn_heads(("kr", "diff"), tok, part, 4 + tok) for tok, part in parts[4:]],
                   3: lambda: swap_keys(parts[:4])}, ("x", "ffn2", 1))
            swap_keys(parts[4:])
            for part in range(4):
                turn_heads(("qr", "diff"), 0, part, 6)
            pe.wait_ge(acc_free, e + 1)
            base = len(NSA_JOBS)

            def diff_first(turn_no):
                if turn_no:
                    pe.wait_ge(turn_read, len(NSA_TURNS) + turn_no)

            for i, sc, tr, pv in job_steps(DIFF_JOBS):
                if i in (0, 4):
                    for part in range(4):
                        copied("qr", "diff", i // 4, part)
                if i == 0:
                    for tok, part in parts:
                        copied("ks", "diff", tok, part)
                if sc:
                    scores(DIFF_JOBS, i, base, lambda h, m: dqs[:, 8 * m + h],
                           lambda h, m, part: dks[:, part, 8 * m + h])
                if tr:
                    turn_p("diff", i - 2, base)
                for part in LATE_PARTS.get(i, ()):
                    turn_heads(("qr", "diff"), 1, part, 7)
                if pv >= 0:
                    values("diff", DIFF_JOBS, pv, base, dpt,
                           lambda h, m, kb: v_b[:, kb, h * DIFF_V:(h + 1) * DIFF_V], DIFF_V, diff_first, 4)
                if ends_turn(DIFF_JOBS, pv, 2):
                    pe.wait_ge(turn_mixed, len(NSA_TURNS) + 2)
                    turn_wide(("x", "diff_o", 0), dq[:, 0, :])
            out_stage("diff_out", "diff_o")
            ffn_stage("ffn3", lambda: turn_x("diff_out", 1), ("x", "diff_out"), False)


def constants():
    import numpy as np
    c = np.zeros((P, C_COLS), np.float32)
    q = np.arange(P)
    squares = np.concatenate([np.eye(P), np.where(q[None, :] <= q[:, None], 0.0, NEG)], 1).astype(np.float32)
    half = ROT // 2
    inv = np.float32(500000.0) ** (-np.arange(half, dtype=np.float32) * np.float32(2.0) / np.float32(ROT))
    ang = np.arange(SEQ, dtype=np.float32)[:, None] * inv[None, :].astype(np.float32)
    for tok in range(TOKS):
        a = np.tile(ang[tok * P:(tok + 1) * P], (1, 2))
        c[:, C_COS + tok * ROT:C_COS + (tok + 1) * ROT] = np.cos(a)
        c[:, C_SIN + tok * ROT:C_SIN + (tok + 1) * ROT] = np.sin(a)
        end = np.arange(16) * CMP_STRIDE + CMP_BLOCK - 1
        sees = (end[None, :] <= (q + tok * P)[:, None]) & (np.arange(16) < N_CMP)[None, :]
        c[:, C_CMP + tok * 16:C_CMP + (tok + 1) * 16] = np.where(sees, 0.0, NEG)
        c[:, C_ANY + tok] = sees.any(1)
    c[:, C_HEAD:C_HEAD + 8] = (q[:, None] // 16) == np.arange(8)[None, :]
    return c, squares


def kernel(**inputs):
    import numpy as np
    import concourse.bacc as bacc
    from concourse.bass_utils import run_bass_kernel_spmd as run

    nc = bacc.Bacc("TRN2", target_bir_lowering=False, num_devices=1)
    arrays = {}

    def dram(name, a):
        a = np.ascontiguousarray(a)
        arrays[name] = a
        return nc.dram_tensor(name, a.shape, mybir.dt.from_np(a.dtype), kind="ExternalInput").ap()

    a = {k: np.asarray(v) for k, v in inputs.items()}

    def ffn(which):
        return [dram(f"ffn{b}_{which}_{layer}", a[f"ffn{b}_{which}"][layer]) for layer in range(DEPTH) for b in (1, 2)]

    def two(name):
        return [a[f"a_cmp_{name}_k"][0], a[f"a_cmp_{name}_v"][0]]

    args = [
        dram("x_in", a["x"][0]),
        dram("const", constants()[0]),
        dram("squares", constants()[1]),
        ffn("w_gate"), ffn("w_up"), ffn("w_down"),
        dram("norm_gain", a["ln_g"].reshape(3 * DEPTH, D)),
        dram("norm_bias", a["ln_b"].reshape(3 * DEPTH, D)),
        dram("w_in", a["a_w_in"][0]),
        dram("w_out_a", a["a_w_out"][0]),
        dram("cmp_pos", np.stack([p.reshape(CMP_BLOCK // 2, 2 * DH).T for p in two("pos")])),
        dram("cmp_w1", np.stack(two("w1"))),
        dram("cmp_b1", np.stack(two("b1"), axis=1)),
        dram("cmp_w2", np.stack(two("w2"))),
        dram("w_kv", a["b_w_kv_shared"]),
        dram("w_q", a["b_w_q"][0]),
        dram("lambdas", np.stack([a[f"b_lambda_{n}"][0] for n in ("q1", "k1", "q2", "k2")])),
        dram("subln_g", a["b_subln_g"][0]),
        dram("w_out_b", a["b_w_out"][0]),
        nc.dram_tensor("out", (SEQ, D), F32, kind="ExternalOutput").ap(),
    ]
    build_program(nc, *args)
    r = run(nc, [arrays], core_ids=[0])
    return r.results[0]["out"].reshape(1, SEQ, D)
```

```python
from contextlib import ExitStack

import concourse.bass as bass
from concourse import mybir

F32 = mybir.dt.float32
F32R = mybir.dt.float32r
BF16 = mybir.dt.bfloat16
ALU = mybir.AluOpType
ACT = mybir.ActivationFunctionType
AX = mybir.AxisListType

P = 128
SEQ, D, FF, DEPTH = 256, 1024, 2816, 2
TOKS = SEQ // P
KT = D // P
FT = FF // P
NSA_HEADS, NSA_GROUPS, DH = 16, 2, 64
CMP_BLOCK, CMP_STRIDE, HID = 32, 16, 128
N_CMP = (SEQ - CMP_BLOCK) // CMP_STRIDE + 1
SLC_BLOCK, SLC_TOPK, WINDOW = 64, 16, 512
DIFF_HEADS, DIFF_V = 8, 128
ROT = DH // 4
KV_COLS = 6 * NSA_GROUPS * DH + 3 * NSA_HEADS
ALPHA = (2 * DEPTH) ** 0.25
EPS = 1e-5
NEG = -1e30
LAMBDA_INIT = 0.8 - 0.6 * 0.7408182206817179

assert SEQ // SLC_BLOCK <= SLC_TOPK and SEQ <= WINDOW
assert TOKS == 2 and KT == 8

C_COS, C_SIN, C_CMP, C_ANY, C_HEAD, C_COLS = 0, 32, 64, 96, 98, 106
KC, VC, KS, VS, KW, VW, GT = 0, 128, 256, 384, 512, 640, 768

SLOTS = 4
UNIT = 2048
G_FULL = FF // 512
HALF = FF - 512 * G_FULL
UNITS_GU = 4 * G_FULL + 2
UNITS_DOWN = FT // 2
UNITS_FFN = UNITS_GU + UNITS_DOWN
DOWN_GROUPS = [[0, 1, 2], [3, 4, 5, 6], [7, 8, 9, 10]]
assert HALF == 256 and DOWN_GROUPS[-1][-1] == UNITS_DOWN - 1

STAGES = ["ffn0", "nsa_in", "nsa_out", "ffn1", "kv", "ffn2", "diff_q", "diff_out", "ffn3"]
STAGE_UNITS = {"nsa_in": 8, "nsa_out": 4, "kv": 8, "diff_q": 4, "diff_out": 4}
STAGE_UNITS.update({f"ffn{i}": UNITS_FFN for i in range(4)})
NORM_OF = {"ffn0": 0, "nsa_out": 1, "ffn1": 2, "ffn2": 3, "diff_out": 4, "ffn3": 5}


def attention_jobs(heads_per_turn):
    jobs, turns = [], []
    for tok in range(TOKS):
        for share in range(2):
            h0 = share * heads_per_turn
            per_job = 2 - tok
            sets = [list(range(h, h + per_job)) for h in range(h0, h0 + heads_per_turn, per_job)]
            jobs += [(len(turns), tok, heads, heads is sets[-1]) for heads in sets]
            turns.append((tok, share))
    return jobs, turns


NSA_JOBS, NSA_TURNS = attention_jobs(NSA_HEADS // 2)
DIFF_JOBS, DIFF_TURNS = attention_jobs(DIFF_HEADS // 2)

TILE0_DONE = {"nsa": (14, 15), "diff": (10, 11)}
LATE_PARTS = {"nsa": {6: (0,), 9: (1,), 11: (2,), 13: (3,)}, "diff": {2: (0,), 3: (2,), 4: (1,), 5: (3,)}}


def job_steps(jobs):
    for i in range(len(jobs) + 3):
        yield i, i < len(jobs), 0 <= i - 2 < len(jobs), i - 3


def ends_turn(jobs, j, turn):
    return j >= 0 and jobs[j][3] and jobs[j][0] == turn


def jobs_through(jobs, turn):
    return sum(job[0] <= turn for job in jobs)


def count_events():
    unit, fill, turn = {}, {}, []
    n = 0
    for stage in STAGES:
        unit[stage] = n
        n += STAGE_UNITS[stage]
    e = 1
    for stage in STAGES:
        groups = G_FULL + 2 if stage.startswith("ffn") else 2 if stage in ("nsa_in", "kv") else 1
        for g in range(groups):
            for tok in range(TOKS):
                fill[stage, g, tok] = e
                e += 1

    def pair(*name):
        turn.extend([(*name, 0), (*name, 1)])

    def four(*name):
        turn.extend([(*name, part) for part in range(4)])

    pair("x", "start", 0)
    pair("x", "start", 1)
    for stage in STAGES:
        if stage.startswith("ffn"):
            for g in range(G_FULL + 1):
                turn.extend([("h", stage, g, 0), ("h", stage, g, 1)])
        if stage == "nsa_in":
            turn.extend([("kc", 0), ("kc", 1)])
            pair("q", 0)
            turn.extend([("kr", 0), ("kr", 1), ("ks", 0), ("ks", 1)])
            four("qr", "nsa", 0)
            for i, _, tr, pv in job_steps(NSA_JOBS):
                if i == 0:
                    pair("q", 1)
                if tr:
                    turn.append(("p", "nsa", i - 2))
                if i == 3:
                    turn.append(("pc",))
                for part in LATE_PARTS["nsa"].get(i, ()):
                    turn.append(("qr", "nsa", 1, part))
                if i in TILE0_DONE["nsa"]:
                    turn.append(("x", "nsa_o", 0, TILE0_DONE["nsa"].index(i)))
            pair("x", "nsa_o", 1)
        if stage == "diff_q":
            for name in ("kr", "ks"):
                for tok in range(TOKS):
                    four(name, "diff", tok)
            four("qr", "diff", 0)
            for i, _, tr, pv in job_steps(DIFF_JOBS):
                if tr:
                    turn.append(("p", "diff", i - 2))
                for part in LATE_PARTS["diff"].get(i, ()):
                    turn.append(("qr", "diff", 1, part))
                if i in TILE0_DONE["diff"]:
                    turn.append(("x", "diff_o", 0, TILE0_DONE["diff"].index(i)))
            pair("x", "diff_o", 1)
        if stage in NORM_OF and stage != "ffn3":
            for tok in range(TOKS):
                pair("x", stage, tok)
    return unit, fill, {name: i for i, name in enumerate(turn)}, {
        name: i for i, name in enumerate([t for t in turn if t[0] in "xh"])}


UNIT_OF, FILL_OF, TURN_OF, SPLIT_OF = count_events()


def units_through(stage, g):
    if stage.startswith("ffn"):
        in_stage = min(4 * (g + 1), UNITS_GU) if g <= G_FULL else UNITS_FFN
    else:
        in_stage = 4 * (g + 1)
    return UNIT_OF[stage] + in_stage


TILE0_FILLS = {(s, g): e // TOKS + 1 for (s, g, tok), e in FILL_OF.items() if tok == 0}
N_UNITS = UNIT_OF["ffn3"] + UNITS_FFN


def unit_shape(n):
    stage = [s for s in STAGES if UNIT_OF[s] <= n][-1]
    j = n - UNIT_OF[stage]
    if stage.startswith("ffn"):
        return (4, 512) if j < 4 * G_FULL else (8, HALF) if j < UNITS_GU else (2, D)
    if stage in ("nsa_out", "diff_out"):
        return 2, D
    if stage == "nsa_in" and j in (2, 3):
        return 4, KV_COLS - 512
    return 4, 512


def build_program(nc, x_in, const, squares_in, w_gates, w_ups, w_downs, ln_g, ln_b, w_in, w_out_a,
                  cmp_pos, cmp_w1, cmp_b1, cmp_w2, w_kv, w_q, lambdas, subln_g, w_out_b, out):
    with ExitStack() as ctx:
        def sb(name, shape, dt=F32, scope=ctx):
            return scope.enter_context(nc.sbuf_tensor(name, shape, dt))

        def sem(name):
            return ctx.enter_context(nc.semaphore(name))

        raw = sb("raw", [P, SLOTS, UNIT])
        w_hi = sb("w_hi", [P, SLOTS, UNIT], F32R)
        w_lo = sb("w_lo", [P, SLOTS, UNIT], F32R)
        x = sb("x", [P, TOKS, D])
        y = sb("y", [P, TOKS, D])
        xt_hi = sb("xt_hi", [P, KT, SEQ], F32R)
        xt_lo = sb("xt_lo", [P, KT, SEQ], F32R)
        norm_gb = sb("norm_gb", [P, 2, D])
        probs = norm_gb[:].rearrange("p a c -> p (a c)")[:, 0:1536].rearrange("p (j c) -> p j c", j=3)
        w1k = norm_gb[:].rearrange("p a (b h) -> p (a b) h", h=HID)
        cst = sb("cst", [P, C_COLS])
        id_r = sb("id_r", [P, P + DH], F32R)
        id_bf = sb("id_bf", [P, P], BF16)
        diag_bf = sb("diag_bf", [P, P], BF16)
        pos_sb = sb("pos_sb", [P, 2, CMP_BLOCK // 2])
        b1_sb = sb("b1_sb", [P, 2])
        w2_sb = sb("w2_sb", [P, 2, DH])
        w2k2 = sb("w2k2", [P, 2, DH])
        lam_in = sb("lam_in", [P, 4, DH])
        lam = sb("lam", [P, 4])
        sub_g = sb("sub_g", [P, DIFF_V])
        half_pow = sb("half_pow", [P, 4])
        stats = sb("stats", [P, TOKS, 2, 6])
        mean_var = sb("mean_var", [P, TOKS, 2])
        rstd = sb("rstd", [P, TOKS, 2])
        rope_a = sb("rope_a", [P, 16, ROT])
        rope_b = sb("rope_b", [P, 16, ROT])
        neg_max = sb("neg_max", [P, 3, 4])
        sums = sb("sums", [P, TOKS, 2, NSA_HEADS])
        share = sb("share", [P, 2, NSA_HEADS])
        rms = sb("rms", [P, 2, 4, 4])

        late = ExitStack()
        with late:
            k_nat = sb("k_nat", [P, TOKS, D], scope=late)
            v_b = sb("v_b", [P, TOKS, D], scope=late)
            ffn = ExitStack()
            with ffn:
                ht_hi = sb("ht_hi", [P, FT, SEQ], F32R, ffn)
                ht_lo = sb("ht_lo", [P, FT, SEQ], F32R, ffn)
            dif = ExitStack()
            with dif:
                dqs = sb("dqs", [P, 2 * DIFF_HEADS, SEQ], F32R, dif)
                dks = sb("dks", [P, 2, 2 * DIFF_HEADS, SEQ], F32R, dif)
        nsa = ExitStack()
        with nsa:
            kv_a = sb("kv_a", [P, TOKS, KV_COLS], scope=nsa)
            nq = sb("nq", [P, TOKS, D], scope=nsa)
            nqs = sb("nqs", [P, NSA_HEADS, SEQ], F32R, nsa)
            nks = sb("nks", [P, 2, 2, NSA_GROUPS, SEQ], F32R, nsa)
            blk = sb("blk", [P, 2, CMP_BLOCK // 2, NSA_GROUPS * N_CMP], scope=nsa)
            w1v = sb("w1v", [P, CMP_BLOCK // 2, HID], scope=nsa)
            hid = sb("hid", [P, 2, NSA_GROUPS * N_CMP], scope=nsa)
            hid_rep = sb("hid_rep", [P, NSA_GROUPS, 8, 16], scope=nsa)
            kcb = sb("kcb", [P, NSA_GROUPS, 2, 16], scope=nsa)
            vcb = sb("vcb", [P, NSA_GROUPS, 8, DH], scope=nsa)
            cs = sb("cs", [P, TOKS, NSA_HEADS, 16], scope=nsa)
            cmax = sb("cmax", [P, TOKS, NSA_HEADS], scope=nsa)
            csum = sb("csum", [P, TOKS, NSA_HEADS], scope=nsa)
            pct = sb("pct", [P, 4, P], scope=nsa)
            gate = sb("gate", [P, TOKS, 3 * NSA_HEADS], scope=nsa)
        lam_pr = y[:, 0, 0:2 * DH].rearrange("p (a d) -> p a d", d=DH)
        squares = y[:, 1, 0:2 * P]
        sil = y[:, :, 0:512]
        h_nat = y[:, :, 512:1024]
        dq = k_nat
        nqt = y[:].rearrange("p t (k s) -> p (t k) s", s=SEQ)
        def flat(t):
            return t[:].rearrange("p a b -> p (a b)")

        beside = [v[:, a:a + 2 * DH * h].rearrange("p (h s d) -> p h s d", s=2, d=DH) for v, a, h in (
            (flat(nqs), 0, 4), (flat(nqs), 2048, 4), (flat(w1v).bitcast(F32R), 0, 16), (flat(xt_lo), 0, 16),
            (flat(dqs), 0, 16), (flat(dqs), 2048, 16), (flat(y).bitcast(F32R), 0, 16), (flat(xt_lo), 0, 16))]
        rotated = [kv_a[:, tok, KS:KS + 512].rearrange("p (m g d) -> p m g d", m=2, d=DH)[:, :, 0:2, :]
                   for tok in range(TOKS)] + [v[:, tok, :].rearrange("p (h d) -> p h d", d=DH)
                                              for v in (nq, k_nat, dq) for tok in range(TOKS)]
        turned_probs = y[:, 0, :].rearrange("p (a c) -> p a c", a=2)
        branch = [y[:, 1, 0:512], y[:, 1, 512:1024]]

        acc = ctx.enter_context(nc.psum_tensor("acc", [P, 4, 512], F32))
        trb = ctx.enter_context(nc.psum_tensor("trb", [P, 2, 512], F32))
        aux = ctx.enter_context(nc.psum_tensor("aux", [P, 2, 512], F32))
        score_bank = [acc[:, 0], acc[:, 1], aux[:, 0]]

        const_in = sem("const_in")
        squares_landed = sem("squares_landed")
        x_landed = [sem(f"x_landed{tok}") for tok in range(TOKS)]
        small_in = sem("small_in")
        norm_in = sem("norm_in")
        w1_in = sem("w1_in")
        raw_in = [sem(f"raw_in{i}") for i in range(SLOTS)]
        hi_ready = sem("hi_ready")
        lo_ready = sem("lo_ready")
        unit_used = sem("unit_used")
        tile0_full = sem("tile0_full")
        half_full = sem("half_full")
        half_ready = sem("half_ready")
        acc_free = sem("acc_free")
        silu_done = sem("silu_done")
        tr_full = sem("tr_full")
        tr_hi = sem("tr_hi")
        tr_free = [sem(f"tr_free{bank}") for bank in range(2)]
        beside_hi = sem("beside_hi")
        beside_ready = sem("beside_ready")
        k_dup = sem("k_dup")
        x_ready = sem("x_ready")
        stats_ready = sem("stats_ready")
        rstd_ready = sem("rstd_ready")
        masks_ready = sem("masks_ready")
        rope_done = sem("rope_done")
        hid_full = sem("hid_full")
        hid_ready = sem("hid_ready")
        cmp_full = sem("cmp_full")
        cmp_ready = sem("cmp_ready")
        cs_full = sem("cs_full")
        cs_shifted = sem("cs_shifted")
        cs_copied = sem("cs_copied")
        cexp_done = sem("cexp_done")
        gate_exp = sem("gate_exp")
        score_full = sem("score_full")
        max_ready = sem("max_ready")
        exp_done = sem("exp_done")
        turn_full = sem("turn_full")
        cmp_out = sem("cmp_out")
        turn_read = sem("turn_read")
        turn_mixed = sem("turn_mixed")
        lam_sum = sem("lam_sum")
        lam_exp = sem("lam_exp")
        dve_step = sem("dve_step")
        pool_step = sem("pool_step")
        rms_ready = sem("rms_ready")
        rms_pow = sem("rms_pow")
        out_done = sem("out_done")

        ident = id_r[:, 0:P].bitcast(F32)
        swap = id_r[:, DH:DH + P]
        cos2 = cst[:, C_COS:C_COS + 32].rearrange("p (t r) -> p t r", t=TOKS)
        sin2 = cst[:, C_SIN:C_SIN + 32].rearrange("p (t r) -> p t r", t=TOKS)
        cmp_mask = cst[:, C_CMP:C_CMP + 32].rearrange("p (t c) -> p t c", t=TOKS)

        def weights(buf, n):
            k, c = unit_shape(n)
            return buf[:, n % SLOTS, 0:k * c].rearrange("p (k c) -> p k c", k=k)

        def rows(w, r0, k, c0, c):
            return w[r0:r0 + k * P, c0:c0 + c].rearrange("(k p) c -> p k c", p=P)

        def bc(ap, *shape):
            return ap.broadcast_to(list(shape))

        def filled(eng, stage, g, tok):
            if tok == 0:
                eng.wait_ge(tile0_full, TILE0_FILLS[stage, g])
            else:
                eng.wait_ge(unit_used, units_through(stage, g))

        block = ctx.enter_context(nc.Block())

        @block.sync
        def _(sp):
            def load_x(tok):
                sp.dma_start(x[:, tok, :], x_in[tok * P:(tok + 1) * P, :]).then_inc(x_landed[tok], 16)

            def load(n, src, freed=None):
                if freed is not None:
                    sp.wait_ge(lo_ready, freed)
                elif n >= SLOTS:
                    sp.wait_ge(lo_ready, n - SLOTS + 1)
                sp.dma_start(weights(raw, n), src).then_inc(raw_in[n % SLOTS], 16)

            def load_ffn(stage):
                i = int(stage[3])
                n0 = UNIT_OF[stage]
                wg, wu, wd = w_gates[i], w_ups[i], w_downs[i]

                def group(g, peeled):
                    for j, (w, half) in enumerate([(wg, 0), (wg, 1), (wu, 0), (wu, 1)]):
                        src = w[half * 512:(half + 1) * 512, bass.ds(g * 512, 512)].rearrange(
                            "(k p) c -> p k c", p=P)
                        if stage == "ffn0" and peeled and j == 3:
                            load_x(1)
                        load(n0 + j, src, None if peeled else g * 4 + (n0 + j - SLOTS + 1))
                        if stage == "ffn0" and peeled and j == 0:
                            sp.dma_start(squares, squares_in).then_inc(squares_landed, 16)
                            load_x(0)

                group(0, True)
                with sp.Fori(1, G_FULL) as g:
                    group(g, False)
                load(n0 + 4 * G_FULL, rows(wg, 0, KT, 512 * G_FULL, HALF))
                load(n0 + 4 * G_FULL + 1, rows(wu, 0, KT, 512 * G_FULL, HALF))
                for j in range(UNITS_DOWN):
                    load(n0 + UNITS_GU + j, rows(wd, 2 * P * j, 2, 0, D))

            def load_columns(stage, w, chunks):
                n = UNIT_OF[stage]
                for c0, c in chunks:
                    for half in range(2):
                        load(n, rows(w, half * 512, 4, c0, c))
                        n += 1

            def load_rows(stage, w):
                for j in range(KT // 2):
                    load(UNIT_OF[stage] + j, rows(w, 2 * P * j, 2, 0, D))

            load_ffn("ffn0")
            load_columns("nsa_in", w_in, [(D, 512), (D + 512, KV_COLS - 512), (0, 512), (512, 512)])
            load_rows("nsa_out", w_out_a)
            load_ffn("ffn1")
            load_columns("kv", w_kv, [(c, 512) for c in range(0, 2 * D, 512)])
            load_ffn("ffn2")
            load_columns("diff_q", w_q, [(0, 512), (512, 512)])
            load_rows("diff_out", w_out_b)
            load_ffn("ffn3")
            sp.wait_ge(x_ready, 2 * len(NORM_OF) - 1)
            sp.dma_start(out[0:P, :], x[:, 0, :]).then_inc(out_done, 16)
            for half in range(2):
                sp.wait_ge(half_ready, half + 1)
                cols = slice(half * 512, (half + 1) * 512)
                sp.dma_start(out[P:2 * P, cols], x[:, 1, cols]).then_inc(out_done, 16)
            sp.wait_ge(out_done, 16 * 3)

        @block.gpsimd
        def _(pool):
            step = [0]

            def link(ins):
                step[0] += 1
                ins.then_inc(pool_step, 1)
                pool.wait_ge(pool_step, step[0])

            pool.wait_ge(raw_in[SLOTS - 1], 16)
            pool.dma_start(cst[:], const).then_inc(const_in, 16)
            for dst, src in ((pos_sb[:], cmp_pos.rearrange("b p l -> p b l")), (b1_sb[:], cmp_b1),
                             (w2_sb[:], cmp_w2.rearrange("b h d -> h b d")),
                             (lam_in[:], lambdas.partition_broadcast(P)), (sub_g[:], subln_g.partition_broadcast(P))):
                pool.dma_start(dst, src).then_inc(small_in, 16)

            def load_norm(k):
                if k:
                    pool.wait_ge(x_ready, 2 * k)
                if k in (1, 4):
                    kind, jobs = ("nsa", NSA_JOBS) if k == 1 else ("diff", DIFF_JOBS)
                    pool.wait_ge(tr_full, TURN_OF["p", kind, len(jobs) - 1] + 1)
                for j, w in enumerate((ln_g, ln_b)):
                    pool.dma_start(norm_gb[:, j, :], w[k].partition_broadcast(P)).then_inc(norm_in, 16)

            def inverse_root(k):
                for tok in range(TOKS):
                    pool.wait_ge(stats_ready, 2 * k + tok + 1)
                    link(pool.tensor_scalar(rstd[:, tok, 0:1], mean_var[:, tok, 1:2], EPS, None, ALU.add))
                    pool.tensor_tensor(rstd[:, tok, 1:2], rstd[:, tok, 0:1], half_pow[:, 0:1],
                                       ALU.pow).then_inc(rstd_ready, 1)

            def rotate(v, tok, heads):
                a, b = rope_a[:, 0:heads], rope_b[:, 0:heads]
                r, h = v[:, :, 0:ROT], ROT // 2
                link(pool.tensor_tensor(a, r, bc(cos2[:, tok:tok + 1, :], P, heads, ROT), ALU.mult))
                link(pool.tensor_tensor(b, r, bc(sin2[:, tok:tok + 1, :], P, heads, ROT), ALU.mult))
                link(pool.tensor_tensor(v[:, :, 0:h], a[:, :, 0:h], b[:, :, h:ROT], ALU.subtract))
                return pool.tensor_tensor(v[:, :, h:ROT], b[:, :, 0:h], a[:, :, h:ROT], ALU.add)

            def split_units(n0, n1):
                for n in range(n0, n1):
                    slot, (k, c) = n % SLOTS, unit_shape(n)
                    pool.wait_ge(raw_in[slot], 16 * (n // SLOTS + 1))
                    pool.wait_ge(unit_used, n - SLOTS + 1)
                    hi = w_hi[:, slot, 0:k * c]
                    pool.tensor_copy(hi, raw[:, slot, 0:k * c]).then_inc(hi_ready, 1)
                    pool.wait_ge(hi_ready, n + 1)
                    pool.tensor_tensor(w_lo[:, slot, 0:k * c], raw[:, slot, 0:k * c], hi.bitcast(F32),
                                       ALU.subtract).then_inc(lo_ready, 1)

            def heads_of(v, tok, c0, heads):
                return v[:, tok, c0:c0 + heads * DH].rearrange("p (h d) -> p h d", d=DH)

            link(pool.memset(half_pow[:], -0.5))
            load_norm(0)
            inverse_root(0)
            pool.wait_ge(const_in, 16)
            pool.wait_ge(x_ready, 2)
            pool.dma_start(w1k, cmp_w1[0].rearrange("(l p) h -> p l h", p=P)).then_inc(w1_in, 16)
            pool.dma_start(w1v[:], cmp_w1[1].rearrange("(l p) h -> p l h", p=P)).then_inc(w1_in, 16)
            for tok in range(TOKS):
                pool.wait_ge(acc_free, FILL_OF["nsa_in", 0, tok] + 1)
                for j, c in enumerate((KC, VC)):
                    dst = y[:, tok, j * 256:(j + 1) * 256].rearrange("p (g r d) -> p g r d", g=2, r=2)
                    for r in range(2):
                        ins = pool.tensor_copy(dst[:, :, r, :], heads_of(kv_a, tok, c, 2))
                ins.then_inc(k_dup, 1)
                link(rotate(heads_of(kv_a, tok, KS, 2), tok, 2))
                ins = rotate(heads_of(kv_a, tok, KW, 2), tok, 2)
                ins.then_inc(rope_done, 1)
                pool.wait_ge(rope_done, tok + 1)
            for tok in range(TOKS):
                pool.wait_ge(acc_free, FILL_OF["nsa_in", 1, tok] + 1)
                pool.wait_ge(tr_full, TURN_OF["q", tok, 1] + 1)
                if tok:
                    pool.wait_ge(rope_done, 3)
                rotate(heads_of(nq, tok, 0, 16), tok, 16).then_inc(rope_done, 1)
            split_units(UNIT_OF["nsa_out"], UNIT_OF["nsa_out"] + 4)
            load_norm(1)
            inverse_root(1)
            load_norm(2)
            inverse_root(2)
            for tok in range(TOKS):
                pool.wait_ge(acc_free, FILL_OF["kv", 0, tok] + 1)
                if tok:
                    pool.wait_ge(rope_done, 5)
                rotate(heads_of(k_nat, tok, 0, 16), tok, 16).then_inc(rope_done, 1)
            load_norm(3)
            inverse_root(3)
            for tok in range(TOKS):
                pool.wait_ge(acc_free, FILL_OF["diff_q", 0, tok] + 1)
                if tok:
                    pool.wait_ge(rope_done, 7)
                rotate(heads_of(dq, tok, 0, 16), tok, 16).then_inc(rope_done, 1)
            split_units(UNIT_OF["diff_out"], UNIT_OF["diff_out"] + 2)
            for k in range(len(DIFF_TURNS)):
                pool.wait_ge(rms_ready, k + 1)
                pool.tensor_tensor(rms[:, 1, k, :], rms[:, 0, k, :], half_pow[:], ALU.pow).then_inc(rms_pow, 1)
                if k == 1:
                    split_units(UNIT_OF["diff_out"] + 2, UNIT_OF["diff_out"] + 3)
                if k == len(DIFF_TURNS) - 2:
                    load_norm(4)
            inverse_root(4)
            load_norm(5)
            inverse_root(5)

        @block.scalar
        def _(act):
            def split_unit(n, slot, in_count, used):
                act.wait_ge(raw_in[slot], in_count)
                if used is not None:
                    act.wait_ge(unit_used, used)
                k, c = unit_shape(n)
                act.activation(w_hi[:, slot, 0:k * c], raw[:, slot, 0:k * c], ACT.Copy).then_inc(hi_ready, 1)

            def split_units(n0, n1):
                for n in range(n0, min(n1, N_UNITS)):
                    split_unit(n, n % SLOTS, 16 * (n // SLOTS + 1), n - SLOTS + 1 if n >= SLOTS else None)

            def high_part(name, dst):
                act.wait_ge(tr_full, TURN_OF[name] + 1)
                act.activation(dst, trb[:, TURN_OF[name] % 2].rearrange("p (k c) -> p k c", c=P), ACT.Copy).then_inc(
                    tr_hi, 1)

            def copy_turned(name, dst):
                t = TURN_OF[name]
                act.wait_ge(tr_full, t + 1)
                act.activation(dst, trb[:, t % 2].rearrange("p (k c) -> p k c", c=P), ACT.Copy).then_inc(
                    tr_free[t % 2], 1)

            def copy_heads(name, tok, part, dst):
                copy_turned((*name, tok, part), dst[:, 4 * part:4 * part + 4, tok * P:(tok + 1) * P])

            def split_beside(k):
                act.wait_ge(rope_done, k + 1)
                dst, src = beside[k][:, :, 0, :], rotated[k]
                if len(src.shape) == 4:
                    for m in range(2):
                        ins = act.activation(dst[:, 2 * m:2 * m + 2], src[:, m], ACT.Copy)
                else:
                    ins = act.activation(dst, src, ACT.Copy)
                ins.then_inc(beside_hi, 1)

            def x_high(of, tok, parts=range(2)):
                for part in parts:
                    high_part(("x", of, tok, part), xt_hi[:, 4 * part:4 * part + 4, tok * P:(tok + 1) * P])

            def ffn_stage(stage, pending):
                n0, e0, t0 = UNIT_OF[stage], FILL_OF[stage, 0, 0], TURN_OF["h", stage, 0, 0]
                pending()

                def silu(tok, c):
                    act.activation(sil[:, tok, 0:c], acc[:, 2 * tok, 0:c], ACT.Silu).then_inc(silu_done, 1)

                def h_high(t, bank, g, tok, k):
                    act.wait_ge(tr_full, t + 1)
                    act.activation(ht_hi[:, bass.ds(4 * g, k), tok * P:(tok + 1) * P],
                                   trb[:, bank, 0:k * P].rearrange("p (k c) -> p k c", c=P),
                                   ACT.Copy).then_inc(tr_hi, 1)

                with act.Fori(0, G_FULL - 1) as g:
                    act.wait_ge(tile0_full, g + TILE0_FILLS[stage, 0])
                    silu(0, 512)
                    for j in range(4):
                        n = n0 + 4 + j
                        if j == 3:
                            act.wait_ge(unit_used, 4 * g + (n0 + 4))
                            silu(1, 512)
                        split_unit(n, n % SLOTS, g * 16 + 16 * (n // SLOTS + 1), g * 4 + (n - SLOTS + 1))
                    h_high(2 * g + t0, t0 % 2, g, 0, 4)
                    h_high(2 * g + (t0 + 1), (t0 + 1) % 2, g, 1, 4)
                for g in (G_FULL - 1, G_FULL):
                    c = 512 if g < G_FULL else HALF
                    filled(act, stage, g, 0)
                    silu(0, c)
                    n = n0 + 4 * (g + 1)
                    split_units(n, n + c // 128 - 1)
                    if g == G_FULL:
                        h_high(t0 + 2 * g, t0 % 2, g, 0, c // P)
                    filled(act, stage, g, 1)
                    silu(1, c)
                    split_units(n + c // 128 - 1, n + c // 128)
                    for tok in range(TOKS):
                        if tok or g < G_FULL:
                            h_high(t0 + 2 * g + tok, (t0 + tok) % 2, g, tok, c // P)
                split_units(n0 + UNITS_GU + 4, n0 + UNITS_FFN + 2)
                if stage != "ffn3":
                    x_high(stage, 0)
                split_units(n0 + UNITS_FFN + 2, n0 + UNITS_FFN + 4)

            def exps(kind, jobs, i, base):
                _, tok, heads, _ = jobs[i]
                width = P * (tok + 1)
                act.wait_ge(max_ready, base + i + 1)
                if i >= 3:
                    act.wait_ge(tr_full, TURN_OF["p", kind, i - 3] + 1)
                k = 0
                for h in heads:
                    for m in range(2):
                        ins = act.activation(probs[:, i % 3, k * width:(k + 1) * width],
                                             score_bank[i % 3][:, k * width:(k + 1) * width], ACT.Exp,
                                             bias=neg_max[:, i % 3, k:k + 1],
                                             accum_out=sums[:, tok, m, h:h + 1])
                        k += 1
                ins.then_inc(exp_done, 1)

            def copy_p(kind, j):
                copy_turned(("p", kind, j), turned_probs[:, j % 2].rearrange("p (k c) -> p k c", c=P))

            split_units(0, 1)
            x_high("start", 0)
            split_units(1, 4)
            ffn_stage("ffn0", lambda: x_high("start", 1))

            n0 = UNIT_OF["nsa_in"]
            x_high("ffn0", 1)
            split_units(n0 + 4, n0 + 8)
            for k in range(2):
                split_beside(k)
            act.wait_ge(small_in, 80)
            for b in range(2):
                act.wait_ge(hid_full, b + 1)
                act.activation(hid[:, b, :], aux[:, b, 0:2 * N_CMP], ACT.Gelu_apprx_tanh,
                               bias=b1_sb[:, b:b + 1]).then_inc(hid_ready, 1)
            for j in range(2):
                copy_turned(("kr", j), nks[:, 0, j].rearrange("p g (t c) -> p (g t) c", c=P))
            split_beside(2)
            for j in range(2):
                copy_turned(("ks", j), nks[:, 1, j].rearrange("p g (t c) -> p (g t) c", c=P))
            act.wait_ge(acc_free, FILL_OF["nsa_in", 0, 1] + 1)
            for tok in range(TOKS):
                ins = act.activation(gate[:, tok, :], kv_a[:, tok, GT:GT + 48], ACT.Exp, scale=-1.0)
            ins.then_inc(gate_exp, 1)
            for part in range(4):
                copy_heads(("qr", "nsa"), 0, part, nqs)

            def compressed_exp(tok):
                act.wait_ge(cs_shifted, tok + 1)
                act.activation(cs[:, tok], cs[:, tok], ACT.Exp).then_inc(cexp_done, 1)

            compressed_exp(0)
            for i, sc, tr, pv in job_steps(NSA_JOBS):
                if tr:
                    copy_p("nsa", i - 2)
                for part in LATE_PARTS["nsa"].get(i, ()):
                    copy_heads(("qr", "nsa"), 1, part, nqs)
                if sc:
                    exps("nsa", NSA_JOBS, i, 0)
                if i == 1:
                    compressed_exp(1)
                if i == 3:
                    split_beside(3)
                if i in TILE0_DONE["nsa"]:
                    x_high("nsa_o", 0, [TILE0_DONE["nsa"].index(i)])
            x_high("nsa_o", 1)
            n0 = UNIT_OF["nsa_out"]
            split_units(n0 + 4, n0 + 6)
            x_high("nsa_out", 0)
            split_units(n0 + 6, n0 + 8)
            ffn_stage("ffn1", lambda: x_high("nsa_out", 1))

            n0 = UNIT_OF["kv"]
            x_high("ffn1", 1)
            split_units(n0 + 4, n0 + 12)
            ffn_stage("ffn2", lambda: None)

            n0 = UNIT_OF["diff_q"]
            x_high("ffn2", 1)
            for k in range(4, 6):
                split_beside(k)
            act.wait_ge(lam_sum, 1)
            act.activation(lam[:, 0:2], lam[:, 0:2], ACT.Exp).then_inc(lam_exp, 1)
            for part in (0, 2):
                copy_heads(("kr", "diff"), 0, part, dks[:, 0])
            split_beside(6)
            for part in (0, 2):
                copy_heads(("kr", "diff"), 1, part, dks[:, 0])
            for tok in range(TOKS):
                for part in (0, 2):
                    copy_heads(("ks", "diff"), tok, part, dks[:, 1])
            for part in (0, 2):
                copy_heads(("qr", "diff"), 0, part, dqs)
            split_beside(7)
            for i, sc, tr, pv in job_steps(DIFF_JOBS):
                if tr:
                    copy_p("diff", i - 2)
                for part in LATE_PARTS["diff"].get(i, ()):
                    copy_heads(("qr", "diff"), 1, part, dqs)
                if sc:
                    exps("diff", DIFF_JOBS, i, len(NSA_JOBS))
                if i in TILE0_DONE["diff"]:
                    x_high("diff_o", 0, [TILE0_DONE["diff"].index(i)])
            act.wait_ge(lo_ready, n0 + 7)
            split_units(n0 + 7, n0 + 8)
            x_high("diff_o", 1)
            n0 = UNIT_OF["diff_out"]
            split_units(n0 + 4, n0 + 6)
            x_high("diff_out", 0)
            split_units(n0 + 6, n0 + 8)
            ffn_stage("ffn3", lambda: x_high("diff_out", 1))

        @block.vector
        def _(dve):
            step = [0]

            def link(ins):
                step[0] += 1
                ins.then_inc(dve_step, 1)
                dve.wait_ge(dve_step, step[0])

            def split_unit(n, slot, ready):
                dve.wait_ge(hi_ready, ready)
                k, c = unit_shape(n)
                dve.tensor_tensor(w_lo[:, slot, 0:k * c], raw[:, slot, 0:k * c],
                                  w_hi[:, slot, 0:k * c].bitcast(F32), ALU.subtract).then_inc(lo_ready, 1)

            def split_units(n0, n1):
                for n in range(n0, min(n1, N_UNITS)):
                    split_unit(n, n % SLOTS, n + 1)

            def low_part(name, hi, lo):
                t = TURN_OF[name]
                dve.wait_ge(tr_hi, SPLIT_OF[name] + 1)
                dve.tensor_tensor(lo, trb[:, t % 2].rearrange("p (k c) -> p k c", c=P), hi.bitcast(F32),
                                  ALU.subtract).then_inc(tr_free[t % 2], 1)

            def x_low(of, tok, parts=range(2)):
                for part in parts:
                    at = slice(4 * part, 4 * part + 4), slice(tok * P, (tok + 1) * P)
                    low_part(("x", of, tok, part), xt_hi[:, at[0], at[1]], xt_lo[:, at[0], at[1]])

            def split_beside(k):
                dve.wait_ge(beside_hi, k + 1)
                hi, lo, src = beside[k][:, :, 0, :], beside[k][:, :, 1, :], rotated[k]
                if len(src.shape) == 4:
                    for m in range(2):
                        ins = dve.tensor_tensor(lo[:, 2 * m:2 * m + 2], src[:, m],
                                                hi[:, 2 * m:2 * m + 2].bitcast(F32), ALU.subtract)
                else:
                    ins = dve.tensor_tensor(lo, src, hi.bitcast(F32), ALU.subtract)
                ins.then_inc(beside_ready, 1)

            def copy_turned(name, dst, k=4):
                t = TURN_OF[name]
                dve.wait_ge(tr_full, t + 1)
                dve.tensor_copy(dst, trb[:, t % 2].rearrange("p (k c) -> p k c", k=k)).then_inc(tr_free[t % 2], 1)

            def norm(stage, tok):
                k = NORM_OF[stage]
                group = G_FULL + 1 if stage.startswith("ffn") else 0
                e = FILL_OF[stage, group, tok]
                filled(dve, stage, group, tok)
                dve.scalar_tensor_tensor(y[:, tok, :], x[:, tok, :], ALPHA,
                                         acc[:, 2 * tok:2 * tok + 2].rearrange("p a c -> p (a c)"),
                                         ALU.mult, ALU.add).then_inc(acc_free, 1)
                dve.wait_ge(acc_free, e + 1)
                for half in range(2):
                    ins = dve.bn_stats(stats[:, tok, half, :], y[:, tok, half * 512:(half + 1) * 512])
                link(ins)
                dve.bn_aggr(mean_var[:, tok, :], stats[:, tok].rearrange("p a b -> p (a b)")).then_inc(stats_ready, 1)
                dve.wait_ge(stats_ready, 2 * k + tok + 1)
                dve.wait_ge(norm_in, 32 * (k + 1))
                link(dve.scalar_tensor_tensor(y[:, tok, :], y[:, tok, :], mean_var[:, tok, 0:1], norm_gb[:, 0, :],
                                              ALU.subtract, ALU.mult))
                dve.wait_ge(rstd_ready, 2 * k + tok + 1)
                dve.scalar_tensor_tensor(x[:, tok, :], y[:, tok, :], rstd[:, tok, 1:2], norm_gb[:, 1, :],
                                         ALU.mult, ALU.add).then_inc(x_ready, 1)

            def ffn_stage(stage, pending):
                n0, e0, s0 = UNIT_OF[stage], FILL_OF[stage, 0, 0], SPLIT_OF["h", stage, 0, 0]
                t0 = TURN_OF["h", stage, 0, 0]
                i0 = 2 * (G_FULL + 1) * int(stage[3])
                pending()

                def gated(i, tok, c):
                    dve.wait_ge(silu_done, i + 1)
                    dve.scalar_tensor_tensor(h_nat[:, tok, 0:c], sil[:, tok, 0:c], 0.5, acc[:, 2 * tok + 1, 0:c],
                                             ALU.mult, ALU.mult).then_inc(acc_free, 1)

                def h_low(s, bank, g, tok, k):
                    dve.wait_ge(tr_hi, s + 1)
                    dve.tensor_tensor(ht_lo[:, bass.ds(4 * g, k), tok * P:(tok + 1) * P],
                                      trb[:, bank, 0:k * P].rearrange("p (k c) -> p k c", c=P),
                                      ht_hi[:, bass.ds(4 * g, k), tok * P:(tok + 1) * P].bitcast(F32),
                                      ALU.subtract).then_inc(tr_free[bank], 1)

                with dve.Fori(0, G_FULL - 1) as g:
                    gated(2 * g + i0, 0, 512)
                    for j in range(4):
                        n = n0 + 4 + j
                        if j == 3:
                            gated(2 * g + (i0 + 1), 1, 512)
                        split_unit(n, n % SLOTS, 4 * g + (n + 1))
                    h_low(2 * g + s0, t0 % 2, g, 0, 4)
                    h_low(2 * g + (s0 + 1), (t0 + 1) % 2, g, 1, 4)
                for g in (G_FULL - 1, G_FULL):
                    c = 512 if g < G_FULL else HALF
                    gated(i0 + 2 * g, 0, c)
                    n = n0 + 4 * (g + 1)
                    split_units(n, n + c // 128 - 1)
                    if g == G_FULL:
                        h_low(s0 + 2 * g, t0 % 2, g, 0, c // P)
                    gated(i0 + 2 * g + 1, 1, c)
                    split_units(n + c // 128 - 1, n + c // 128)
                    for tok in range(TOKS):
                        if tok or g < G_FULL:
                            h_low(s0 + 2 * g + tok, (t0 + tok) % 2, g, tok, c // P)
                split_units(n0 + UNITS_GU + 4, n0 + UNITS_FFN)
                norm(stage, 0)
                split_units(n0 + UNITS_FFN, n0 + UNITS_FFN + 2)
                if stage != "ffn3":
                    x_low(stage, 0)
                split_units(n0 + UNITS_FFN + 2, n0 + UNITS_FFN + 3)
                if stage == "ffn3":
                    last_norm()
                else:
                    norm(stage, 1)
                split_units(n0 + UNITS_FFN + 3, n0 + UNITS_FFN + 4)

            def last_norm():
                tok, k, e = 1, NORM_OF["ffn3"], FILL_OF["ffn3", G_FULL + 1, 1]
                halves = [slice(half * 512, (half + 1) * 512) for half in range(2)]
                for half, cols in enumerate(halves):
                    if half == 0:
                        dve.wait_ge(half_full, 1)
                    else:
                        filled(dve, "ffn3", G_FULL + 1, tok)
                    ins = dve.scalar_tensor_tensor(y[:, tok, cols], x[:, tok, cols], ALPHA, acc[:, 2 * tok + half],
                                                   ALU.mult, ALU.add)
                    link(ins)
                    ins = dve.bn_stats(stats[:, tok, half, :], y[:, tok, cols])
                link(ins)
                dve.bn_aggr(mean_var[:, tok, :], stats[:, tok].rearrange("p a b -> p (a b)")).then_inc(stats_ready, 1)
                dve.wait_ge(stats_ready, 2 * k + tok + 1)
                dve.wait_ge(norm_in, 32 * (k + 1))
                for cols in halves:
                    ins = dve.scalar_tensor_tensor(y[:, tok, cols], y[:, tok, cols], mean_var[:, tok, 0:1],
                                                   norm_gb[:, 0, cols], ALU.subtract, ALU.mult)
                link(ins)
                dve.wait_ge(rstd_ready, 2 * k + tok + 1)
                for cols in halves:
                    dve.scalar_tensor_tensor(x[:, tok, cols], y[:, tok, cols], rstd[:, tok, 1:2], norm_gb[:, 1, cols],
                                             ALU.mult, ALU.add).then_inc(half_ready, 1)

            def out_stage(stage):
                n = UNIT_OF[stage] + 4
                norm(stage, 0)
                split_units(n, n + 2)
                x_low(stage, 0)
                split_units(n + 2, n + 3)
                norm(stage, 1)
                split_units(n + 3, n + 4)

            def maxima(jobs, i, base):
                _, tok, heads, _ = jobs[i]
                maps = 2 * len(heads)
                dve.wait_ge(score_full, base + i + 1)
                dve.tensor_reduce(neg_max[:, i % 3, 0:maps],
                                  score_bank[i % 3].rearrange("p (m k) -> p m k", m=maps), AX.X, ALU.max,
                                  negate=True).then_inc(max_ready, 1)

            dve.wait_ge(squares_landed, 16)
            dve.tensor_copy(id_r[:, 0:P], squares[:, 0:P])
            dve.tensor_copy(id_r[:, P:P + DH], squares[:, 0:DH]).then_inc(masks_ready, 1)
            dve.tensor_copy(id_bf[:], squares[:, 0:P]).then_inc(acc_free, 1)
            dve.tensor_copy(diag_bf[:], squares[:, P:2 * P]).then_inc(masks_ready, 1)
            split_units(0, 1)
            x_low("start", 0)
            split_units(1, 4)
            ffn_stage("ffn0", lambda: x_low("start", 1))

            n0 = UNIT_OF["nsa_in"]
            x_low("ffn0", 1)
            dve.wait_ge(small_in, 80)
            dve.wait_ge(const_in, 16)
            dve.tensor_copy(w2k2[:, 0, :], w2_sb[:, 0, :])
            dve.tensor_copy(w2k2[:, 1, :], w2_sb[:, 0, :])
            dve.memset(hid_rep[:], 0.0)
            link(dve.memset(kcb[:], 0.0))
            for tok in range(TOKS):
                filled(dve, "nsa_in", 0, tok)
                dve.tensor_copy(kv_a[:, tok, :], acc[:, 2 * tok:2 * tok + 2].rearrange("p a c -> p (a c)")[
                    :, 0:KV_COLS]).then_inc(acc_free, 1)
                split_units(n0 + 4 + 2 * tok, n0 + 6 + 2 * tok)
            for k in range(2):
                split_beside(k)
            for b in range(2):
                t = TURN_OF["kc", b]
                dve.wait_ge(tr_full, t + 1)
                for g in range(NSA_GROUPS):
                    for r in range(2):
                        rr = slice(r * DH, (r + 1) * DH)
                        lanes = trb[rr, t % 2, g * SEQ:(g + 1) * SEQ].rearrange("p (c l r) -> p c l r", l=8, r=2)
                        for a in range(2):
                            ins = dve.tensor_tensor(
                                blk[rr, b, 8 * a:8 * a + 8, g * N_CMP:(g + 1) * N_CMP],
                                lanes[:, a:a + N_CMP, :, r].rearrange("p c l -> p l c"),
                                bc(pos_sb[rr, b, 8 * a:8 * a + 8].unsqueeze(2), DH, 8, N_CMP), ALU.add)
                ins.then_inc(tr_free[t % 2], 1)

            def queries_out(tok):
                filled(dve, "nsa_in", 1, tok)
                dve.tensor_scalar(nq[:, tok, :], acc[:, 2 * tok:2 * tok + 2].rearrange("p a c -> p (a c)"),
                                  DH ** -0.5, None, ALU.mult).then_inc(acc_free, 1)

            def copy_queries(tok):
                for part in range(2):
                    copy_turned(("q", tok, part), nqt[:, 4 * part:4 * part + 4, tok * P:(tok + 1) * P])

            queries_out(0)
            copy_queries(0)
            dve.wait_ge(hid_ready, 2)
            for g in range(NSA_GROUPS):
                ins = dve.tensor_copy(hid_rep[:, g, :, 0:N_CMP],
                                      bc(hid[:, 1:2, g * N_CMP:(g + 1) * N_CMP], P, 8, N_CMP))
            ins.then_inc(cmp_ready, 1)
            dve.wait_ge(cmp_full, 1)
            for r in range(2):
                rr = slice(r * DH, (r + 1) * DH)
                ins = dve.tensor_copy(kcb[rr, :, r, 0:N_CMP],
                                      aux[rr, 0, 64:64 + 2 * N_CMP].rearrange("p (g c) -> p g c", g=2))
            ins.then_inc(cmp_ready, 1)
            dve.wait_ge(cmp_full, 2)
            heads8 = cst[:, C_HEAD:C_HEAD + 8].unsqueeze(2)
            for g in range(NSA_GROUPS):
                ins = dve.tensor_tensor(vcb[:, g], bc(aux[:, 1, 64 + g * DH:64 + (g + 1) * DH].unsqueeze(1), P, 8, DH),
                                        bc(heads8, P, 8, DH), ALU.mult)
            ins.then_inc(cmp_ready, 1)
            split_beside(2)
            dve.wait_ge(gate_exp, 1)
            gates = gate[:].rearrange("p t c -> p (t c)")
            link(dve.tensor_scalar(gates, gates, 1.0, None, ALU.add))
            dve.reciprocal(gates, gates)
            queries_out(1)

            def compressed_shift(tok):
                dve.wait_ge(cs_full, tok + 1)
                dve.tensor_tensor(cs[:, tok], aux[:, tok, 0:256].rearrange("p (h c) -> p h c", c=16),
                                  bc(cmp_mask[:, tok:tok + 1, :], P, NSA_HEADS, 16), ALU.add).then_inc(cs_copied, 1)
                dve.wait_ge(cs_copied, tok + 1)
                link(dve.tensor_reduce(cmax[:, tok, :], cs[:, tok], AX.X, ALU.max))
                dve.tensor_tensor(cs[:, tok], cs[:, tok], bc(cmax[:, tok, :].unsqueeze(2), P, NSA_HEADS, 16),
                                  ALU.subtract).then_inc(cs_shifted, 1)

            def compressed_share(tok):
                dve.wait_ge(cexp_done, tok + 1)
                link(dve.tensor_reduce(csum[:, tok, :], cs[:, tok], AX.X, ALU.add))
                link(dve.reciprocal(csum[:, tok, :], csum[:, tok, :]))
                link(dve.scalar_tensor_tensor(csum[:, tok, :], csum[:, tok, :], cst[:, C_ANY + tok:C_ANY + tok + 1],
                                              gate[:, tok, 0:NSA_HEADS], ALU.mult, ALU.mult))

            def nsa_mix(turn):
                tok, g = NSA_TURNS[turn]
                h0 = g * 8
                heads = slice(h0, h0 + 8)
                dve.wait_ge(exp_done, jobs_through(NSA_JOBS, turn))
                link(dve.reciprocal(share[:, :, 0:8], sums[:, tok, :, heads]))
                link(dve.tensor_tensor(share[:, :, 0:8], share[:, :, 0:8],
                                       gate[:, tok, NSA_HEADS:].rearrange("p (m h) -> p m h", m=2)[:, :, heads],
                                       ALU.mult))
                o = nq[:, tok, h0 * DH:(h0 + 8) * DH].rearrange("p (h d) -> p h d", d=DH)
                dst = [o] + [b.rearrange("p (h d) -> p h d", d=DH) for b in branch]
                parts = [(aux[:, 1], csum[:, tok, heads]), (acc[:, 2], share[:, 0, 0:8]), (acc[:, 3], share[:, 1, 0:8])]
                for j, (to, (bank, f)) in enumerate(zip(dst, parts)):
                    if j == 0:
                        dve.wait_ge(cmp_out, turn + 1)
                    if j == 1:
                        dve.wait_ge(turn_full, turn + 1)
                    ins = dve.tensor_tensor(to, bank.rearrange("p (h d) -> p h d", d=DH),
                                            bc(f.unsqueeze(2), P, 8, DH), ALU.mult)
                ins.then_inc(turn_read, 1)
                dve.wait_ge(turn_read, turn + 1)
                link(dve.tensor_tensor(o, o, dst[1], ALU.add))
                dve.tensor_tensor(o, o, dst[2], ALU.add).then_inc(turn_mixed, 1)

            compressed_shift(0)
            for i, sc, tr, pv in job_steps(NSA_JOBS):
                if sc:
                    maxima(NSA_JOBS, i, 0)
                if i == 0:
                    copy_queries(1)
                if i == 1:
                    compressed_shift(1)
                if i == 3:
                    copy_turned(("pc",), pct[:])
                    split_beside(3)
                if i in (4, 5):
                    compressed_share(i - 4)
                if pv >= 0 and NSA_JOBS[pv][3]:
                    nsa_mix(NSA_JOBS[pv][0])
                if i in TILE0_DONE["nsa"]:
                    x_low("nsa_o", 0, [TILE0_DONE["nsa"].index(i)])
            x_low("nsa_o", 1)
            out_stage("nsa_out")
            ffn_stage("ffn1", lambda: x_low("nsa_out", 1))

            n0 = UNIT_OF["kv"]
            x_low("ffn1", 1)
            for tok in range(TOKS):
                filled(dve, "kv", 0, tok)
                dve.tensor_copy(k_nat[:, tok, :], acc[:, 2 * tok:2 * tok + 2].rearrange("p a c -> p (a c)")).then_inc(
                    acc_free, 1)
                split_units(n0 + 4 + 2 * tok, n0 + 6 + 2 * tok)
            for tok in range(TOKS):
                filled(dve, "kv", 1, tok)
                dve.tensor_copy(v_b[:, tok, :], acc[:, 2 * tok:2 * tok + 2].rearrange("p a c -> p (a c)")).then_inc(
                    acc_free, 1)
                split_units(n0 + 8 + 2 * tok, n0 + 10 + 2 * tok)
            ffn_stage("ffn2", lambda: None)

            n0 = UNIT_OF["diff_q"]
            x_low("ffn2", 1)
            link(dve.tensor_tensor(lam_pr, lam_in[:, 0:4:2, :], lam_in[:, 1:4:2, :], ALU.mult))
            dve.tensor_reduce(lam[:, 0:2], lam_pr, AX.X, ALU.add).then_inc(lam_sum, 1)
            for k in range(4, 6):
                split_beside(k)

            def diff_queries_out(tok):
                filled(dve, "diff_q", 0, tok)
                dve.wait_ge(beside_ready, 5 + tok)
                dve.tensor_scalar(dq[:, tok, :], acc[:, 2 * tok:2 * tok + 2].rearrange("p a c -> p (a c)"),
                                  DH ** -0.5, None, ALU.mult).then_inc(acc_free, 1)

            diff_queries_out(0)
            dve.wait_ge(lam_exp, 1)
            link(dve.tensor_tensor(lam[:, 2:3], lam[:, 0:1], lam[:, 1:2], ALU.subtract))
            dve.tensor_scalar(lam[:, 3:4], lam[:, 2:3], LAMBDA_INIT, None, ALU.add)

            def copy_heads(name, tok, part, dst):
                copy_turned((name, "diff", tok, part), dst[:, 4 * part:4 * part + 4, tok * P:(tok + 1) * P])

            for part in (1, 3):
                copy_heads("kr", 0, part, dks[:, 0])
            split_beside(6)
            for part in (1, 3):
                copy_heads("kr", 1, part, dks[:, 0])
            for part in (1, 3):
                copy_heads("ks", 0, part, dks[:, 1])
            copy_heads("ks", 1, 1, dks[:, 1])
            diff_queries_out(1)
            copy_heads("ks", 1, 3, dks[:, 1])
            for part in (1, 3):
                copy_heads("qr", 0, part, dqs)
            split_beside(7)

            def diff_read(turn):
                tok, g = DIFF_TURNS[turn]
                heads = slice(4 * g, 4 * g + 4)
                dve.wait_ge(exp_done, len(NSA_JOBS) + jobs_through(DIFF_JOBS, turn))
                link(dve.reciprocal(share[:, :, 0:4], sums[:, tok, :, heads]))
                link(dve.tensor_scalar(share[:, 1, 0:4], share[:, 1, 0:4], lam[:, 3:4], None, ALU.mult))
                dve.wait_ge(turn_full, len(NSA_TURNS) + turn + 1)
                for m, dst in enumerate(diff_parts(turn)):
                    ins = dve.tensor_tensor(dst, acc[:, 2 + m].rearrange("p (h d) -> p h d", d=DIFF_V),
                                            bc(share[:, m, 0:4].unsqueeze(2), P, 4, DIFF_V), ALU.mult)
                ins.then_inc(turn_read, 1)

            def diff_parts(turn):
                tok, g = DIFF_TURNS[turn]
                return [v.rearrange("p (h d) -> p h d", d=DIFF_V)
                        for v in (dq[:, tok, g * 512:(g + 1) * 512], branch[0])]

            def diff_subtract(turn):
                o, t = diff_parts(turn)
                dve.wait_ge(turn_read, len(NSA_TURNS) + turn + 1)
                link(dve.tensor_tensor(o, o, t, ALU.subtract))
                link(dve.tensor_tensor(t, o, o, ALU.mult))
                link(dve.tensor_reduce(rms[:, 0, turn, :], t, AX.X, ALU.add))
                dve.tensor_scalar(rms[:, 0, turn, :], rms[:, 0, turn, :], 1.0 / DIFF_V, EPS, ALU.mult, ALU.add).then_inc(
                    rms_ready, 1)

            def diff_norm(turn):
                o, _ = diff_parts(turn)
                dve.wait_ge(rms_pow, turn + 1)
                link(dve.tensor_tensor(o, o, bc(rms[:, 1, turn, :].unsqueeze(2), P, 4, DIFF_V), ALU.mult))
                dve.scalar_tensor_tensor(o, o, 1.0 - LAMBDA_INIT, bc(sub_g[:].unsqueeze(1), P, 4, DIFF_V),
                                         ALU.mult, ALU.mult).then_inc(turn_mixed, 1)

            last = len(DIFF_TURNS) - 1
            norm_lag = (4, 3)
            for i, sc, tr, pv in job_steps(DIFF_JOBS):
                if sc:
                    maxima(DIFF_JOBS, i, len(NSA_JOBS))
                for turn in range(last):
                    if ends_turn(DIFF_JOBS, pv - 1, turn):
                        diff_subtract(turn)
                    if turn < 2 and ends_turn(DIFF_JOBS, pv - norm_lag[turn], turn):
                        diff_norm(turn)
                if pv >= 0 and DIFF_JOBS[pv][3]:
                    diff_read(DIFF_JOBS[pv][0])
                if i in TILE0_DONE["diff"]:
                    x_low("diff_o", 0, [TILE0_DONE["diff"].index(i)])
            diff_subtract(last)
            diff_norm(last - 1)
            diff_norm(last)
            split_units(n0 + 7, n0 + 8)
            x_low("diff_o", 1)
            out_stage("diff_out")
            ffn_stage("ffn3", lambda: x_low("diff_out", 1))

        @block.tensor
        def _(pe):
            def three(out_ap, s_hi, s_lo, hi, lo, first, last):
                pe.matmul(out_ap, s_hi, hi, start=first, stop=False)
                pe.matmul(out_ap, s_hi, lo, start=False, stop=False)
                return pe.matmul(out_ap, s_lo, hi, start=False, stop=last)

            def columns_unit(n, j, tok, inner=None):
                hi, lo = weights(w_hi, n), weights(w_lo, n)
                cols = hi.shape[2]
                for k in range(4):
                    if inner and k in inner:
                        inner[k]()
                    kt = 4 * (j % 2) + k
                    ins = three(acc[:, 2 * tok + j // 2, 0:cols], xt_hi[:, kt, tok * P:(tok + 1) * P],
                                xt_lo[:, kt, tok * P:(tok + 1) * P], hi[:, k, :], lo[:, k, :], kt == 0, kt == KT - 1)
                return ins

            def half_unit(n, j, tok):
                hi, lo = weights(w_hi, n), weights(w_lo, n)
                for kt in range(KT):
                    ins = three(acc[:, 2 * tok + j, 0:HALF], xt_hi[:, kt, tok * P:(tok + 1) * P],
                                xt_lo[:, kt, tok * P:(tok + 1) * P], hi[:, kt, :], lo[:, kt, :], kt == 0,
                                kt == KT - 1)
                return ins

            def rows_unit(s_hi, s_lo, tiles):
                def emit(n, j, tok, halves=range(2)):
                    hi, lo = weights(w_hi, n), weights(w_lo, n)
                    for k in range(2):
                        kt = 2 * j + k
                        sh, sl = (s[:, kt, tok * P:(tok + 1) * P] for s in (s_hi, s_lo))
                        for c in halves:
                            cols = slice(c * 512, (c + 1) * 512)
                            ins = three(acc[:, 2 * tok + c], sh, sl, hi[:, k, cols], lo[:, k, cols], kt == 0,
                                        kt == tiles - 1)
                    return ins
                return emit

            def run_units(tok, n0, js, emit, ready=None, between=None, inner=None):
                for pos, j in enumerate(js):
                    n = n0 + j
                    if between and pos in between:
                        between[pos]()
                    if tok == 0:
                        pe.wait_ge(lo_ready, n + 1 if ready is None else ready + pos)
                    ins = emit(n, j, tok, inner[pos]) if inner and pos in inner else emit(n, j, tok)
                    if tok == 1:
                        ins.then_inc(unit_used, 1)
                return ins

            def turn_blocks(t, bank, blocks, wait):
                if wait is not None:
                    pe.wait_ge(tr_free[bank], wait)
                for j, b in enumerate(blocks):
                    ins = pe.transpose(trb[:, bank, j * P:(j + 1) * P], b, ident)
                ins.then_inc(tr_full, 1)

            def turn(name, blocks):
                t = TURN_OF[name]
                turn_blocks(t, t % 2, blocks, t // 2 if t >= 2 else None)

            def turn_wide(name, src, parts=range(2)):
                for part in parts:
                    turn((*name, part), [src[:, (4 * part + j) * P:(4 * part + j + 1) * P] for j in range(4)])

            def turn_x(stage, tok):
                pe.wait_ge(x_ready, 2 * NORM_OF[stage] + tok + 1)
                turn_wide(("x", stage, tok), x[:, tok, :])

            def copied(*name):
                t = TURN_OF[name]
                pe.wait_ge(tr_free[t % 2], t // 2 + 1)

            def open_acc(e):
                if e >= 2:
                    pe.wait_ge(acc_free, e - 1)

            def finish(tok, ins):
                if tok == 0:
                    ins.then_inc(tile0_full, 1)

            def group(tok, e, n0, js, emit, between=None, operand=None, inner=None):
                open_acc(e)
                if operand is not None:
                    for part in range(2):
                        copied(*operand, part)
                finish(tok, run_units(tok, n0, js, emit, between=between, inner=inner))

            def ffn_stage(stage, turn_rest, operand, next_x):
                n0, e0, t0 = UNIT_OF[stage], FILL_OF[stage, 0, 0], TURN_OF["h", stage, 0, 0]

                def turn_h(g, tok, k):
                    pe.wait_ge(acc_free, 2 * g + (e0 + tok + 1))
                    turn_blocks(None, (t0 + tok) % 2, [h_nat[:, tok, j * P:(j + 1) * P] for j in range(k)],
                                g + (t0 + tok) // 2)

                group(0, e0, n0, range(4), columns_unit, {3: turn_rest}, (*operand, 0))
                for part in range(2):
                    copied(*operand, 1, part)
                with pe.Fori(0, G_FULL - 1) as g:
                    pe.wait_ge(acc_free, 2 * g + e0)
                    ins = run_units(1, n0, range(4), columns_unit,
                                    between={3: lambda: turn_h(g, 0, 4)})
                    finish(1, ins)
                    pe.wait_ge(acc_free, 2 * g + (e0 + 1))
                    ins = run_units(0, n0, range(4), columns_unit, ready=4 * g + (n0 + 5),
                                    between={3: lambda: turn_h(g, 1, 4)})
                    finish(0, ins)
                g = G_FULL - 1
                group(1, e0 + 2 * g + 1, n0 + 4 * g, range(4), columns_unit,
                      {3: lambda: turn_h(G_FULL - 1, 0, 4)})
                group(0, e0 + 2 * g + 2, n0 + 4 * g + 4, range(2), half_unit,
                      {1: lambda: turn_h(G_FULL - 1, 1, 4)})
                g = G_FULL
                group(1, e0 + 2 * g + 1, n0 + 4 * g, range(2), half_unit,
                      {1: lambda: turn_h(g, 0, 2)})
                emit = rows_unit(ht_hi, ht_lo, FT)
                e = e0 + 2 * (G_FULL + 1)
                open_acc(e)
                for i, js in enumerate(DOWN_GROUPS):
                    if i == len(DOWN_GROUPS) - 1:
                        for tok in range(TOKS):
                            copied("h", stage, G_FULL, tok)
                    ins = run_units(0, n0 + UNITS_GU, js, emit, between={
                        len(js) - 1: lambda: turn_h(G_FULL, 1, 2)}
                        if i == 0 else None)
                    if i == len(DOWN_GROUPS) - 1:
                        finish(0, ins)
                    if i == 0:
                        open_acc(e + 1)
                    if stage == "ffn3" and i == len(DOWN_GROUPS) - 1:
                        for half in range(2):
                            for j in js:
                                ins = emit(n0 + UNITS_GU + j, j, 1, [half])
                                if half:
                                    ins.then_inc(unit_used, 1)
                            if not half:
                                ins.then_inc(half_full, 1)
                        continue
                    ins = run_units(1, n0 + UNITS_GU, js, emit, between={
                        3: lambda: turn_x(stage, 0)} if next_x and i == len(DOWN_GROUPS) - 1 else None)
                    if i == len(DOWN_GROUPS) - 1:
                        finish(1, ins)

            def out_stage(stage, o_name):
                n0, e = UNIT_OF[stage], FILL_OF[stage, 0, 0]
                emit = rows_unit(xt_hi, xt_lo, KT)
                turns = len(NSA_TURNS) if stage == "nsa_out" else len(NSA_TURNS) + len(DIFF_TURNS)
                jobs = len(NSA_JOBS) if stage == "nsa_out" else len(NSA_JOBS) + len(DIFF_JOBS)
                src = nq if stage == "nsa_out" else dq

                def turn_o():
                    pe.wait_ge(turn_mixed, turns)
                    turn_wide(("x", o_name, 1), src[:, 1, :])

                pe.wait_ge(exp_done, jobs)
                group(0, e, n0, range(4), emit, {3: turn_o}, ("x", o_name, 0))
                group(1, e + 1, n0, range(4), emit, {3: lambda: turn_x(stage, 0)}, ("x", o_name, 1))

            def scores(jobs, i, base, q_t, key_t):
                _, tok, heads, _ = jobs[i]
                width = P * (tok + 1)
                if i >= 3:
                    pe.wait_ge(exp_done, base + i - 2)
                bank, k = score_bank[i % 3], 0
                for h in heads:
                    for m in range(2):
                        for part in range(2):
                            pe.matmul(bank[:, k * width:(k + 1) * width], q_t(h, m)[:, tok * P:(tok + 1) * P],
                                      key_t(h, m, part)[:, 0:width], start=(part == 0), stop=False)
                        ins = pe.matmul(bank[:, (k + 1) * width - P:(k + 1) * width], id_bf[:], diag_bf[:],
                                        start=False, stop=True)
                        k += 1
                ins.then_inc(score_full, 1)

            def turn_p(kind, i, base):
                pe.wait_ge(exp_done, base + i + 1)
                turn(("p", kind, i), [probs[:, i % 3, j * P:(j + 1) * P] for j in range(4)])

            def values(kind, jobs, j, v_of, width, first, per_turn):
                turn_no, tok, heads, last = jobs[j]
                if j == 0 or jobs[j - 1][3]:
                    first(turn_no)
                copied("p", kind, j)
                k = 0
                for h in heads:
                    for m in range(2):
                        for kb in range(tok + 1):
                            ins = pe.matmul(acc[:, 2 + m, (h % per_turn) * width:(h % per_turn + 1) * width],
                                            turned_probs[:, j % 2, k * P:(k + 1) * P], v_of(h, m, kb), start=(kb == 0),
                                            stop=(kb == tok))
                            k += 1
                if last:
                    ins.then_inc(turn_full, 1)

            def warm_up(n):
                for _ in range(n):
                    pe.matmul(aux[:, 0, 0:P], id_bf[:], id_bf[:], start=True, stop=True)

            pe.wait_ge(masks_ready, 2)
            warm_up(8)
            pe.wait_ge(x_landed[0], 16)
            turn_wide(("x", "start", 0), x[:, 0, :])
            warm_up(18)

            def turn_start():
                pe.wait_ge(x_landed[1], 16)
                turn_wide(("x", "start", 1), x[:, 1, :])

            ffn_stage("ffn0", turn_start, ("x", "start"), True)

            n0 = UNIT_OF["nsa_in"]

            def turn_kc(b):
                pe.wait_ge(k_dup, 2)
                turn(("kc", b), [y[:, tok, b * 256 + g * P:b * 256 + (g + 1) * P] for g in range(NSA_GROUPS)
                                 for tok in range(TOKS)])

            def turn_kr(m):
                pe.wait_ge(beside_ready, 2)
                turn(("kr", m), [beside[tok][:, 2 * m + g].rearrange("p s d -> p (s d)").bitcast(F32)
                                 for g in range(NSA_GROUPS) for tok in range(TOKS)])

            def swap_halves(name, of, src):
                t = TURN_OF[name]
                copied(*of)
                pe.wait_ge(tr_free[t % 2], t // 2)
                pe.matmul(trb[:, t % 2], swap, src, start=True, stop=True).then_inc(tr_full, 1)

            def hidden(b):
                copied("kc", b)
                pe.wait_ge(w1_in, 32)
                w = w1k if b == 0 else w1v[:]
                for pair in range(CMP_BLOCK // 2):
                    ins = pe.matmul(aux[:, b, 0:2 * N_CMP], w[:, pair, :], blk[:, b, pair, :], start=(pair == 0),
                                    stop=(pair == CMP_BLOCK // 2 - 1))
                ins.then_inc(hid_full, 1)

            def second_layer():
                pe.wait_ge(hid_ready, 1)
                pe.matmul(aux[:, 0, 64:64 + 2 * N_CMP], w2k2[:].rearrange("p r d -> p (r d)"), hid[:, 0, :],
                          start=True, stop=True).then_inc(cmp_full, 1)
                pe.wait_ge(cmp_ready, 1)
                for g in range(NSA_GROUPS):
                    ins = pe.matmul(aux[:, 1, 64 + g * DH:64 + (g + 1) * DH],
                                    hid_rep[:, g].rearrange("p h c -> p (h c)"), w2_sb[:, 1, :], start=True, stop=True)
                ins.then_inc(cmp_full, 1)

            def turn_q(tok):
                pe.wait_ge(acc_free, FILL_OF["nsa_in", 1, tok] + 1)
                turn_wide(("q", tok), nq[:, tok, :])

            def turn_heads(name, tok, part, k):
                pe.wait_ge(beside_ready, k + 1)
                turn((*name, tok, part), [beside[k][:, 4 * part + j].rearrange("p s d -> p (s d)").bitcast(F32)
                                          for j in range(4)])

            def compressed_scores(tok):
                for part in range(2):
                    copied("q", tok, part)
                if tok == 0:
                    pe.wait_ge(cmp_ready, 3)
                for pair in range(NSA_HEADS // 2):
                    ins = pe.matmul(aux[:, tok, pair * 32:(pair + 1) * 32], nqt[:, pair, tok * P:(tok + 1) * P],
                                    kcb[:, pair // 4].rearrange("p r c -> p (r c)"), start=True, stop=True)
                ins.then_inc(cs_full, 1)

            e = FILL_OF["nsa_in", 0, 0]
            group(0, e, n0, range(4), columns_unit, {3: lambda: turn_x("ffn0", 1)}, ("x", "ffn0", 0))
            group(1, e + 1, n0, range(4), columns_unit, None, ("x", "ffn0", 1))
            group(0, e + 2, n0 + 4, range(4), columns_unit, {2: lambda: turn_kc(0), 3: lambda: turn_kc(1)})
            group(1, e + 3, n0 + 4, range(4), columns_unit,
                  {0: lambda: hidden(0), 1: lambda: (hidden(1), turn_q(0)),
                   2: lambda: (turn_kr(0), turn_kr(1), second_layer()),
                   3: lambda: [swap_halves(("ks", m), ("kr", m), nks[:, 0, m].rearrange("p g t -> p (g t)"))
                               for m in range(2)]})
            compressed_scores(0)
            for part in range(4):
                turn_heads(("qr", "nsa"), 0, part, 2)

            def nsa_first(turn_no):
                tok, g = NSA_TURNS[turn_no]
                if turn_no:
                    pe.wait_ge(turn_read, turn_no)
                else:
                    pe.wait_ge(cs_copied, 2)
                    copied("pc")
                pe.matmul(aux[:, 1], pct[:, 2 * tok + g, :], vcb[:, g].rearrange("p h d -> p (h d)"), start=True,
                          stop=True).then_inc(cmp_out, 1)

            pe.wait_ge(masks_ready, 2)
            pe.wait_ge(acc_free, e + 3)
            for i, sc, tr, pv in job_steps(NSA_JOBS):
                if i < 8 and i % 2 == 0:
                    copied("qr", "nsa", 0, i // 2)
                if 8 <= i < 24 and i % 4 == 0:
                    copied("qr", "nsa", 1, i // 4 - 2)
                if i == 0:
                    for m in range(2):
                        copied("ks", m)
                if i == 2:
                    pe.wait_ge(cs_copied, 1)
                if sc:
                    scores(NSA_JOBS, i, 0, lambda h, m: nqs[:, h], lambda h, m, part: nks[:, part, m, h // 8])
                if i == 0:
                    turn_q(1)
                if i == 1:
                    compressed_scores(1)
                if tr:
                    turn_p("nsa", i - 2, 0)
                if i == 3:
                    pe.wait_ge(cexp_done, 2)
                    turn(("pc",), [cs[:, tok, 8 * g:8 * g + 8].rearrange("p h c -> p (h c)")
                                   for tok in range(TOKS) for g in range(NSA_GROUPS)])
                for part in LATE_PARTS["nsa"].get(i, ()):
                    turn_heads(("qr", "nsa"), 1, part, 3)
                if pv >= 0:
                    values("nsa", NSA_JOBS, pv,
                           lambda h, m, kb: kv_a[:, kb, (VS, VW)[m] + (h // 8) * DH:(VS, VW)[m] + (h // 8 + 1) * DH],
                           DH, nsa_first, 8)
                if i in TILE0_DONE["nsa"]:
                    half = TILE0_DONE["nsa"].index(i)
                    pe.wait_ge(turn_mixed, half + 1)
                    turn_wide(("x", "nsa_o", 0), nq[:, 0, :], [half])
            out_stage("nsa_out", "nsa_o")
            ffn_stage("ffn1", lambda: turn_x("nsa_out", 1), ("x", "nsa_out"), True)

            n0, e = UNIT_OF["kv"], FILL_OF["kv", 0, 0]

            group(0, e, n0, range(4), columns_unit, {3: lambda: turn_x("ffn1", 1)}, ("x", "ffn1", 0))
            group(1, e + 1, n0, range(4), columns_unit, None, ("x", "ffn1", 1))
            group(0, e + 2, n0 + 4, range(4), columns_unit)
            group(1, e + 3, n0 + 4, range(4), columns_unit)
            ffn_stage("ffn2", lambda: None, ("x", "ffn1"), True)

            n0, e = UNIT_OF["diff_q"], FILL_OF["diff_q", 0, 0]
            def swap_keys(parts):
                for tok, part in parts:
                    swap_halves(("ks", "diff", tok, part), ("kr", "diff", tok, part),
                                dks[:, 0, 4 * part:4 * part + 4, tok * P:(tok + 1) * P])

            parts = [(tok, part) for tok in range(TOKS) for part in range(4)]
            group(0, e, n0, range(4), columns_unit,
                  {3: lambda: turn_x("ffn2", 1)}, ("x", "ffn2", 0))
            group(1, e + 1, n0, range(4), columns_unit, None, ("x", "ffn2", 1), inner={
                1: {k: lambda k=k: turn_heads(("kr", "diff"), 0, k, 4) for k in range(4)},
                2: {k: lambda k=k: turn_heads(("kr", "diff"), 1, k, 5) for k in range(4)},
                3: {k: lambda k=k: swap_keys(parts[2 * k:2 * k + 2]) for k in range(4)}})
            for part in range(4):
                turn_heads(("qr", "diff"), 0, part, 6)
            pe.wait_ge(acc_free, e + 1)
            base = len(NSA_JOBS)

            def diff_first(turn_no):
                if turn_no:
                    pe.wait_ge(turn_read, len(NSA_TURNS) + turn_no)

            for i, sc, tr, pv in job_steps(DIFF_JOBS):
                if i in (0, 2):
                    for m in range(2):
                        copied("qr", "diff", 0, 2 * m + i // 2)
                if i in (4, 8):
                    for m in range(2):
                        copied("qr", "diff", 1, 2 * m + i // 8)
                if i == 0:
                    for tok, part in parts:
                        copied("ks", "diff", tok, part)
                if sc:
                    scores(DIFF_JOBS, i, base, lambda h, m: dqs[:, 8 * m + h],
                           lambda h, m, part: dks[:, part, 8 * m + h])
                if tr:
                    turn_p("diff", i - 2, base)
                for part in LATE_PARTS["diff"].get(i, ()):
                    turn_heads(("qr", "diff"), 1, part, 7)
                if pv >= 0:
                    values("diff", DIFF_JOBS, pv,
                           lambda h, m, kb: v_b[:, kb, h * DIFF_V:(h + 1) * DIFF_V], DIFF_V, diff_first, 4)
                if i in TILE0_DONE["diff"]:
                    half = TILE0_DONE["diff"].index(i)
                    pe.wait_ge(turn_mixed, len(NSA_TURNS) + half + 1)
                    turn_wide(("x", "diff_o", 0), dq[:, 0, :], [half])
            out_stage("diff_out", "diff_o")
            ffn_stage("ffn3", lambda: turn_x("diff_out", 1), ("x", "diff_out"), False)


def constants():
    import numpy as np
    c = np.zeros((P, C_COLS), np.float32)
    q = np.arange(P)
    squares = np.concatenate([np.eye(P), np.where(q[None, :] <= q[:, None], 0.0, NEG)], 1).astype(np.float32)
    half = ROT // 2
    inv = np.float32(500000.0) ** (-np.arange(half, dtype=np.float32) * np.float32(2.0) / np.float32(ROT))
    ang = np.arange(SEQ, dtype=np.float32)[:, None] * inv[None, :].astype(np.float32)
    for tok in range(TOKS):
        a = np.tile(ang[tok * P:(tok + 1) * P], (1, 2))
        c[:, C_COS + tok * ROT:C_COS + (tok + 1) * ROT] = np.cos(a)
        c[:, C_SIN + tok * ROT:C_SIN + (tok + 1) * ROT] = np.sin(a)
        end = np.arange(16) * CMP_STRIDE + CMP_BLOCK - 1
        sees = (end[None, :] <= (q + tok * P)[:, None]) & (np.arange(16) < N_CMP)[None, :]
        c[:, C_CMP + tok * 16:C_CMP + (tok + 1) * 16] = np.where(sees, 0.0, NEG)
        c[:, C_ANY + tok] = sees.any(1)
    c[:, C_HEAD:C_HEAD + 8] = (q[:, None] // 16) == np.arange(8)[None, :]
    return c, squares


def kernel(**inputs):
    import numpy as np
    import concourse.bacc as bacc
    from concourse.bass_utils import run_bass_kernel_spmd as run

    nc = bacc.Bacc("TRN2", target_bir_lowering=False, num_devices=1)
    arrays = {}

    def dram(name, a):
        a = np.ascontiguousarray(a)
        arrays[name] = a
        return nc.dram_tensor(name, a.shape, mybir.dt.from_np(a.dtype), kind="ExternalInput").ap()

    a = {k: np.asarray(v) for k, v in inputs.items()}

    def ffn(which):
        return [dram(f"ffn{b}_{which}_{layer}", a[f"ffn{b}_{which}"][layer]) for layer in range(DEPTH) for b in (1, 2)]

    def two(name):
        return [a[f"a_cmp_{name}_k"][0], a[f"a_cmp_{name}_v"][0]]

    args = [
        dram("x_in", a["x"][0]),
        dram("const", constants()[0]),
        dram("squares", constants()[1]),
        ffn("w_gate"), ffn("w_up"), ffn("w_down"),
        dram("norm_gain", a["ln_g"].reshape(3 * DEPTH, D)),
        dram("norm_bias", a["ln_b"].reshape(3 * DEPTH, D)),
        dram("w_in", a["a_w_in"][0]),
        dram("w_out_a", a["a_w_out"][0]),
        dram("cmp_pos", np.stack([p.reshape(CMP_BLOCK // 2, 2 * DH).T for p in two("pos")])),
        dram("cmp_w1", np.stack(two("w1"))),
        dram("cmp_b1", np.stack(two("b1"), axis=1)),
        dram("cmp_w2", np.stack(two("w2"))),
        dram("w_kv", a["b_w_kv_shared"]),
        dram("w_q", a["b_w_q"][0]),
        dram("lambdas", np.stack([a[f"b_lambda_{n}"][0] for n in ("q1", "k1", "q2", "k2")])),
        dram("subln_g", a["b_subln_g"][0]),
        dram("w_out_b", a["b_w_out"][0]),
        nc.dram_tensor("out", (SEQ, D), F32, kind="ExternalOutput").ap(),
    ]
    build_program(nc, *args)
    r = run(nc, [arrays], core_ids=[0])
    return r.results[0]["out"].reshape(1, SEQ, D)
```
